# Optimizing a Trainium2 kernel written in Bass

```python
import jax
import jax.numpy as jnp
from jax import lax
import numpy as np
import math
import jax, jax.numpy as jnp

D_MODEL = 1024
BATCH = 1
SEQ = 256
DEPTH = 2

GRID_W = 64
CTX_LEN = 256
N_MIXERS = 4
MIX_RET, MIX_NAT, MIX_POOL, MIX_SWA = 0, 1, 2, 3
N_RET = len(range(MIX_RET, DEPTH, N_MIXERS))
N_NAT = len(range(MIX_NAT, DEPTH, N_MIXERS))
N_POOL = len(range(MIX_POOL, DEPTH, N_MIXERS))
N_SWA = len(range(MIX_SWA, DEPTH, N_MIXERS))
EPS = 1e-6
NEG_INF = -1e30
ROPE_BASE = 10000.0
FFN_HIDDEN = 2816
RET_HEADS = 4
RET_QK_DIM = D_MODEL // RET_HEADS
RET_V_DIM = 2 * RET_QK_DIM
RET_CHUNK = 128
NAT_HEADS = 16
NAT_HEAD_DIM = D_MODEL // NAT_HEADS
NAT_KH = 8
NAT_KW = 16
POOL_WINDOWS = (2, 4, 8, 16)
POOL_GROUPS = len(POOL_WINDOWS)
POOL_GROUP_DIM = D_MODEL // POOL_GROUPS
SWA_Q_HEADS = 16
SWA_KV_HEADS = 4
SWA_HEAD_DIM = D_MODEL // SWA_Q_HEADS
SWA_WINDOW = 128
SWA_BLOCK = 128


def rms_norm(x, g):
    xf = x.astype(jnp.float32)
    y = xf * lax.rsqrt(jnp.mean(xf * xf, axis=-1, keepdims=True) + EPS)
    return (y * g.astype(jnp.float32)).astype(x.dtype)

def ada_in(h, g, m, j):
    xn = rms_norm(h, g)
    return (xn * (1.0 + m[:, j, 1][:, None]) + m[:, j, 0][:, None]).astype(h.dtype)

def gated_residual(h, m, j, y, w):
    return h + (w * m[:, j, 2][:, None] * y).astype(h.dtype)

def swiglu(x, w_in, w_out):
    a, b = jnp.split(x @ w_in, 2, axis=-1)
    return (jax.nn.silu(a) * b) @ w_out

def rope_angles(positions, dim):
    seg = dim // len(positions)
    inv = ROPE_BASE ** (-jnp.arange(0, seg, 2, dtype=jnp.float32) / seg)
    return jnp.concatenate([jnp.tile(p.astype(jnp.float32)[:, None] * inv, (1, 2)) for p in positions], axis=-1)

def apply_rope(x, ang, n_axes):
    xf = x.astype(jnp.float32)
    segs = jnp.split(xf, 2 * n_axes, axis=-1)
    rot = jnp.concatenate([s for a in range(n_axes) for s in (-segs[2 * a + 1], segs[2 * a])], axis=-1)
    return (xf * jnp.cos(ang)[None, :, None] + rot * jnp.sin(ang)[None, :, None]).astype(x.dtype)

def retention_scan(q, k, v, log_gamma, s0, include_diag):
    B, T, H, _ = q.shape
    dv = v.shape[-1]
    C = RET_CHUNK
    N = T // C
    idx = jnp.arange(C, dtype=jnp.float32)
    diff = idx[:, None] - idx[None, :]
    keep = (diff >= 0) if include_diag else (diff > 0)
    intra = jnp.where(keep[None], jnp.exp(jnp.maximum(diff, 0.0)[None] * log_gamma[:, None, None]), 0.0)
    q_dec = jnp.exp((idx + 1.0)[None] * log_gamma[:, None])
    k_dec = jnp.exp((C - 1.0 - idx)[None] * log_gamma[:, None])
    c_dec = jnp.exp(C * log_gamma)[:, None, None]

    def chunks(a):
        return a.reshape(B, N, C, H, a.shape[-1]).transpose(1, 0, 3, 2, 4)

    def step(s, qkv):
        qn, kn, vn = qkv
        att = jnp.einsum('bhid,bhjd->bhij', qn, kn) * intra
        o = jnp.einsum('bhij,bhjv->bhiv', att, vn) + jnp.einsum('bhid,bhdv->bhiv', qn * q_dec[..., None], s)
        s = s * c_dec + jnp.einsum('bhjd,bhjv->bhdv', kn * k_dec[..., None], vn)
        return s, o

    s_fin, o = lax.scan(step, s0, (chunks(q), chunks(k), chunks(v)))
    return o.transpose(1, 0, 3, 2, 4).reshape(B, T, H, dv), s_fin

def retention_bidir(q, k, v, lg_f, lg_b, s0_f, s0_b):
    o_f, s_f = retention_scan(q, k, v, lg_f, s0_f, True)
    rev = lambda a: jnp.flip(a, axis=1)
    o_b, s_b = retention_scan(rev(q), rev(k), rev(v), lg_b, s0_b, False)
    return o_f + rev(o_b), s_f, s_b

def retention_mixer(xl, xc, w_in, w_out, gn_g, decay_f, decay_b, ctx_out):
    H, DK, DV = RET_HEADS, RET_QK_DIM, RET_V_DIM
    lg_f = jax.nn.log_sigmoid(decay_f.astype(jnp.float32))
    lg_b = jax.nn.log_sigmoid(decay_b.astype(jnp.float32))

    def project(x, ang):
        B, T, _ = x.shape
        q, k, v, g = jnp.split(x @ w_in, [H * DK, 2 * H * DK, 2 * H * DK + H * DV], axis=-1)
        q = q.reshape(B, T, H, DK)
        k = k.reshape(B, T, H, DK) * DK ** -0.5
        v = v.reshape(B, T, H, DV)
        if ang is not None:
            q = apply_rope(q, ang, 1)
            k = apply_rope(k, ang, 1)
        return q.astype(jnp.float32), k.astype(jnp.float32), v.astype(jnp.float32), g

    def read_out(o, g):
        mu = jnp.mean(o, axis=-1, keepdims=True)
        var = jnp.mean(jnp.square(o - mu), axis=-1, keepdims=True)
        on = (o - mu) * lax.rsqrt(var + EPS) * gn_g.astype(jnp.float32).reshape(H, DV)
        B, T = o.shape[:2]
        return (jax.nn.silu(g) * on.reshape(B, T, H * DV).astype(g.dtype)) @ w_out

    qc, kc, vc, gc = project(xc, None)
    Bc, L = xc.shape[:2]
    if ctx_out:
        zeros = jnp.zeros((Bc, H, DK, DV), jnp.float32)
        oc, s_f, s_b = retention_bidir(qc, kc, vc, lg_f, lg_b, zeros, zeros)
        yc = read_out(oc, gc)
    else:
        pos = jnp.arange(L, dtype=jnp.float32)[:, None]
        s_f = jnp.einsum('bthd,bthv->bhdv', kc * jnp.exp((L - 1.0 - pos) * lg_f)[None, :, :, None], vc)
        s_b = jnp.einsum('bthd,bthv->bhdv', kc * jnp.exp(pos * lg_b)[None, :, :, None], vc)
        yc = None
    T = xl.shape[1]
    ang = rope_angles([jnp.arange(T)], DK)
    ql, kl, vl, gl = project(xl, ang)
    ol, _, _ = retention_bidir(ql, kl, vl, lg_f, lg_b, s_f, s_b)
    return read_out(ol, gl), yc

def nat_mixer(xl, xc, w_qkv, w_o, rpb, ctx_out):
    H, DH = NAT_HEADS, NAT_HEAD_DIM

    def project(x):
        B, T, _ = x.shape
        q, k, v = jnp.split(x @ w_qkv, 3, axis=-1)
        return (q * DH ** -0.5).reshape(B, T, H, DH), k.reshape(B, T, H, DH), v.reshape(B, T, H, DH)

    qc, kc, vc = project(xc)
    ql, kl, vl = project(xl)
    B, T, _ = xl.shape
    rows = T // GRID_W
    kh = min(NAT_KH, rows)
    nk = kh * NAT_KW
    qg = ql.reshape(B, rows, GRID_W, H, DH)
    kg = kl.reshape(B, rows, GRID_W, H, DH)
    vg = vl.reshape(B, rows, GRID_W, H, DH)
    cols = jnp.arange(GRID_W)
    col_idx = jnp.clip(cols - NAT_KW // 2, 0, GRID_W - NAT_KW)[:, None] + jnp.arange(NAT_KW)
    col_bias_idx = col_idx - cols[:, None] + NAT_KW - 1

    def row_block(r):
        r0 = jnp.clip(r - kh // 2, 0, rows - kh)
        kw = lax.dynamic_slice_in_dim(kg, r0, kh, axis=1)[:, :, col_idx]
        vw = lax.dynamic_slice_in_dim(vg, r0, kh, axis=1)[:, :, col_idx]
        qr = lax.dynamic_index_in_dim(qg, r, axis=1, keepdims=False)
        row_bias_idx = r0 + jnp.arange(kh) - r + NAT_KH - 1
        bias = rpb[:, row_bias_idx][:, :, col_bias_idx].transpose(0, 2, 1, 3)
        s_nb = jnp.einsum('bchd,bacnhd->bhcan', qr, kw).astype(jnp.float32) + bias.astype(jnp.float32)
        s_cx = jnp.einsum('bchd,bjhd->bhcj', qr, kc).astype(jnp.float32)
        p = jax.nn.softmax(jnp.concatenate([s_nb.reshape(B, H, GRID_W, nk), s_cx], axis=-1), axis=-1).astype(vl.dtype)
        p_nb = p[..., :nk].reshape(B, H, GRID_W, kh, NAT_KW)
        return jnp.einsum('bhcan,bacnhd->bchd', p_nb, vw) + jnp.einsum('bhcj,bjhd->bchd', p[..., nk:], vc)

    o = lax.map(row_block, jnp.arange(rows))
    yl = o.transpose(1, 0, 2, 3, 4).reshape(B, T, H * DH) @ w_o
    yc = None
    if ctx_out:
        p = jax.nn.softmax(jnp.einsum('bihd,bjhd->bhij', qc, kc).astype(jnp.float32), axis=-1).astype(vc.dtype)
        oc = jnp.einsum('bhij,bjhd->bihd', p, vc)
        yc = oc.reshape(oc.shape[0], oc.shape[1], H * DH) @ w_o
    return yl, yc

def pool_mixer(x, w_grp, scale):
    B, T, D = x.shape
    G, Dg = POOL_GROUPS, POOL_GROUP_DIM
    xf = x.astype(jnp.float32).reshape(B, T, G, Dg)
    csum = jnp.concatenate([jnp.zeros((B, 1, G, Dg), jnp.float32), jnp.cumsum(xf, axis=1)], axis=1)
    half = jnp.asarray([w // 2 for w in POOL_WINDOWS])
    t = jnp.arange(T)[:, None]
    lo = jnp.clip(t - half, 0, T)
    hi = jnp.clip(t + half, 0, T)
    grp = jnp.arange(G)[None, :]
    mean = (csum[:, hi, grp] - csum[:, lo, grp]) / (hi - lo).astype(jnp.float32)[None, :, :, None]
    pooled = (mean - xf).astype(x.dtype)
    return jnp.einsum('btgc,gcd->btgd', pooled, w_grp).reshape(B, T, D) * scale

def swa_mixer(xl, xc, w_qkv, w_o, sink, ctx_out):
    HQ, HKV, DH = SWA_Q_HEADS, SWA_KV_HEADS, SWA_HEAD_DIM
    G = HQ // HKV

    def project(x, ang):
        B, T, _ = x.shape
        q, k, v = jnp.split(x @ w_qkv, [HQ * DH, (HQ + HKV) * DH], axis=-1)
        q = q.reshape(B, T, HQ, DH)
        k = k.reshape(B, T, HKV, DH)
        v = v.reshape(B, T, HKV, DH)
        if ang is not None:
            q = apply_rope(q, ang, 2)
            k = apply_rope(k, ang, 2)
        return (q * DH ** -0.5).reshape(B, T, HKV, G, DH), k, v

    B, T, _ = xl.shape
    t = jnp.arange(T)
    ang = rope_angles([t // GRID_W, t % GRID_W], DH)
    ql, kl, vl = project(xl, ang)
    qc, kc, vc = project(xc, None)
    sink_l = sink.astype(jnp.float32).reshape(HKV, G)
    nb = T // SWA_BLOCK
    nw = SWA_WINDOW // SWA_BLOCK
    nk = (2 * nw + 1) * SWA_BLOCK

    def band(a):
        ap = jnp.pad(a, ((0, 0), (SWA_WINDOW, SWA_WINDOW), (0, 0), (0, 0))).reshape(B, nb + 2 * nw, SWA_BLOCK, HKV, DH)
        return jnp.concatenate([ap[:, o:o + nb] for o in range(2 * nw + 1)], axis=2)

    kb, vb = band(kl), band(vl)
    qb = ql.reshape(B, nb, SWA_BLOCK, HKV, G, DH)
    qpos = (jnp.arange(nb)[:, None] * SWA_BLOCK + jnp.arange(SWA_BLOCK))[:, :, None]
    kpos = (jnp.arange(nb)[:, None] * SWA_BLOCK - SWA_WINDOW + jnp.arange(nk))[:, None, :]
    allowed = (jnp.abs(qpos - kpos) <= SWA_WINDOW) & (kpos >= 0) & (kpos < T)
    s_loc = jnp.where(allowed, jnp.einsum('bnikgd,bnjkd->bkgnij', qb, kb).astype(jnp.float32), NEG_INF)
    s_cx = jnp.einsum('bnikgd,bjkd->bkgnij', qb, kc).astype(jnp.float32)
    s_sk = jnp.broadcast_to(sink_l[None, :, :, None, None, None], s_loc.shape[:-1] + (1,))
    p = jax.nn.softmax(jnp.concatenate([s_loc, s_cx, s_sk], axis=-1), axis=-1)[..., :-1].astype(vl.dtype)
    o = jnp.einsum('bkgnij,bnjkd->bnikgd', p[..., :nk], vb) + jnp.einsum('bkgnij,bjkd->bnikgd', p[..., nk:], vc)
    yl = o.reshape(B, T, HQ * DH) @ w_o
    yc = None
    if ctx_out:
        s = jnp.einsum('bikgd,bjkd->bkgij', qc, kc).astype(jnp.float32)
        sk = jnp.broadcast_to(sink_l[None, :, :, None, None], s.shape[:-1] + (1,))
        pc = jax.nn.softmax(jnp.concatenate([s, sk], axis=-1), axis=-1)[..., :-1].astype(vc.dtype)
        oc = jnp.einsum('bkgij,bjkd->bikgd', pc, vc)
        yc = oc.reshape(oc.shape[0], oc.shape[1], HQ * DH) @ w_o
    return yl, yc

def first_inputs(seed: int = 0) -> dict:
    key = jax.random.key(seed)
    ks = jax.random.split(key, 24)
    D, F = D_MODEL, FFN_HIDDEN
    nrm = lambda k, shape, s: jax.random.normal(k, shape, jnp.float32) * s
    ret_in = 2 * RET_HEADS * RET_QK_DIM + 2 * RET_HEADS * RET_V_DIM
    ret_v = RET_HEADS * RET_V_DIM
    decay_logit = jnp.log(2.0 ** (5.0 + jnp.arange(RET_HEADS, dtype=jnp.float32)) - 1.0)
    nat_w = NAT_HEADS * NAT_HEAD_DIM
    swa_in = (SWA_Q_HEADS + 2 * SWA_KV_HEADS) * SWA_HEAD_DIM
    swa_o = SWA_Q_HEADS * SWA_HEAD_DIM
    return {
        'x': nrm(ks[0], (BATCH, SEQ, D), 1.0),
        'c': nrm(ks[1], (BATCH, D), 1.0),
        'ctx': nrm(ks[2], (BATCH, CTX_LEN, D), 1.0),
        'c_ctx': nrm(ks[3], (D,), 1.0),
        'w_mod': nrm(ks[4], (DEPTH, D, 9 * D), 0.5 * D ** -0.5),
        'b_mod': nrm(ks[5], (DEPTH, 9 * D), 0.01),
        'norm_g': 1.0 + nrm(ks[6], (DEPTH, 3, D), 0.02),
        'ffn_w_in': nrm(ks[7], (DEPTH, 2, D, 2 * F), D ** -0.5),
        'ffn_w_out': nrm(ks[8], (DEPTH, 2, F, D), F ** -0.5),
        'ret_w_in': nrm(ks[9], (N_RET, D, ret_in), D ** -0.5),
        'ret_w_out': nrm(ks[10], (N_RET, ret_v, D), ret_v ** -0.5),
        'ret_gn_g': 1.0 + nrm(ks[11], (N_RET, ret_v), 0.02),
        'ret_decay_f': decay_logit + nrm(ks[12], (N_RET, RET_HEADS), 0.05),
        'ret_decay_b': decay_logit + nrm(ks[13], (N_RET, RET_HEADS), 0.05),
        'nat_w_qkv': nrm(ks[14], (N_NAT, D, 3 * nat_w), D ** -0.5),
        'nat_w_o': nrm(ks[15], (N_NAT, nat_w, D), nat_w ** -0.5),
        'nat_rpb': nrm(ks[16], (N_NAT, NAT_HEADS, 2 * NAT_KH - 1, 2 * NAT_KW - 1), 0.1),
        'pool_w': nrm(ks[17], (N_POOL, POOL_GROUPS, POOL_GROUP_DIM, POOL_GROUP_DIM), POOL_GROUP_DIM ** -0.5),
        'pool_scale': 1.0 + nrm(ks[18], (N_POOL, D), 0.02),
        'swa_w_qkv': nrm(ks[19], (N_SWA, D, swa_in), D ** -0.5),
        'swa_w_o': nrm(ks[20], (N_SWA, swa_o, D), swa_o ** -0.5),
        'swa_sink': nrm(ks[21], (N_SWA, SWA_Q_HEADS), 0.5),
        'final_norm_g': 1.0 + nrm(ks[22], (D,), 0.02),
    }

def first_block(x, c, ctx, c_ctx, w_mod, b_mod, norm_g, ffn_w_in, ffn_w_out,
              ret_w_in, ret_w_out, ret_gn_g, ret_decay_f, ret_decay_b,
              nat_w_qkv, nat_w_o, nat_rpb, pool_w, pool_scale,
              swa_w_qkv, swa_w_o, swa_sink, final_norm_g):
    D = x.shape[-1]
    h, hc = x, ctx
    s_c = jax.nn.silu(c)
    s_cc = jax.nn.silu(c_ctx)[None]
    for i in range(DEPTH):
        kind, occ = i % N_MIXERS, i // N_MIXERS
        last = i == DEPTH - 1
        ctx_live = (not last) or kind != MIX_POOL
        ml = (s_c @ w_mod[i] + b_mod[i]).reshape(-1, 3, 3, D)
        h = gated_residual(h, ml, 0, swiglu(ada_in(h, norm_g[i, 0], ml, 0), ffn_w_in[i, 0], ffn_w_out[i, 0]), 0.5)
        xl = ada_in(h, norm_g[i, 1], ml, 1)
        xc = None
        if ctx_live:
            mc = (s_cc @ w_mod[i] + b_mod[i]).reshape(-1, 3, 3, D)
            hc = gated_residual(hc, mc, 0, swiglu(ada_in(hc, norm_g[i, 0], mc, 0), ffn_w_in[i, 0], ffn_w_out[i, 0]), 0.5)
            xc = ada_in(hc, norm_g[i, 1], mc, 1)
        if kind == MIX_RET:
            yl, yc = retention_mixer(xl, xc, ret_w_in[occ], ret_w_out[occ], ret_gn_g[occ],
                                     ret_decay_f[occ], ret_decay_b[occ], not last)
        elif kind == MIX_NAT:
            yl, yc = nat_mixer(xl, xc, nat_w_qkv[occ], nat_w_o[occ], nat_rpb[occ], not last)
        elif kind == MIX_POOL:
            yl = pool_mixer(xl, pool_w[occ], pool_scale[occ])
            yc = None if last else pool_mixer(xc, pool_w[occ], pool_scale[occ])
        else:
            yl, yc = swa_mixer(xl, xc, swa_w_qkv[occ], swa_w_o[occ], swa_sink[occ], not last)
        h = gated_residual(h, ml, 1, yl, 1.0)
        if not last:
            hc = gated_residual(hc, mc, 1, yc, 1.0)
            hc = gated_residual(hc, mc, 2, swiglu(ada_in(hc, norm_g[i, 2], mc, 2), ffn_w_in[i, 1], ffn_w_out[i, 1]), 0.5)
        h = gated_residual(h, ml, 2, swiglu(ada_in(h, norm_g[i, 2], ml, 2), ffn_w_in[i, 1], ffn_w_out[i, 1]), 0.5)
    return rms_norm(h, final_norm_g)


RMS_EPS = 1e-6
Q_BLOCK = 128
NEG_INF_2 = -1e30

T5_BUCKETS = 32
T5_MAX_EXACT = T5_BUCKETS // 2
T5_MAX_DISTANCE = 1024

DIFF_HEADS = 4
DIFF_HEAD_DIM = 64
DIFF_QK_WIDTH = DIFF_HEADS * 2 * DIFF_HEAD_DIM
DIFF_V_WIDTH = DIFF_HEADS * 2 * DIFF_HEAD_DIM

MOBA_HEADS = 4
MOBA_HEAD_DIM = 128
MOBA_BLOCK = 256
MOBA_TOPK = 3
MOBA_Q_CHUNK = 32
MOBA_WIDTH = MOBA_HEADS * MOBA_HEAD_DIM

MLA_HEADS = 8
MLA_Q_RANK = 256
MLA_KV_RANK = 128
MLA_NOPE_DIM = 64
MLA_ROPE_DIM = 32
MLA_V_DIM = 64
MLA_WIDTH = MLA_HEADS * MLA_V_DIM
ROPE_THETA = 10000.0

N_BRANCH = 3
BRANCH_WIDTH = 512
N_BIAS_HEADS = DIFF_HEADS + MOBA_HEADS
D_FF = 4 * D_MODEL

IN_SPLITS = (DIFF_QK_WIDTH, DIFF_QK_WIDTH, DIFF_V_WIDTH,
             MOBA_WIDTH, MOBA_WIDTH, MOBA_WIDTH,
             MLA_Q_RANK, MLA_KV_RANK, MLA_ROPE_DIM,
             N_BRANCH * D_MODEL)
IN_OFFSETS = tuple(sum(IN_SPLITS[:i + 1]) for i in range(len(IN_SPLITS) - 1))
D_IN = sum(IN_SPLITS)


def _rms_norm(x, w):
    xf = x.astype(jnp.float32)
    y = xf * lax.rsqrt(jnp.mean(xf * xf, axis=-1, keepdims=True) + RMS_EPS)
    return (y * w.astype(jnp.float32)).astype(x.dtype)

def _t5_bucket(rel):
    n = jnp.maximum(rel, 0)
    nf = jnp.maximum(n, 1).astype(jnp.float32)
    large = T5_MAX_EXACT + (jnp.log(nf / T5_MAX_EXACT)
                            / math.log(T5_MAX_DISTANCE / T5_MAX_EXACT)
                            * (T5_BUCKETS - T5_MAX_EXACT)).astype(jnp.int32)
    large = jnp.minimum(large, T5_BUCKETS - 1)
    return jnp.where(n < T5_MAX_EXACT, n, large)

def _rope(x, positions):
    d = x.shape[-1]
    half = d // 2
    inv_freq = ROPE_THETA ** (-jnp.arange(half, dtype=jnp.float32) * 2.0 / d)
    ang = positions.astype(jnp.float32)[:, :, None, None] * inv_freq
    cos, sin = jnp.cos(ang), jnp.sin(ang)
    xf = x.astype(jnp.float32)
    x1, x2 = xf[..., :half], xf[..., half:]
    return jnp.concatenate([x1 * cos - x2 * sin, x2 * cos + x1 * sin], axis=-1).astype(x.dtype)

def _diff_attention(q1, q2, k1, k2, v, lam, bias_table):
    B, S, H, dh = q1.shape
    scale = 1.0 / math.sqrt(dh)
    k_pos = jnp.arange(S)
    table = bias_table.astype(jnp.float32)

    def block(c):
        start = c * Q_BLOCK
        q_pos = start + jnp.arange(Q_BLOCK)
        rel = q_pos[:, None] - k_pos[None, :]
        bias = jnp.transpose(table[_t5_bucket(rel)], (2, 0, 1))
        visible = rel >= 0

        def probs(q, k):
            qb = lax.dynamic_slice_in_dim(q, start, Q_BLOCK, axis=1)
            s = jnp.einsum('bqhd,bkhd->bhqk', qb, k).astype(jnp.float32) * scale + bias
            return jax.nn.softmax(jnp.where(visible, s, NEG_INF_2), axis=-1)

        w = probs(q1, k1) - lam * probs(q2, k2)
        return jnp.einsum('bhqk,bkhd->bqhd', w.astype(v.dtype), v)

    out = lax.map(block, jnp.arange(S // Q_BLOCK))
    return jnp.transpose(out, (1, 0, 2, 3, 4)).reshape(B, S, H, v.shape[-1])

def _moba_attention(q, k, v, bias_table):
    B, S, H, d = q.shape
    scale = 1.0 / math.sqrt(d)
    n_blk = -(-S // MOBA_BLOCK)
    s_pad = n_blk * MOBA_BLOCK
    topk = min(MOBA_TOPK, n_blk)
    pad = ((0, 0), (0, s_pad - S), (0, 0), (0, 0))
    kbh = jnp.transpose(jnp.pad(k, pad).reshape(B, n_blk, MOBA_BLOCK, H, d), (0, 3, 1, 2, 4))
    vbh = jnp.transpose(jnp.pad(v, pad).reshape(B, n_blk, MOBA_BLOCK, H, d), (0, 3, 1, 2, 4))
    k_mean = jnp.mean(kbh.astype(jnp.float32), axis=3)
    blk_ids = jnp.arange(n_blk)
    offs = jnp.arange(MOBA_BLOCK)
    table = bias_table.astype(jnp.float32)
    table_t = table.T
    bi = jnp.arange(B)[:, None, None, None]
    hi = jnp.arange(H)[None, :, None, None]
    hi5 = jnp.arange(H)[None, :, None, None, None]

    def chunk(c):
        start = c * MOBA_Q_CHUNK
        own = start // MOBA_BLOCK
        q_pos = start + jnp.arange(MOBA_Q_CHUNK)
        qbt = jnp.transpose(lax.dynamic_slice_in_dim(q, start, MOBA_Q_CHUNK, axis=1), (0, 2, 1, 3))
        gate = jnp.einsum('bhqd,bhnd->bhqn', qbt.astype(jnp.float32), k_mean)
        gate = jnp.where(blk_ids < own, gate, NEG_INF_2)
        _, idx = lax.top_k(gate, topk)
        valid = idx < own
        k_sel = kbh[bi, hi, idx]
        v_sel = vbh[bi, hi, idx]
        s_sel = jnp.einsum('bhqd,bhqnld->bhqnl', qbt, k_sel).astype(jnp.float32) * scale
        sel_pos = idx[..., None] * MOBA_BLOCK + offs
        rel_sel = q_pos[None, None, :, None, None] - sel_pos
        s_sel = jnp.where(valid[..., None], s_sel + table_t[hi5, _t5_bucket(rel_sel)], NEG_INF_2)
        k_own = lax.dynamic_index_in_dim(kbh, own, axis=2, keepdims=False)
        v_own = lax.dynamic_index_in_dim(vbh, own, axis=2, keepdims=False)
        rel_own = q_pos[:, None] - (own * MOBA_BLOCK + offs)[None, :]
        bias_own = jnp.transpose(table[_t5_bucket(rel_own)], (2, 0, 1))
        s_own = jnp.einsum('bhqd,bhld->bhql', qbt, k_own).astype(jnp.float32) * scale + bias_own
        s_own = jnp.where(rel_own >= 0, s_own, NEG_INF_2)
        n_sel = topk * MOBA_BLOCK
        s = jnp.concatenate([s_sel.reshape(B, H, MOBA_Q_CHUNK, n_sel), s_own], axis=-1)
        p = jax.nn.softmax(s, axis=-1).astype(v.dtype)
        p_sel = p[..., :n_sel].reshape(B, H, MOBA_Q_CHUNK, topk, MOBA_BLOCK)
        p_own = p[..., n_sel:]
        return (jnp.einsum('bhqnl,bhqnld->bqhd', p_sel, v_sel)
                + jnp.einsum('bhql,bhld->bqhd', p_own, v_own))

    out = lax.map(chunk, jnp.arange(S // MOBA_Q_CHUNK))
    return jnp.transpose(out, (1, 0, 2, 3, 4)).reshape(B, S, H, d)

def _dense_causal_attention(q, k, v, scale):
    B, S, H, _ = q.shape
    k_pos = jnp.arange(S)

    def block(c):
        start = c * Q_BLOCK
        qb = lax.dynamic_slice_in_dim(q, start, Q_BLOCK, axis=1)
        s = jnp.einsum('bqhd,bkhd->bhqk', qb, k).astype(jnp.float32) * scale
        rel = (start + jnp.arange(Q_BLOCK))[:, None] - k_pos[None, :]
        p = jax.nn.softmax(jnp.where(rel >= 0, s, NEG_INF_2), axis=-1).astype(v.dtype)
        return jnp.einsum('bhqk,bkhd->bqhd', p, v)

    out = lax.map(block, jnp.arange(S // Q_BLOCK))
    return jnp.transpose(out, (1, 0, 2, 3, 4)).reshape(B, S, H, v.shape[-1])

def second_inputs(seed: int = 0) -> dict:
    key = jax.random.key(seed)
    ks = jax.random.split(key, 20)

    def nrm(k, shape, scale):
        return jax.random.normal(k, shape, jnp.float32) * scale

    x = nrm(ks[0], (BATCH, SEQ, D_MODEL), 1.0)
    offsets = jax.random.randint(ks[1], (BATCH, 1), 0, 4096, dtype=jnp.int32)
    positions = offsets + jnp.arange(SEQ, dtype=jnp.int32)[None, :]
    return {
        'x': x,
        'positions': positions,
        'rel_bias': nrm(ks[2], (T5_BUCKETS, N_BIAS_HEADS), 0.5),
        'norm_mix_pre': 1.0 + nrm(ks[3], (DEPTH, D_MODEL), 0.05),
        'norm_mix_post': 1.0 + nrm(ks[4], (DEPTH, D_MODEL), 0.05),
        'norm_mlp_pre': 1.0 + nrm(ks[5], (DEPTH, D_MODEL), 0.05),
        'norm_mlp_post': 1.0 + nrm(ks[6], (DEPTH, D_MODEL), 0.05),
        'w_in': nrm(ks[7], (DEPTH, D_MODEL, D_IN), D_MODEL ** -0.5),
        'diff_lambda': nrm(ks[8], (DEPTH, 4, DIFF_HEAD_DIM), 0.1),
        'diff_subln': 1.0 + nrm(ks[9], (DEPTH, 2 * DIFF_HEAD_DIM), 0.05),
        'mla_q_norm': 1.0 + nrm(ks[10], (DEPTH, MLA_Q_RANK), 0.05),
        'mla_w_uq': nrm(ks[11], (DEPTH, MLA_Q_RANK, MLA_HEADS * (MLA_NOPE_DIM + MLA_ROPE_DIM)), MLA_Q_RANK ** -0.5),
        'mla_kv_norm': 1.0 + nrm(ks[12], (DEPTH, MLA_KV_RANK), 0.05),
        'mla_w_ukv': nrm(ks[13], (DEPTH, MLA_KV_RANK, MLA_HEADS * (MLA_NOPE_DIM + MLA_V_DIM)), MLA_KV_RANK ** -0.5),
        'w_branch': nrm(ks[14], (DEPTH, N_BRANCH, BRANCH_WIDTH, D_MODEL), BRANCH_WIDTH ** -0.5),
        'w_out': nrm(ks[15], (DEPTH, D_MODEL, D_MODEL), D_MODEL ** -0.5),
        'w_up': nrm(ks[16], (DEPTH, D_MODEL, D_FF), D_MODEL ** -0.5),
        'w_down': nrm(ks[17], (DEPTH, D_FF, D_MODEL), D_FF ** -0.5),
    }

def second_block(x, positions, rel_bias, norm_mix_pre, norm_mix_post, norm_mlp_pre, norm_mlp_post,
              w_in, diff_lambda, diff_subln, mla_q_norm, mla_w_uq, mla_kv_norm, mla_w_ukv,
              w_branch, w_out, w_up, w_down):
    B, S, _ = x.shape
    for l in range(DEPTH):
        lam_init = 0.8 - 0.6 * math.exp(-0.3 * l)
        h = _rms_norm(x, norm_mix_pre[l])
        proj = jnp.einsum('bsd,de->bse', h, w_in[l])
        dq, dk, dv, mq, mk, mv, c_q, c_kv, k_pe, g = jnp.split(proj, IN_OFFSETS, axis=-1)

        dq = dq.reshape(B, S, DIFF_HEADS, 2, DIFF_HEAD_DIM)
        dk = dk.reshape(B, S, DIFF_HEADS, 2, DIFF_HEAD_DIM)
        dv = dv.reshape(B, S, DIFF_HEADS, 2 * DIFF_HEAD_DIM)
        lam_vecs = diff_lambda[l].astype(jnp.float32)
        lam = (jnp.exp(jnp.sum(lam_vecs[0] * lam_vecs[1]))
               - jnp.exp(jnp.sum(lam_vecs[2] * lam_vecs[3])) + lam_init)
        oa = _diff_attention(dq[..., 0, :], dq[..., 1, :], dk[..., 0, :], dk[..., 1, :], dv,
                             lam, rel_bias[:, :DIFF_HEADS])
        oa = (_rms_norm(oa, diff_subln[l]) * (1.0 - lam_init)).reshape(B, S, DIFF_V_WIDTH)

        ob = _moba_attention(mq.reshape(B, S, MOBA_HEADS, MOBA_HEAD_DIM),
                             mk.reshape(B, S, MOBA_HEADS, MOBA_HEAD_DIM),
                             mv.reshape(B, S, MOBA_HEADS, MOBA_HEAD_DIM),
                             rel_bias[:, DIFF_HEADS:]).reshape(B, S, MOBA_WIDTH)

        q = jnp.einsum('bsr,re->bse', _rms_norm(c_q, mla_q_norm[l]), mla_w_uq[l])
        q = q.reshape(B, S, MLA_HEADS, MLA_NOPE_DIM + MLA_ROPE_DIM)
        q = jnp.concatenate([q[..., :MLA_NOPE_DIM], _rope(q[..., MLA_NOPE_DIM:], positions)], axis=-1)
        kv = jnp.einsum('bsr,re->bse', _rms_norm(c_kv, mla_kv_norm[l]), mla_w_ukv[l])
        kv = kv.reshape(B, S, MLA_HEADS, MLA_NOPE_DIM + MLA_V_DIM)
        k_rope = jnp.broadcast_to(_rope(k_pe[:, :, None, :], positions), (B, S, MLA_HEADS, MLA_ROPE_DIM))
        k = jnp.concatenate([kv[..., :MLA_NOPE_DIM], k_rope], axis=-1)
        oc = _dense_causal_attention(q, k, kv[..., MLA_NOPE_DIM:],
                                     1.0 / math.sqrt(MLA_NOPE_DIM + MLA_ROPE_DIM)).reshape(B, S, MLA_WIDTH)

        branches = jnp.stack([oa, ob, oc], axis=2)
        br = jnp.einsum('bsgc,gcd->bsgd', branches, w_branch[l])
        gates = jax.nn.sigmoid(g.reshape(B, S, N_BRANCH, D_MODEL))
        mixed = jnp.einsum('bsd,de->bse', jnp.sum(gates * br, axis=2), w_out[l])
        x = x + _rms_norm(mixed, norm_mix_post[l])

        h = _rms_norm(x, norm_mlp_pre[l])
        u = jnp.square(jax.nn.relu(jnp.einsum('bsd,df->bsf', h, w_up[l])))
        x = x + _rms_norm(jnp.einsum('bsf,fd->bsd', u, w_down[l]), norm_mlp_post[l])
    return x


def setup_inputs(seed=0):
    out = dict(first_inputs(seed))
    for name, value in second_inputs(seed + 1).items():
        if name != "x":
            out[name + "_2"] = value
    return out


def reference(
    x, c, ctx, c_ctx, w_mod, b_mod, norm_g, ffn_w_in, ffn_w_out, ret_w_in, ret_w_out, ret_gn_g,
    ret_decay_f, ret_decay_b, nat_w_qkv, nat_w_o, nat_rpb, pool_w, pool_scale, swa_w_qkv,
    swa_w_o, swa_sink, final_norm_g, positions_2, rel_bias_2, norm_mix_pre_2, norm_mix_post_2,
    norm_mlp_pre_2, norm_mlp_post_2, w_in_2, diff_lambda_2, diff_subln_2, mla_q_norm_2,
    mla_w_uq_2, mla_kv_norm_2, mla_w_ukv_2, w_branch_2, w_out_2, w_up_2, w_down_2,
):
    x = first_block(
        x, c, ctx, c_ctx, w_mod, b_mod, norm_g, ffn_w_in, ffn_w_out, ret_w_in, ret_w_out,
        ret_gn_g, ret_decay_f, ret_decay_b, nat_w_qkv, nat_w_o, nat_rpb, pool_w, pool_scale,
        swa_w_qkv, swa_w_o, swa_sink, final_norm_g,
    )
    return second_block(
        x, positions_2, rel_bias_2, norm_mix_pre_2, norm_mix_post_2, norm_mlp_pre_2,
        norm_mlp_post_2, w_in_2, diff_lambda_2, diff_subln_2, mla_q_norm_2, mla_w_uq_2,
        mla_kv_norm_2, mla_w_ukv_2, w_branch_2, w_out_2, w_up_2, w_down_2,
    )


_drawn_inputs = setup_inputs


def setup_inputs(seed=0):
    import zlib

    import numpy as np

    out = dict(_drawn_inputs(seed))
    spreads = {}
    factors = {'norm_g': 3.723,
     'ret_gn_g': 8.0,
     'nat_rpb': 8.0,
     'mla_q_norm_2': 5.756,
     'mla_kv_norm_2': 2.858}
    for name, (base, spread) in spreads.items():
        noise = np.random.default_rng([zlib.crc32(name.encode()), seed]).standard_normal(out[name].shape)
        drawn = base * np.exp(spread * noise) if base else spread * noise
        out[name] = jnp.asarray(drawn.astype(out[name].dtype))
    for name, factor in factors.items():
        out[name] = (out[name] * factor).astype(out[name].dtype)
    return out
```

```python
from contextlib import ExitStack

import numpy as np
import concourse.bass as bass
from concourse import mybir

F32 = mybir.dt.float32
F32R = mybir.dt.float32r
I32 = mybir.dt.int32
ALU = mybir.AluOpType
ACT = mybir.ActivationFunctionType
AX = mybir.AxisListType

P = 128
D = 1024
DC = D // P
T = 256
T2 = 2 * T
EPS = 1e-6
NEG = -1e30
FFN = 2816
FC = FFN // P
FH = FC // 2
WB = 256
BLK = DC * WB
RAW = 4
SPL = 2
RH, NH, DH, MH = 4, 16, 4, 8
NMOD = 72
LOG2PI = (6.28125, 0.0019350051879882812, 2.0 * np.pi - 6.28125 - 0.0019350051879882812)
LAM_INIT = [0.8 - 0.6 * float(np.exp(-0.3 * l)) for l in range(2)]

C_ID, C_MASK, C_CAUSAL, C_INV, C_ROT, C_REV, C_REV64, C_HOT = 0, 128, 192, 320, 321, 353, 481, 609
C_SMALL = 609 + 512
C_COS, C_SIN, C_DF, C_DB, C_DIFF = 0, 256, 512, 896, 1280
C_RET = 1664


def shape_constants():
    p = np.arange(P)[:, None]
    small = np.zeros((P, C_SMALL), np.float32)
    small[:, C_ID:C_ID + P] = np.eye(P)
    small[:, C_REV:C_REV + P] = np.eye(P)[::-1]
    small[:, C_REV64:C_REV64 + P] = np.kron(np.eye(2), np.eye(64)[::-1])
    col, key = 63 - p % 64, np.arange(64)[None]
    lo = np.clip(col - 8, 0, 48)
    small[:, C_MASK:C_MASK + 64] = np.where((key >= lo) & (key < lo + 16), 0.0, NEG)
    small[:, C_CAUSAL:C_CAUSAL + P] = np.where(np.arange(P)[None] <= p, 0.0, NEG)
    inv = np.float32(10000.0) ** (-np.arange(16, dtype=np.float32) * np.float32(2.0) / np.float32(32))
    small[64:80, C_INV] = inv
    small[80:96, C_INV] = inv
    for i in range(16):
        small[64 + i + 16, C_ROT + i] = -1.0
        small[64 + i, C_ROT + i + 16] = 1.0
    rel = 255 - np.arange(512)
    n = np.maximum(rel, 0)
    nf = np.maximum(n, 1).astype(np.float32)
    large = 16 + (np.log(nf / np.float32(16)) / np.float32(np.log(64.0)) * np.float32(16)).astype(np.int32)
    bucket = np.where(n < 16, n, np.minimum(large, 31))
    for x in range(512):
        if rel[x] >= 0:
            small[bucket[x], C_HOT + x] = 1.0
        else:
            small[32, C_HOT + x] = NEG
    ret = np.zeros((P, C_RET), np.float32)
    invr = np.float32(10000.0) ** (-np.arange(0, 256, 2, dtype=np.float32) / np.float32(256))
    ang = invr[:, None] * np.arange(T, dtype=np.float32)[None]
    ret[:, C_COS:C_COS + T] = np.cos(ang)
    ret[:, C_SIN:C_SIN + T] = np.sin(ang)
    diff = np.arange(384)[None] - 128 - p
    ret[:, C_DF:C_DF + 384] = np.maximum(diff, 0)
    ret[:, C_DB:C_DB + 384] = np.maximum(-diff, 0)
    ret[:, C_DIFF:C_DIFF + 384] = diff
    return small, ret


VA = {"b_mod0": 0, "norm_g": 72, "final": 120}
VB = {"b_mod1": 0, "gn_g": 72, "c": 88, "c_ctx": 96}
VC = {"mix_pre": 0, "mix_post": 16, "mlp_pre": 32, "mlp_post": 48, "q_norm": 64, "kv_norm": 68, "subln": 70}
NVB, NVC = 104, 72


class Gemm:

    def __init__(self, name, kind, groups, x, tok, dst=None, arg=None):
        self.name, self.kind, self.groups, self.x, self.tok = name, kind, groups, x, tok
        self.dst, self.arg = dst, arg
        self.per_group = len(groups[0][1])


def program(nc, A):
    ctx = ExitStack()
    with ctx:
        def sem(name):
            return ctx.enter_context(nc.semaphore(name))

        def keep(name, shape, dt=F32):
            return ctx.enter_context(nc.sbuf_tensor(name, shape, dt))

        raw = [keep(f"raw{i}", [P, BLK]) for i in range(RAW)]
        wh = [keep(f"w_high{i}", [P, BLK], F32R) for i in range(SPL)]
        wl = [keep(f"w_low{i}", [P, BLK], F32R) for i in range(SPL)]
        h = keep("h", [P, DC, T2])
        cst = keep("cst", [P, C_HOT])
        ones = keep("ones", [P, P])
        vecA = keep("vecA", [P, P])
        vecB = keep("vecB", [P, NVB])
        vecC = keep("vecC", [P, NVC])
        mod = keep("mod", [P, 2 * NMOD, 2])
        nsc = keep("nsc", [P, 6, DC, 2])
        half = keep("half", [P, 6, DC, 2])
        zero = keep("zero", [P, 1])
        eps = keep("eps", [P, 1])
        sc = keep("sc", [P, DC, 2])
        mrow = keep("mrow", [2, 4, WB])
        dec = keep("dec", [P, 8])
        lg = keep("lg", [P, 6, 8])
        lam = keep("lam", [P, 8])
        lamn = keep("lam_negated", [P, 2])
        dxb = keep("decay_negated", [P, 1])
        std = keep("std", [P, T2])
        rstd = keep("rstd", [P, T2])
        ident = cst[:, C_ID:C_ID + P]

        def first_named(tensors, prefix):
            return [(prefix + n, sh, dt) for n, sh, dt in tensors]

        def scope(tensors):
            with ExitStack() as s:
                return [s.enter_context(nc.sbuf_tensor(n, sh, dt)) for n, sh, dt in tensors]

        first = [("xh", [P, DC, T2], F32R), ("xl", [P, DC, T2], F32R), ("xt", [P, 4, T], F32),
                 ("sq", [P, 2, T2], F32), ("hf", [P, 2, T2], F32)]
        xh, xl, xt, sq, hf, hidh, hidl = scope(
            first + [("hid_high", [P, FH, T2], F32R), ("hid_low", [P, FH, T2], F32R)])
        sa = sq
        xrows = scope(first_named(first, "i_") + [("pad0", [P, 11 * T2], F32), ("xrows", [P, 4, D], F32), ("vrows", [P, 3, P], F32),
                               ("lamv", [P, 2, 4, 64], F32), ("lamp", [P, 2, 2, 64], F32), ("rpbp", [112, 127], F32),
                               ("gt5", [8, 512], F32), ("tab", [33, 8], F32),
                               ("hot", [33, 512], F32)])[6:]
        xrows, vrows, lamv, lamp, rpbp, gt5, tab, hot = xrows
        oh, ol, cret, qk, qr, vr, gr, att, oc, dx = scope(first_named(first, "r_") + [
            ("ret_high", [P, 4, T2], F32R), ("ret_low", [P, 4, T2], F32R), ("cret", [P, C_RET], F32),
            ("qk", [P, 4, T2], F32), ("qr", [P, 4, T], F32), ("vr", [P, 4, T2], F32), ("gr", [P, 4, T2], F32),
            ("att", [P, 6, T], F32), ("oc", [P, 4, T2], F32), ("dx", [P, 3, 384], F32)])[5:]
        att_bufs = [("pexp", [P, 2, 512], F32), ("ptr", [P, 2, 512], F32), ("dg", [P, 2, P], F32),
                    ("stat", [P, 4, 8], F32)]
        nah, nal, nq, nk, nv, tt, pexp, ptr, dg, stat = scope(first_named(first, "n_") + [
            ("nat_high", [P, DC, T], F32R), ("nat_low", [P, DC, T], F32R), ("nq", [P, DC, T], F32),
            ("nk", [P, DC, T2], F32), ("nv", [P, 4, D], F32), ("tt", [P, 2, 6, 64], F32)] + att_bufs)[5:]
        (yh, yl, yt, sq2, hf2, ah, al, q2, k2, v2, cqh, cql, ckh, ckl, mq, mk, mv, t5, ang, po, oraw,
         pexp2, ptr2, dg2, stat2) = scope([
             ("yh", [P, DC, T], F32R), ("yl", [P, DC, T], F32R), ("yt", [P, 4, T], F32), ("sq2", [P, 2, T], F32),
             ("hf2", [P, 2, T], F32), ("act_high", [P, 12, T], F32R), ("act_low", [P, 12, T], F32R),
             ("q2", [P, 4, T], F32), ("k2", [P, 4, T], F32), ("v2", [P, 2, 512], F32),
             ("cq_high", [P, 2, T], F32R), ("cq_low", [P, 2, T], F32R), ("ckv_high", [P, 1, T], F32R),
             ("ckv_low", [P, 1, T], F32R), ("mq", [P, MH, T], F32), ("mk", [P, MH, T], F32),
             ("mv", [P, 2, 512], F32), ("t5", [P, 8, 384], F32), ("ang", [P, 4, T], F32), ("posi", [P, T], I32),
             ("oraw", [P, 4, T], F32)]
             + [(n + "2", [s[0], s[1], min(s[2], T)], d) for n, s, d in att_bufs])
        cq, ckv, kpe = oraw[:, 0:2, :], oraw[:, 2, :], oraw[:, 3, :]
        rows_of = t5[:, :, :].rearrange("p a b -> p (a b)")
        out_buf = [rows_of[:, D * t:D * t + D] for t in range(2)]
        sig, mixed = mq, mk
        yb = mixed

        bank = [ctx.enter_context(nc.psum_tensor(f"gemm{i}", [P, 512], F32)) for i in range(4)]
        aux = [ctx.enter_context(nc.psum_tensor(f"aux{i}", [P, 512], F32)) for i in range(4)]

        rpb_dram = nc.dram_tensor("rpb_padded", [112, 127], F32)
        t5_dram = nc.dram_tensor("t5_by_distance", [8, 512], F32)

        def kview(w, k0, nk, c0, n):
            return w[k0 * P:(k0 + nk) * P, c0:c0 + n].rearrange("(k p) n -> p k n", p=P)

        def A_groups(w, cols, kbs=((0, DC),), c00=0):
            return [([(kview(w, k0, nk, c00 + c, WB), k0, nk, WB) for k0, nk in kbs],
                     [("A", 0, P), ("A", P, P)]) for c in range(0, cols, WB)]

        def B_groups(w, cols, tiles, c00=0):
            return [([(kview(w, 0, DC, c00 + c, WB), 0, DC, WB)],
                     [("B", t, lambda ap: ap) for t in range(tiles)]) for c in range(0, cols, WB)]

        gemms = []

        def add(*a, **k):
            gemms.append(Gemm(*a, **k))

        X = (lambda c: xh[:, c, :], lambda c: xl[:, c, :])
        Hd = (lambda c: hidh[:, c, :], lambda c: hidl[:, c, :])

        def ffn(l, f, tok, j):
            w_in, w_out = A["ffn_w_in"][l, f], A["ffn_w_out"][l, f]
            for s in range(2):
                groups = []
                for g in range(FH):
                    c0 = (s * FH + g) * P
                    ap = w_in[:, :].rearrange("(k p) (s n) -> p k s n", p=P, s=2)[:, :, :, c0:c0 + P]
                    groups.append(([(ap, 0, DC, WB)], [("A", 0, P), ("A", P, P)]))
                add(f"in{l}{f}{s}", "swiglu", groups, X, tok)
                add(f"out{l}{f}{s}", "resid", A_groups(w_out, D, ((s * FH, 6), (s * FH + 6, 5))),
                    (lambda c, s=s: hidh[:, c - s * FH, :], lambda c, s=s: hidl[:, c - s * FH, :]), tok, arg=3 * l + j)

        ffn(0, 0, (0, T2), 0)
        wr = A["ret_w_in"][0]
        Rt = (lambda c: oh[:, c % 4, :], lambda c: ol[:, c % 4, :])

        def ret_out(hh):
            add(f"ret_out{hh}", "resid", A_groups(A["ret_w_out"][0], D, ((4 * hh, 4),)), Rt, (0, T2), arg=1)

        for hh in range(RH):
            add(f"ret_q{hh}", "scaled", A_groups(wr, 256, c00=256 * hh), X, (0, T2),
                dst=lambda i: qk[:, i, :], arg=1.0)
            add(f"ret_k{hh}", "scaled", A_groups(wr, 256, c00=1024 + 256 * hh), X, (0, T2),
                dst=lambda i: qk[:, 2 + i, :], arg=1.0 / 16)
            add(f"ret_v{hh}", "scaled", B_groups(wr, 512, 4, c00=2048 + 512 * hh), X, (0, T2),
                dst=lambda i: vr[:, i % 4, (i // 4) * WB:(i // 4 + 1) * WB], arg=1.0)
            add(f"ret_g{hh}", "silu", A_groups(wr, 512, c00=4096 + 512 * hh), X, (0, T2),
                dst=lambda i: gr[:, i, :])
            ret_out(hh)
        ffn(0, 1, (0, T2), 2)
        ffn(1, 0, (0, T2), 0)
        wn = A["nat_w_qkv"][0]
        add("nat_q", "scaled", A_groups(wn, D), X, (0, T), dst=lambda i: nq[:, i, :], arg=0.125)
        add("nat_k", "scaled", A_groups(wn, D, c00=D), X, (0, T2), dst=lambda i: nk[:, i, :], arg=1.0)
        add("nat_v", "scaled", B_groups(wn, D, 4, c00=2 * D), X, (0, T2),
            dst=lambda i: nv[:, i % 4, (i // 4) * WB:(i // 4 + 1) * WB], arg=1.0)
        add("nat_o", "resid", A_groups(A["nat_w_o"][0], D), (lambda c: nah[:, c, :], lambda c: nal[:, c, :]),
            (0, T), arg=4)
        ffn(1, 1, (0, T), 2)
        Y = (lambda c: yh[:, c, :], lambda c: yl[:, c, :])
        L = (0, T)
        v2dst = lambda i: v2[:, i % 2, (i // 2) * WB:(i // 2 + 1) * WB]
        for l in range(2):
            w = A["w_in_2"][l]
            for a, (name, s) in enumerate((("diff", 0.125), ("moba", float(128 ** -0.5)))):
                o = 1536 * a
                add(f"{name}_q{l}", "scaled", A_groups(w, 512, c00=o), Y, L, dst=lambda i: q2[:, i, :], arg=s)
                add(f"{name}_k{l}", "scaled", A_groups(w, 512, c00=o + 512), Y, L, dst=lambda i: k2[:, i, :], arg=1.0)
                add(f"{name}_v{l}", "scaled", B_groups(w, 512, 2, c00=o + 1024), Y, L, dst=v2dst, arg=1.0)
            add(f"mla_cq{l}", "scaled", A_groups(w, 256, c00=3072), Y, L, dst=lambda i: cq[:, i, :], arg=1.0)
            add(f"mla_ckv{l}", "scaled", [([(kview(w, 0, DC, 3328, 160), 0, DC, 160)],
                                          [("A", 0, P), ("A", 64, 96)])], Y, L,
                dst=lambda i: (ckv[:, :], kpe[64:96, :])[i], arg=1.0)
            add(f"mla_uq{l}", "scaled", [([(kview(A["mla_w_uq_2"][l], 0, 2, 0, 768), 0, 2, 768)],
                                         [("A", 96 * i, 96) for i in range(MH)])],
                (lambda c: cqh[:, c, :], lambda c: cql[:, c, :]), L, dst=lambda i: mq[0:96, i, :],
                arg=float(96 ** -0.5))
            vcols = lambda ap: ap.rearrange("p (h n) -> p h n", h=MH)[:, :, 64:128]
            add(f"mla_ukv{l}", "scaled", [([(kview(A["mla_w_ukv_2"][l], 0, 1, 0, 1024), 0, 1, 1024)],
                                          [("A", P * i, P) for i in range(MH)] + [("B", t, vcols) for t in range(2)])],
                (lambda c: ckh[:, c, :], lambda c: ckl[:, c, :]), L,
                dst=lambda i: mk[0:64, i, :] if i < MH else mv[:, i - MH, :], arg=1.0)
            for g in range(3):
                add(f"gate{g}{l}", "sigmoid", A_groups(w, D, c00=3488 + g * D), Y, L, dst=lambda i: sig[:, i, :])
                add(f"branch{g}{l}", "mix", A_groups(A["w_branch_2"][l, g], D, ((0, 4),)),
                    (lambda c, g=g: ah[:, 4 * g + c, :], lambda c, g=g: al[:, 4 * g + c, :]), L, arg=g)
            add(f"mixed{l}", "copy_y", A_groups(A["w_out_2"][l], D), Y, L, arg=0)
            for s in range(4):
                add(f"up{l}{s}", "relu2", A_groups(A["w_up_2"][l], D, c00=s * D), Y, L)
                add(f"down{l}{s}", "copy_y", A_groups(A["w_down_2"][l], D, ((s * DC, DC),)),
                    (lambda c, s=s: ah[:, c - s * DC, :], lambda c, s=s: al[:, c - s * DC, :]), L, arg=s)

        chunks = blocks = hids = mixes = partials = relus = 0
        block_list, used = [], []
        G = {}
        for g in gemms:
            G[g.name] = g
            g.n0, g.s0, g.hid0, g.mix0, g.rl0 = chunks, blocks, hids, mixes, relus
            for bl, ch in g.groups:
                chunks += len(ch)
                for i, b in enumerate(bl):
                    block_list.append(b)
                    blocks += 1
                    if i == len(bl) - 1:
                        used.append(("chunk", chunks))
                    else:
                        partials += 1
                        used.append(("partial", partials))
            g.n1 = chunks
            g.nch = g.n1 - g.n0
            hids += {"swiglu": g.nch // 2, "relu2": g.nch}.get(g.kind, 0)
            relus += g.nch if g.kind == "relu2" else 0
            mixes += g.nch if g.kind == "mix" and g.arg else 0
        NB = blocks

        norms = {}
        order = []

        def add_norm(name, **k):
            k["u"] = len(order)
            norms[name] = k
            order.append(name)

        def nmod(l, j):
            return dict(scale=lambda c, ts: nsc[:, 3 * l + j, c, ts:ts + 1],
                        bias=lambda c, ts: mod[:, l * NMOD + 24 * j + c, ts:ts + 1])

        def gcol(v, o):
            return dict(scale=lambda c, ts: v[:, o + c:o + c + 1], bias=lambda c, ts: zero[:, 0:1])

        N1 = dict(buf=(xh, xl, xt, sq), nc=DC, dim=D, src=lambda c: h[:, c, :])
        N2 = dict(buf=(yh, yl, yt, sq2), nc=DC, dim=D, src=lambda c: h[:, c, :])
        for l in range(2):
            for j in range(3):
                add_norm(f"n{l}{j}", **N1, tok=T if (l, j) == (1, 2) else T2, how="split", **nmod(l, j),
                         after={(0, 0): "init", (0, 1): "out001", (0, 2): "ret_out3", (1, 0): "out011",
                                (1, 1): "out101", (1, 2): "nat_o"}[l, j])
        add_norm("final", **N1, tok=T, how="assign", **gcol(vecA, VA["final"]), after="out111")
        for l in range(2):
            add_norm(f"mix_pre{l}", **N2, tok=T, how="split", **gcol(vecC, VC["mix_pre"] + 8 * l), after="self")
            add_norm(f"cq{l}", buf=(cqh, cql, yt, sq2), nc=2, dim=256, src=lambda c: cq[:, c, :], tok=T, how="split",
                     **gcol(vecC, VC["q_norm"] + 2 * l), after=f"mla_cq{l}")
            add_norm(f"ckv{l}", buf=(ckh, ckl, yt, sq2), nc=1, dim=128, src=lambda c: ckv[:, :], tok=T, how="split",
                     **gcol(vecC, VC["kv_norm"] + l), after=f"mla_ckv{l}")
            add_norm(f"mix_post{l}", **(N2 | dict(src=lambda c: yb[:, c, :])), tok=T, how="add",
                     **gcol(vecC, VC["mix_post"] + 8 * l), after=f"mixed{l}")
            add_norm(f"mlp_pre{l}", **N2, tok=T, how="split", **gcol(vecC, VC["mlp_pre"] + 8 * l), after="self")
            add_norm(f"mlp_post{l}", **(N2 | dict(src=lambda c: yb[:, c, :])), tok=T, how="add",
                     **gcol(vecC, VC["mlp_post"] + 8 * l), after=f"down{l}3")
        sqs = pieces = updates = 0
        for name in order:
            N = norms[name]
            N["sq0"], N["p0"], N["up0"] = sqs, pieces, updates
            sqs += N["nc"]
            if N["how"] == "split":
                pieces += N["nc"] * (N["tok"] // T)
            else:
                updates += N["nc"]

        class Att:
            pass

        atts = {}
        unit_total = tile_total = 0

        def add_att(name, tiles, bufs):
            nonlocal unit_total, tile_total
            a = Att()
            a.name, a.tiles, a.bufs = name, tiles, bufs
            a.u0, a.t0 = unit_total, tile_total
            a.units = [(t, i) for t, tile in enumerate(tiles) for i in range(len(tile["units"]))]
            unit_total += len(a.units)
            tile_total += len(tiles)
            a.u1, a.t1 = unit_total, tile_total
            atts[name] = a

        tiles = []
        for hd in range(NH):
            c, r = hd // 2, 64 * (hd % 2)
            for qt in range(2):
                tiles.append(dict(
                    units=[dict(qk=(nq[r:r + 64, c, P * qt:P * qt + P], nk[r:r + 64, c, :]), coef=None,
                                bias=(0, T, tt[:, hd % 2, 2 - 2 * qt:6 - 2 * qt, :]))],
                    keys=512, rows=(r, r + 64),
                    v=lambda k, hd=hd: nv[:, k, 64 * hd:64 * hd + 64],
                    out=(nah[r:r + 64, c, P * qt:P * qt + P], nal[r:r + 64, c, P * qt:P * qt + P]),
                    head=hd))
        add_att("nat", tiles, (pexp, ptr, dg, stat))
        for l in range(2):
            B2 = (pexp2, ptr2, dg2, stat2)
            tiles = []
            for hd in range(DH):
                for qt in range(2):
                    n = P * (qt + 1)
                    y0 = P * (1 - qt)
                    tiles.append(dict(
                        units=[dict(qk=(q2[r:r + 64, hd, P * qt:P * qt + P], k2[r:r + 64, hd, 0:n]), coef=co,
                                    bias=(0, n, t5[:, hd, y0:y0 + n])) for r, co in ((0, None), (64, l))],
                        keys=n, rows=(0, P), v=lambda k, hd=hd: v2[:, k, P * hd:P * hd + P],
                        out=oraw[:, hd, P * qt:P * qt + P], head=hd))
            add_att(f"diff{l}", tiles, B2)
            tiles = []
            for hd in range(DH):
                for qt in range(2):
                    n = P * (qt + 1)
                    y0 = P * (1 - qt)
                    tiles.append(dict(
                        units=[dict(qk=(q2[:, hd, P * qt:P * qt + P], k2[:, hd, 0:n]), coef=None,
                                    bias=(0, n, t5[:, 4 + hd, y0:y0 + n]))],
                        keys=n, rows=(0, P), v=lambda k, hd=hd: v2[:, k, P * hd:P * hd + P],
                        out=(ah[:, 4 + hd, P * qt:P * qt + P], al[:, 4 + hd, P * qt:P * qt + P]), head=hd))
            add_att(f"moba{l}", tiles, B2)
            tiles = []
            for hd in range(MH):
                r = 64 * (hd % 2)
                for qt in range(2):
                    n = P * (qt + 1)
                    tiles.append(dict(
                        units=[dict(qk=(mq[0:96, hd, P * qt:P * qt + P], mk[0:96, hd, 0:n]), coef=None,
                                    bias=(P * qt, P * qt + P, cst[:, C_CAUSAL:C_CAUSAL + P]))],
                        keys=n, rows=(r, r + 64), v=lambda k, hd=hd: mv[:, k, 64 * hd:64 * hd + 64],
                        out=(ah[r:r + 64, 8 + hd // 2, P * qt:P * qt + P], al[r:r + 64, 8 + hd // 2, P * qt:P * qt + P]),
                        head=hd))
            add_att(f"mla{l}", tiles, B2)

        consts_in = sem("consts_in")
        rows_in = sem("rows_in")
        x_in = sem("x_in")
        small_in = sem("small_in")
        ret_consts_in = sem("ret_consts_in")
        raw_in = [sem(f"raw_in{i}") for i in range(RAW)]
        chunk_mod = sem("mod_row_in_psum")
        mod_row = sem("mod_row")
        mod_cols = sem("mod_cols")
        mod_out = sem("mod_out")
        w_high = sem("w_high_ready")
        w_low = sem("w_low_ready")
        block_used = sem("partial_block_used")
        chunk_ready = sem("chunk_ready")
        even_free = sem("even_chunk_out")
        odd_free = sem("odd_chunk_out")
        hid_f = sem("hidden_ready")
        hid_high = sem("hidden_high_ready")
        hid_low = sem("hidden_low_ready")
        mix_f = sem("mixed_ready")
        mix_high = sem("mixed_high_ready")
        mix_low = sem("mixed_low_ready")
        sq_ready = sem("square_ready")
        sq_used = sem("square_used")
        std_ready = sem("std_ready")
        rstd_ready = sem("rstd_ready")
        xt_ready = sem("scaled_ready")
        x_high = sem("x_high_ready")
        x_low = sem("x_low_ready")
        h_update = sem("h_updated")
        dve_chain = sem("dve_chain")
        act_chain = sem("act_chain")
        pool_ready = sem("pool_ready")
        vec_turned = sem("vectors_turned")
        vec_ready = sem("vectors_ready")
        x_turned = sem("x_turned")
        h_init = sem("h_init")
        c_silu = sem("c_silu")
        cexp = sem("decay_exp")
        cabs = sem("decay_abs")
        cln = sem("decay_ln")
        lg_ready = sem("log_decay_ready")
        lam_dots = sem("lambda_dots")
        lam_exp = sem("lambda_exp")
        coef_ready = sem("coefficients_ready")
        t5_g = sem("t5_product")
        t5_row = sem("t5_row_ready")
        t5_out = sem("t5_stored")
        t5_in = sem("t5_loaded")
        rpb_in = sem("rpb_in")
        rpb_out = sem("rpb_stored")
        tt_in = [sem(f"nat_bias_in{i}") for i in range(2)]
        tt_masked = sem("nat_bias_masked")
        rd_exp = sem("ret_decay_terms")
        rd_x = sem("ret_cross_ready")
        r_rope = sem("ret_rope_ready")
        r_score = sem("ret_scores_ready")
        r_att = sem("ret_weights_ready")
        r_o = sem("ret_o_ready")
        r_of = sem("ret_o_out")
        r_mu = sem("ret_mean_ready")
        r_cen = sem("ret_centred")
        r_sq = sem("ret_square")
        r_sqf = sem("ret_square_used")
        r_std = sem("ret_std_ready")
        r_gat = sem("ret_gated")
        r_high = sem("ret_high_ready")
        r_low = sem("ret_low_ready")
        s_ready = sem("scores_ready")
        s_max = sem("scores_max")
        p_ready = sem("probs_ready")
        dg_ready = sem("diagonal_ready")
        p_used = sem("probs_used")
        pt_out = sem("turned_probs_out")
        o_ready = sem("attention_out_ready")
        o_high = sem("attention_high_ready")
        o_low = sem("attention_low_ready")
        pos_in = sem("positions_in")
        ang_r = sem("angles_ready")
        sin_ready = sem("sines_ready")
        rot_x = sem("rotated_ready")
        rot_used = sem("rotated_used")
        roped = sem("rope_done")
        sub_sq = sem("subln_square")
        sub_ms = sem("subln_mean_square")
        sub_std = sem("subln_std")
        sub_t = sem("subln_scaled")
        sub_high = sem("subln_high")
        sub_low = sem("subln_low")
        out_turned = sem("out_turned")
        out_rows = sem("out_rows_ready")
        out_stored = sem("out_stored")

        def wait_chunk_out(eng, n):
            eng.wait_ge(odd_free if n % 2 else even_free, n // 2 + 1)

        def wait_gemm_out(eng, name):
            wait_chunk_out(eng, G[name].n1 - 2)
            wait_chunk_out(eng, G[name].n1 - 1)

        def scaled_src(g, i, ps, dst):
            r0 = 64 if g.name[:7] == "mla_ckv" and i == 1 else 0
            return ps[r0:r0 + dst.shape[0], 0:dst.shape[1]]

        def free(n):
            return odd_free if n % 2 else even_free

        def wait_block_used(eng, s):
            kind, v = used[s]
            eng.wait_ge(chunk_ready if kind == "chunk" else block_used, v)

        def wait_source(eng, N, c):
            a = N["after"]
            if a == "init":
                eng.wait_ge(h_init, c + 1)
            elif a == "self":
                if N["up0"]:
                    eng.wait_ge(h_update, N["up0"])
            else:
                wait_chunk_out(eng, G[a].n1 - N["nc"] + c if a[:7] != "mla_ckv" else G[a].n0)

        class Chain:

            def __init__(self, eng, s):
                self.eng, self.s, self.n = eng, s, 0

            def __call__(self, ins):
                self.n += 1
                ins.then_inc(self.s, 1)
                self.eng.wait_ge(self.s, self.n)

        block = ctx.enter_context(nc.Block())

        @block.sync
        def _(sp):
            sp.dma_start(cst[:, :], A["consts"][:, 0:C_HOT]).then_inc(consts_in, 16)
            for r0, n, i, src in (
                    (VA["b_mod0"], 72, 0, A["b_mod"][0:1]), (VA["norm_g"], 48, 0, A["norm_g"]),
                    (VA["final"], 8, 0, A["final_norm_g"]), (VB["b_mod1"], 72, 1, A["b_mod"][1:2]),
                    (VB["gn_g"], 16, 1, A["ret_gn_g"]), (VB["c"], 8, 1, A["c"]), (VB["c_ctx"], 8, 1, A["c_ctx"]),
                    (VC["mix_pre"], 16, 2, A["norm_mix_pre_2"]), (VC["mix_post"], 16, 2, A["norm_mix_post_2"]),
                    (VC["mlp_pre"], 16, 2, A["norm_mlp_pre_2"]), (VC["mlp_post"], 16, 2, A["norm_mlp_post_2"]),
                    (VC["q_norm"], 4, 2, A["mla_q_norm_2"]), (VC["kv_norm"], 2, 2, A["mla_kv_norm_2"]),
                    (VC["subln"], 2, 2, A["diff_subln_2"])):
                flat = src
                if len(src.shape) == 3:
                    flat = src.rearrange("a b (r n) -> (a b r) n", n=P)
                elif len(src.shape) == 2:
                    flat = src.rearrange("a (r n) -> (a r) n", n=P)
                else:
                    flat = src.rearrange("(r n) -> r n", n=P)
                sp.dma_start(vrows[r0:r0 + n, i, :], flat).then_inc(rows_in, 16)

            def load_block(b):
                slot = b % RAW
                if b >= RAW:
                    prev = b - RAW
                    if prev < NMOD:
                        sp.wait_ge(chunk_mod, prev + 1)
                    else:
                        sp.wait_ge(w_low, prev - NMOD + 1)
                if b < NMOD:
                    l, c0 = b // 36, (b % 36) * WB
                    ap, nk, w = kview(A["w_mod"][l], 0, DC, c0, WB), DC, WB
                    dst = raw[slot][:, :].rearrange("p (k n) -> p k n", k=nk)
                    sp.dma_start(dst, ap).then_inc(raw_in[slot], 16)
                    return
                ap, k0, nk, w = block_list[b - NMOD]
                if len(ap.shape) == 4:
                    for s in range(2):
                        dst = raw[slot][:, 0:nk * w].rearrange("p (k s n) -> p k s n", k=nk, s=2)[:, :, s, :]
                        sp.dma_start(dst, ap[:, :, s, :]).then_inc(raw_in[slot], 16)
                    return
                dst = raw[slot][:, 0:nk * w].rearrange("p (k n) -> p k n", k=nk)
                sp.dma_start(dst, ap).then_inc(raw_in[slot], 16)

            for b in range(4):
                load_block(b)
            for t in range(4):
                src = A["x"] if t < 2 else A["ctx"]
                sp.dma_start(xrows[:, t, :], src[0, P * (t % 2):P * (t % 2) + P, :]).then_inc(x_in, 16)
            for b in range(4, NMOD + NB):
                load_block(b)
            for t in range(2):
                sp.wait_ge(out_rows, 4 * (t + 1))
                sp.dma_start(A["out"][0, P * t:P * t + P, :],
                             out_buf[t]).then_inc(out_stored, 16)
            sp.wait_ge(out_stored, 32)

        raw_value, counts = [], [0] * RAW
        for b in range(NMOD + NB):
            two = b >= NMOD and len(block_list[b - NMOD][0].shape) == 4
            counts[b % RAW] += 32 if two else 16
            raw_value.append(counts[b % RAW])

        @block.gpsimd
        def _(pool):
            pool.memset(ones[:, :], 1.0).then_inc(pool_ready, 1)
            pool.memset(zero[:, :], 0.0).then_inc(pool_ready, 1)
            pool.memset(eps[:, :], EPS).then_inc(pool_ready, 1)
            pool.memset(rpbp[:, :], 0.0).then_inc(pool_ready, 1)
            pool.memset(tab[:, :], 1.0).then_inc(pool_ready, 1)
            pool.wait_ge(pool_ready, 5)
            dsrc = lambda a: bass.AP(a.tensor, a.offset, [[0, P], [1, 4]])
            pool.dma_start(dec[:, 0:4], dsrc(A["ret_decay_f"])).then_inc(small_in, 16)
            pool.dma_start(dec[:, 4:8], dsrc(A["ret_decay_b"])).then_inc(small_in, 16)
            pool.dma_start(lamv[:, :, :, :], bass.AP(A["diff_lambda_2"].tensor, 0, [[0, P], [1, 512]])).then_inc(small_in, 16)
            pool.dma_start(tab[0:32, :], A["rel_bias_2"]).then_inc(small_in, 16)
            pool.dma_start(hot[:, :], A["consts"][0:33, C_HOT:C_HOT + 512]).then_inc(small_in, 16)
            for hd in range(NH):
                pool.dma_start(rpbp[7 * hd:7 * hd + 7, 48:79], A["nat_rpb"][0, hd, 4:11, :]).then_inc(rpb_in, 16)
            pool.wait_ge(rpb_in, 16 * NH)
            pool.dma_start(rpb_dram.ap(), rpbp[:, :]).then_inc(rpb_out, 16)
            pool.wait_ge(t5_row, 1)
            pool.dma_start(t5_dram.ap(), gt5[:, :]).then_inc(t5_out, 16)
            pool.wait_ge(x_turned, 8)
            pool.wait_ge(h_init, 8)
            pool.wait_ge(coef_ready, 1)
            pool.wait_ge(t5_out, 16)
            pool.wait_ge(rpb_out, 16)
            wait_gemm_out(pool, "out001")
            pool.dma_start(cret[:, :], A["ret_consts"]).then_inc(ret_consts_in, 16)
            wait_gemm_out(pool, "out101")
            for hd in range(NH):
                if hd >= 2:
                    pool.wait_ge(s_ready, atts["nat"].u0 + 2 * (hd - 2) + 2)
                for r2 in range(2):
                    src = bass.AP(rpb_dram, (7 * hd + 1 - r2) * 127, [[1, 64], [127, 6], [1, 64]])
                    pool.dma_start(tt[64 * r2:64 * r2 + 64, hd % 2, :, :], src).then_inc(tt_in[hd % 2], 16)
            pool.wait_ge(x_low, norms["mix_pre0"]["p0"])
            pool.wait_ge(h_update, 8)
            for g in range(8):
                src = bass.AP(t5_dram, g * 512, [[1, P], [1, 384]])
                pool.dma_start(t5[:, g, :], src).then_inc(t5_in, 16)
            pool.dma_start(po[64:96, :], bass.AP(A["positions_2"].tensor, 0, [[0, 32], [1, T]])).then_inc(pos_in, 16)

        @block.scalar
        def _(act):
            chain = Chain(act, act_chain)
            split = [0]

            def splits_upto(s):
                while split[0] <= min(s, NB - 1):
                    i = split[0]
                    _, _, nk, w = block_list[i]
                    act.wait_ge(raw_in[(i + NMOD) % RAW], raw_value[i + NMOD])
                    if i >= SPL:
                        wait_block_used(act, i - SPL)
                    act.activation(wh[i % SPL][:, 0:nk * w], raw[(i + NMOD) % RAW][:, 0:nk * w],
                                   ACT.Copy).then_inc(w_high, 1)
                    split[0] += 1

            def norm(name):
                N = norms[name]
                X_h, X_l, x_t, s_q = N["buf"]
                u, tok = N["u"], N["tok"]
                for c in range(N["nc"]):
                    wait_source(act, N, c)
                    i = N["sq0"] + c
                    if i >= 2:
                        act.wait_ge(sq_used, i - 1)
                    act.activation(s_q[:, i % 2, 0:tok], N["src"](c)[:, 0:tok], ACT.Square).then_inc(sq_ready, 1)
                act.wait_ge(sq_used, N["sq0"] + N["nc"])
                if u >= 1:
                    act.wait_ge(rstd_ready, u)
                act.activation(std[:, 0:tok], aux[3][:, 0:tok], ACT.Sqrt, bias=eps[:, 0:1],
                               scale=1.0 / N["dim"]).then_inc(std_ready, 1)
                if N["how"] == "split":
                    for k in range(N["nc"] * (tok // T)):
                        c, ts = divmod(k, tok // T)
                        p = N["p0"] + k
                        act.wait_ge(xt_ready, p + 1)
                        act.activation(X_h[:, c, ts * T:ts * T + T], x_t[:, p % 4, :], ACT.Identity,
                                       bias=N["bias"](c, ts)).then_inc(x_high, 1)

            def gemm(name):
                g = G[name]
                n, s = g.n0, g.s0
                t0, t1 = g.tok
                tok = t1 - t0
                if n:
                    wait_chunk_out(act, n - 2)
                    wait_chunk_out(act, n - 1)
                for bl, ch in g.groups:
                    s += len(bl)
                    splits_upto(s)
                    for ci, (o, a0, M) in enumerate(ch):
                        i = n - g.n0
                        ps = bank[n % 4]
                        if g.kind == "scaled":
                            if n % 2 == 0:
                                act.wait_ge(chunk_ready, n + 1)
                                dst = g.dst(i)
                                act.activation(dst, scaled_src(g, i, ps, dst), ACT.Copy, scale=g.arg).then_inc(free(n), 1)
                        elif g.kind == "silu":
                            act.wait_ge(chunk_ready, n + 1)
                            act.activation(g.dst(i), ps[:, 0:tok], ACT.Silu).then_inc(free(n), 1)
                        elif g.kind == "sigmoid":
                            act.wait_ge(chunk_ready, n + 1)
                            act.activation(g.dst(i), ps[:, 0:tok], ACT.Sigmoid).then_inc(free(n), 1)
                        elif g.kind == "swiglu":
                            pr = g.hid0 + i // 2
                            if n % 2 == 0:
                                act.wait_ge(chunk_ready, n + 1)
                                if n >= 4:
                                    act.wait_ge(odd_free, n // 2 - 1)
                                act.activation(sa[:, pr % 2, 0:tok], ps[:, 0:tok], ACT.Silu).then_inc(even_free, 1)
                            else:
                                act.wait_ge(odd_free, n // 2 + 1)
                                act.activation(hidh[:, i // 2, 0:tok], hf[:, pr % 2, 0:tok], ACT.Copy).then_inc(hid_high, 1)
                        elif g.kind == "relu2":
                            pr = g.hid0 + i
                            act.wait_ge(hid_f, g.rl0 + i + 1)
                            act.activation(ah[:, i, :], hf2[:, pr % 2, :], ACT.Copy).then_inc(hid_high, 1)
                        elif g.kind == "mix" and g.arg == 2:
                            m = g.mix0 + i
                            act.wait_ge(mix_f, m + 1)
                            act.activation(yh[:, i, :], mixed[:, i, :], ACT.Copy).then_inc(mix_high, 1)
                        n += 1

            def attention(name):
                a = atts[name]
                pe_, pt_, dg_, st_ = a.bufs

                def turn_out(t):
                    tg = a.t0 + t
                    last = a.u0 + max(j for j, (tt_, _) in enumerate(a.units) if tt_ == t)
                    act.wait_ge(p_used, last + 1)
                    if tg >= 2:
                        act.wait_ge(o_ready, tg - 1)
                    k = a.tiles[t]["keys"]
                    act.activation(pt_[:, tg % 2, 0:k], aux[2][:, 0:k], ACT.Copy).then_inc(pt_out, 1)

                def out_high(t):
                    tg = a.t0 + t
                    tile = a.tiles[t]
                    r0, r1 = tile["rows"]
                    act.wait_ge(o_ready, tg + 1)
                    dst = tile["out"][0] if isinstance(tile["out"], tuple) else tile["out"]
                    act.activation(dst, aux[3][r0:r1, 0:P], ACT.Copy).then_inc(o_high, 1)

                for j, (t, i) in enumerate(a.units):
                    u = a.u0 + j
                    k = a.tiles[t]["keys"]
                    act.wait_ge(s_max, u + 1)
                    if u >= 2:
                        act.wait_ge(p_used, u - 1)
                    if u >= 8:
                        act.wait_ge(dg_ready, u - 7)
                    act.activation(pe_[:, u % 2, 0:k], aux[u % 2][:, 0:k], ACT.Exp, bias=st_[:, 0, u % 8:u % 8 + 1],
                                   accum_out=st_[:, 1, u % 8:u % 8 + 1]).then_inc(p_ready, 1)
                    if j and a.units[j - 1][0] != t:
                        turn_out(t - 1)
                        if t >= 2:
                            out_high(t - 2)
                turn_out(len(a.tiles) - 1)
                out_high(len(a.tiles) - 2)
                out_high(len(a.tiles) - 1)

            act.wait_ge(pool_ready, 5)
            act.wait_ge(vec_ready, 3)
            act.activation(sc[:, :, 0], vecB[:, VB["c"]:VB["c"] + 8], ACT.Silu).then_inc(c_silu, 1)
            act.activation(sc[:, :, 1], vecB[:, VB["c_ctx"]:VB["c_ctx"] + 8], ACT.Silu).then_inc(c_silu, 1)
            for c in range(DC):
                act.wait_ge(x_turned, c + 1)
                act.activation(h[:, c, :], aux[c % 4][:, :], ACT.Copy).then_inc(h_init, 1)
            act.wait_ge(small_in, 80)
            chain(act.activation(lg[:, 0, :], dec[:, :], ACT.Abs))
            act.activation(lg[:, 1, :], lg[:, 0, :], ACT.Exp, scale=-1.0).then_inc(cexp, 1)
            act.wait_ge(cabs, 1)
            act.activation(lg[:, 3, :], lg[:, 2, :], ACT.Ln).then_inc(cln, 1)
            act.wait_ge(lam_dots, 1)
            act.activation(lam[:, 4:8], lam[:, 0:4], ACT.Exp).then_inc(lam_exp, 1)
            for b in range(NMOD):
                act.wait_ge(chunk_mod, b + 1)
                if b >= 4:
                    act.wait_ge(mod_cols, b - 3)
                act.activation(mrow[:, b % 4, :], bank[b % 4][0:2, 0:WB], ACT.Copy).then_inc(mod_row, 1)

            def ffn(l, f, j):
                norm(f"n{l}{j}")
                for s in range(2):
                    gemm(f"in{l}{f}{s}")
                    gemm(f"out{l}{f}{s}")

            splits_upto(1)
            act.wait_ge(rpb_out, 16)
            act.wait_ge(t5_out, 16)
            ffn(0, 0, 0)
            norm("n01")
            for hh in range(RH):
                if hh == 0:
                    act.wait_ge(ret_consts_in, 16)
                    act.wait_ge(lg_ready, 3)
                f, b = lg[:, 4, hh:hh + 1], lg[:, 4, 4 + hh:5 + hh]
                f2, b2 = lg[:, 5, hh:hh + 1], lg[:, 5, 4 + hh:5 + hh]
                if hh:
                    act.wait_ge(r_att, 3 * hh)
                act.activation(dx[:, 1, :], cret[:, C_DIFF:C_DIFF + 384], ACT.Exp, bias=f2, scale=f).then_inc(rd_exp, 1)
                act.wait_ge(rd_x, 4 * hh + 1)
                act.activation(dx[:, 2, :], cret[:, C_DIFF:C_DIFF + 384], ACT.Exp, bias=b2,
                               scale=dxb[:, 0:1]).then_inc(rd_exp, 1)
                act.wait_ge(rd_x, 4 * hh + 3)
                act.activation(dx[:, 0, :], dx[:, 0, :], ACT.Exp).then_inc(rd_exp, 1)
                gemm(f"ret_q{hh}")
                gemm(f"ret_k{hh}")
                gemm(f"ret_v{hh}")
                gemm(f"ret_g{hh}")
                for v in range(4):
                    act.wait_ge(r_o, 4 * hh + v + 1)
                    if hh and v == 0:
                        act.wait_ge(r_low, 4 * hh)
                    act.activation(oc[:, v, :], aux[(v + 3) % 4][:, :], ACT.Copy).then_inc(r_of, 1)
                for v in range(4):
                    act.wait_ge(r_cen, 4 * hh + v + 1)
                    i = 4 * hh + v
                    if i >= 2:
                        act.wait_ge(r_sqf, i - 1)
                    act.activation(sa[:, i % 2, :], oc[:, v, :], ACT.Square).then_inc(r_sq, 1)
                act.wait_ge(r_sqf, 4 * hh + 4)
                act.activation(std[:, :], aux[1][:, :], ACT.Sqrt, bias=eps[:, 0:1], scale=1.0 / 512).then_inc(r_std, 1)
                for v in range(4):
                    act.wait_ge(r_gat, 4 * hh + v + 1)
                    act.activation(oh[:, v, :], oc[:, v, :], ACT.Copy).then_inc(r_high, 1)
                gemm(f"ret_out{hh}")
            ffn(0, 1, 2)
            ffn(1, 0, 0)
            norm("n11")
            gemm("nat_q")
            gemm("nat_k")
            gemm("nat_v")
            attention("nat")
            gemm("nat_o")
            ffn(1, 1, 2)
            norm("final")
            act.wait_ge(ang_r, 1)
            act.activation(ang[64:96, 1, :], ang[64:96, 0, :], ACT.Sin).then_inc(sin_ready, 1)
            act.activation(ang[64:96, 2, :], ang[64:96, 0, :], ACT.Sin, scale=0.5).then_inc(sin_ready, 1)
            for l in range(2):
                norm(f"mix_pre{l}")
                for k in "qkv":
                    gemm(f"diff_{k}{l}")
                attention(f"diff{l}")
                for hd in range(DH):
                    i = DH * l + hd
                    act.wait_ge(o_high, atts[f"diff{l}"].t0 + 2 * hd + 2)
                    if i:
                        act.wait_ge(sub_ms, i)
                    act.activation(sq2[:, 0, :], oraw[:, hd, :], ACT.Square).then_inc(sub_sq, 1)
                    act.wait_ge(sub_ms, i + 1)
                    if i:
                        act.wait_ge(sub_t, i)
                    act.activation(std[:, 0:T], aux[3][:, 0:T], ACT.Sqrt, bias=eps[:, 0:1],
                                   scale=1.0 / P).then_inc(sub_std, 1)
                    act.wait_ge(sub_t, i + 1)
                    act.activation(ah[:, hd, :], oraw[:, hd, :], ACT.Copy, scale=1.0 - LAM_INIT[l]).then_inc(sub_high, 1)
                for k in "qkv":
                    gemm(f"moba_{k}{l}")
                attention(f"moba{l}")
                gemm(f"mla_cq{l}")
                gemm(f"mla_ckv{l}")
                norm(f"cq{l}")
                norm(f"ckv{l}")
                gemm(f"mla_uq{l}")
                gemm(f"mla_ukv{l}")
                attention(f"mla{l}")
                for g in range(3):
                    gemm(f"gate{g}{l}")
                    gemm(f"branch{g}{l}")
                gemm(f"mixed{l}")
                norm(f"mix_post{l}")
                norm(f"mlp_pre{l}")
                for s in range(4):
                    gemm(f"up{l}{s}")
                    gemm(f"down{l}{s}")
                norm(f"mlp_post{l}")

        @block.vector
        def _(dve):
            chain = Chain(dve, dve_chain)
            split = [0]

            def splits_upto(s):
                while split[0] <= min(s, NB - 1):
                    i = split[0]
                    _, _, nk, w = block_list[i]
                    dve.wait_ge(w_high, i + 1)
                    dve.tensor_tensor(wl[i % SPL][:, 0:nk * w], raw[(i + NMOD) % RAW][:, 0:nk * w],
                                      wh[i % SPL][:, 0:nk * w].bitcast(F32), ALU.subtract).then_inc(w_low, 1)
                    split[0] += 1

            def norm(name):
                N = norms[name]
                X_h, X_l, x_t, s_q = N["buf"]
                u, tok = N["u"], N["tok"]
                dve.wait_ge(std_ready, u + 1)
                if N["p0"]:
                    dve.wait_ge(x_low, N["p0"])
                dve.reciprocal(rstd[:, 0:tok], std[:, 0:tok]).then_inc(rstd_ready, 1)
                dve.wait_ge(rstd_ready, u + 1)
                if N["how"] != "split":
                    for c in range(N["nc"]):
                        if N["how"] == "assign":
                            dve.scalar_tensor_tensor(out=h[:, c, 0:T], in0=h[:, c, 0:T], scalar=N["scale"](c, 0),
                                                     in1=rstd[:, 0:T], op0=ALU.mult, op1=ALU.mult).then_inc(h_update, 1)
                        else:
                            chain(dve.scalar_tensor_tensor(out=yb[:, c, :], in0=yb[:, c, :], scalar=N["scale"](c, 0),
                                                           in1=rstd[:, 0:T], op0=ALU.mult, op1=ALU.mult))
                            dve.tensor_tensor(h[:, c, 0:T], h[:, c, 0:T], yb[:, c, :], ALU.add).then_inc(h_update, 1)
                    return

                def low(k):
                    c, ts = divmod(k, tok // T)
                    p = N["p0"] + k
                    dve.wait_ge(x_high, p + 1)
                    dve.scalar_tensor_tensor(out=X_l[:, c, ts * T:ts * T + T], in0=x_t[:, p % 4, :],
                                             scalar=N["bias"](c, ts), in1=X_h[:, c, ts * T:ts * T + T].bitcast(F32),
                                             op0=ALU.add, op1=ALU.subtract).then_inc(x_low, 1)

                n = N["nc"] * (tok // T)
                for k in range(n):
                    c, ts = divmod(k, tok // T)
                    p = N["p0"] + k
                    if p >= 4:
                        dve.wait_ge(x_low, p - 3)
                    dve.scalar_tensor_tensor(out=x_t[:, p % 4, :], in0=N["src"](c)[:, ts * T:ts * T + T],
                                             scalar=N["scale"](c, ts), in1=rstd[:, ts * T:ts * T + T],
                                             op0=ALU.mult, op1=ALU.mult).then_inc(xt_ready, 1)
                    if k >= 2:
                        low(k - 2)
                for k in range(max(0, n - 2), n):
                    low(k)

            def gemm(name):
                g = G[name]
                n, s = g.n0, g.s0
                t0, t1 = g.tok
                tok = t1 - t0
                if n:
                    wait_chunk_out(dve, n - 2)
                    wait_chunk_out(dve, n - 1)
                for bl, ch in g.groups:
                    s += len(bl)
                    splits_upto(s)
                    for ci, (o, a0, M) in enumerate(ch):
                        i = n - g.n0
                        ps = bank[n % 4]
                        if g.kind == "scaled":
                            if n % 2:
                                dve.wait_ge(chunk_ready, n + 1)
                                dst = g.dst(i)
                                dve.tensor_scalar(dst, scaled_src(g, i, ps, dst), g.arg, None,
                                                  ALU.mult).then_inc(free(n), 1)
                        elif g.kind == "resid":
                            dve.wait_ge(chunk_ready, n + 1)
                            for ts in range(tok // T):
                                ins = dve.scalar_tensor_tensor(
                                    out=h[:, i, ts * T:ts * T + T], in0=ps[:, ts * T:ts * T + T],
                                    scalar=half[:, g.arg, i, ts:ts + 1], in1=h[:, i, ts * T:ts * T + T],
                                    op0=ALU.mult, op1=ALU.add)
                            ins.then_inc(free(n), 1)
                        elif g.kind == "swiglu":
                            pr = g.hid0 + i // 2
                            if n % 2:
                                dve.wait_ge(chunk_ready, n + 1)
                                dve.wait_ge(even_free, n // 2 + 1)
                                if pr >= 2:
                                    dve.wait_ge(hid_low, pr - 1)
                                dve.tensor_tensor(hf[:, pr % 2, 0:tok], sa[:, pr % 2, 0:tok], ps[:, 0:tok],
                                                  ALU.mult).then_inc(odd_free, 1)
                                dve.wait_ge(hid_high, pr + 1)
                                dve.tensor_tensor(hidl[:, i // 2, 0:tok], hf[:, pr % 2, 0:tok],
                                                  hidh[:, i // 2, 0:tok].bitcast(F32), ALU.subtract).then_inc(hid_low, 1)
                        elif g.kind == "relu2":
                            pr = g.hid0 + i
                            dve.wait_ge(chunk_ready, n + 1)
                            if pr >= 2:
                                dve.wait_ge(hid_low, pr - 1)
                            dve.tensor_scalar(yt[:, pr % 4, :], ps[:, 0:T], 0.0, None, ALU.max).then_inc(free(n), 1)
                            dve.wait_ge(free(n), n // 2 + 1)
                            dve.tensor_tensor(hf2[:, pr % 2, :], yt[:, pr % 4, :], yt[:, pr % 4, :],
                                              ALU.mult).then_inc(hid_f, 1)
                            dve.wait_ge(hid_high, pr + 1)
                            dve.tensor_tensor(al[:, i, :], hf2[:, pr % 2, :], ah[:, i, :].bitcast(F32),
                                              ALU.subtract).then_inc(hid_low, 1)
                        elif g.kind == "mix":
                            m = g.mix0 + i
                            dve.wait_ge(chunk_ready, n + 1)
                            if g.arg == 0:
                                dve.tensor_tensor(mixed[:, i, :], ps[:, 0:T], sig[:, i, :], ALU.mult).then_inc(free(n), 1)
                            else:
                                dve.tensor_tensor(yt[:, m % 4, :], ps[:, 0:T], sig[:, i, :], ALU.mult).then_inc(free(n), 1)
                                dve.wait_ge(free(n), n // 2 + 1)
                                if g.arg == 2:
                                    dve.wait_ge(mix_f, m - 7)
                                dve.tensor_tensor(mixed[:, i, :], mixed[:, i, :], yt[:, m % 4, :],
                                                  ALU.add).then_inc(mix_f, 1)
                            if g.arg == 2:
                                dve.wait_ge(mix_f, m + 1)
                                dve.wait_ge(mix_high, 8 * (m // 16) + i + 1)
                                dve.tensor_tensor(yl[:, i, :], mixed[:, i, :], yh[:, i, :].bitcast(F32),
                                                  ALU.subtract).then_inc(mix_low, 1)
                        elif g.kind == "copy_y":
                            dve.wait_ge(chunk_ready, n + 1)
                            if g.arg == 0:
                                dve.tensor_copy(yb[:, i, :], ps[:, 0:T]).then_inc(free(n), 1)
                            else:
                                dve.tensor_tensor(yb[:, i, :], yb[:, i, :], ps[:, 0:T], ALU.add).then_inc(free(n), 1)
                        n += 1

            def attention(name):
                a = atts[name]
                pe_, pt_, dg_, st_ = a.bufs

                def row_max(j):
                    t, i = a.units[j]
                    u = a.u0 + j
                    k = a.tiles[t]["keys"]
                    s8 = u % 8
                    dve.wait_ge(s_ready, u + 1)
                    if u >= 8:
                        dve.wait_ge(p_used, u - 7)
                    chain(dve.tensor_reduce(st_[:, 2, s8:s8 + 1], aux[u % 2][:, 0:k], AX.X, ALU.max))
                    dve.tensor_scalar(st_[:, 0, s8:s8 + 1], st_[:, 2, s8:s8 + 1], -1.0, None, ALU.mult).then_inc(s_max, 1)

                def diagonal(j):
                    t, i = a.units[j]
                    u = a.u0 + j
                    s8 = u % 8
                    dve.wait_ge(p_ready, u + 1)
                    if u >= 2:
                        dve.wait_ge(p_used, u - 1)
                    chain(dve.reciprocal(st_[:, 3, s8:s8 + 1], st_[:, 1, s8:s8 + 1]))
                    co = a.tiles[t]["units"][i]["coef"]
                    if co is None:
                        dve.tensor_scalar(dg_[:, u % 2, :], ident, st_[:, 3, s8:s8 + 1], None,
                                          ALU.mult).then_inc(dg_ready, 1)
                    else:
                        dve.tensor_scalar(dg_[:, u % 2, :], ident, st_[:, 3, s8:s8 + 1], lamn[:, co:co + 1],
                                          ALU.mult, ALU.mult).then_inc(dg_ready, 1)

                def out_low(t):
                    tg = a.t0 + t
                    tile = a.tiles[t]
                    r0, r1 = tile["rows"]
                    dve.wait_ge(o_high, tg + 1)
                    if isinstance(tile["out"], tuple):
                        dve.tensor_tensor(tile["out"][1], aux[3][r0:r1, 0:P], tile["out"][0].bitcast(F32),
                                          ALU.subtract).then_inc(o_low, 1)
                    else:
                        dve.sem_inc(o_low, 1)

                def mask_bias(hd):
                    dve.wait_ge(tt_in[hd % 2], 32 * (hd // 2 + 1))
                    b = tt[:, hd % 2, :, :]
                    m = cst[:, C_MASK:C_MASK + 64]
                    for e in range(6):
                        ins = dve.tensor_tensor(tt[:, hd % 2, e, :], tt[:, hd % 2, e, :], m, ALU.add)
                    ins.then_inc(tt_masked, 1)

                n = len(a.units)
                if name == "nat":
                    mask_bias(0)
                    mask_bias(1)
                row_max(0)
                for j, (t, i) in enumerate(a.units):
                    if j + 1 < n:
                        row_max(j + 1)
                    diagonal(j)
                    if j and a.units[j - 1][0] != t and t >= 2:
                        out_low(t - 2)
                    if name == "nat" and j % 2 == 0 and j >= 2 and j // 2 + 1 < NH:
                        mask_bias(j // 2 + 1)
                out_low(len(a.tiles) - 2)
                out_low(len(a.tiles) - 1)

            dve.wait_ge(vec_turned, 3)
            for i, (v, w) in enumerate(((vecA, P), (vecB, NVB), (vecC, NVC))):
                dve.tensor_copy(v[:, :], aux[i][:, 0:w]).then_inc(vec_ready, 1)
            dve.wait_ge(small_in, 80)
            dve.wait_ge(t5_g, 1)
            dve.tensor_copy(gt5[:, :], aux[3][0:8, :]).then_inc(t5_row, 1)
            dve.wait_ge(cexp, 1)
            dve.tensor_scalar(lg[:, 2, :], lg[:, 1, :], 1.0, None, ALU.add).then_inc(cabs, 1)
            dve.wait_ge(cln, 1)
            chain(dve.tensor_scalar(lg[:, 2, :], lg[:, 2, :], -1.0, 1e-30, ALU.add, ALU.max))
            chain(dve.reciprocal(lg[:, 2, :], lg[:, 2, :]))
            chain(dve.tensor_tensor(lg[:, 2, :], lg[:, 2, :], lg[:, 1, :], ALU.mult))
            chain(dve.tensor_tensor(lg[:, 2, :], lg[:, 2, :], lg[:, 3, :], ALU.mult))
            chain(dve.tensor_scalar(lg[:, 0, :], dec[:, :], 0.0, None, ALU.min))
            chain(dve.tensor_tensor(lg[:, 4, :], lg[:, 0, :], lg[:, 2, :], ALU.subtract))
            dve.tensor_scalar(lg[:, 5, :], lg[:, 4, :], float(T), None, ALU.mult).then_inc(lg_ready, 3)
            for l in range(2):
                for k in range(2):
                    chain(dve.tensor_tensor(lamp[:, l, k, :], lamv[:, l, 2 * k, :], lamv[:, l, 2 * k + 1, :], ALU.mult))
            for l in range(2):
                for k in range(2):
                    ins = dve.tensor_reduce(lam[:, 2 * l + k:2 * l + k + 1], lamp[:, l, k, :], AX.X, ALU.add)
                    if l + k < 2:
                        chain(ins)
            ins.then_inc(lam_dots, 1)
            dve.wait_ge(lam_exp, 1)
            for l in range(2):
                chain(dve.tensor_tensor(lamn[:, l:l + 1], lam[:, 5 + 2 * l:6 + 2 * l], lam[:, 4 + 2 * l:5 + 2 * l],
                                        ALU.subtract))
                chain(dve.tensor_scalar(lamn[:, l:l + 1], lamn[:, l:l + 1], -LAM_INIT[l], None, ALU.add))
            for q in range(NMOD // 4):
                dve.wait_ge(mod_cols, 4 * q + 4)
                dve.tensor_copy(mod[:, 8 * q:8 * q + 8, :],
                                aux[q % 2][:, 0:16].rearrange("p (c v) -> p c v", v=2)).then_inc(mod_out, 1)
            dve.wait_ge(mod_out, NMOD // 4)
            for v in range(2):
                chain(dve.tensor_tensor(mod[:, 0:NMOD, v], mod[:, 0:NMOD, v], vecA[:, 0:NMOD], ALU.add))
                chain(dve.tensor_tensor(mod[:, NMOD:, v], mod[:, NMOD:, v], vecB[:, 0:NMOD], ALU.add))
            for i in range(6):
                m0 = NMOD * (i // 3) + 24 * (i % 3)
                for v in range(2):
                    chain(dve.scalar_tensor_tensor(out=nsc[:, i, :, v], in0=mod[:, m0 + 8:m0 + 16, v], scalar=1.0,
                                                   in1=vecA[:, VA["norm_g"] + 8 * i:VA["norm_g"] + 8 * i + 8],
                                                   op0=ALU.add, op1=ALU.mult))
                ins = dve.tensor_scalar(half[:, i, :, :], mod[:, m0 + 16:m0 + 24, :], 1.0 if i % 3 == 1 else 0.5, None,
                                        ALU.mult)
                if i < 5:
                    chain(ins)
            ins.then_inc(coef_ready, 1)

            def ffn(l, f, j):
                norm(f"n{l}{j}")
                for s in range(2):
                    gemm(f"in{l}{f}{s}")
                    gemm(f"out{l}{f}{s}")

            splits_upto(1)
            dve.wait_ge(rpb_out, 16)
            dve.wait_ge(t5_out, 16)
            ffn(0, 0, 0)
            norm("n01")
            for hh in range(RH):
                if hh == 0:
                    dve.wait_ge(ret_consts_in, 16)
                dve.tensor_scalar(dxb[:, 0:1], lg[:, 4, 4 + hh:5 + hh], -1.0, None, ALU.mult).then_inc(rd_x, 1)
                dve.wait_ge(rd_x, 4 * hh + 1)
                dve.tensor_scalar(dx[:, 0, :], cret[:, C_DB:C_DB + 384], lg[:, 4, 4 + hh:5 + hh], None,
                                  ALU.mult).then_inc(rd_x, 1)
                dve.wait_ge(rd_x, 4 * hh + 2)
                dve.scalar_tensor_tensor(out=dx[:, 0, :], in0=cret[:, C_DF:C_DF + 384], scalar=lg[:, 4, hh:hh + 1],
                                         in1=dx[:, 0, :], op0=ALU.mult, op1=ALU.add).then_inc(rd_x, 1)
                dve.wait_ge(rd_exp, 3 * hh + 3)
                dve.tensor_tensor(dx[:, 1, :], dx[:, 1, :], dx[:, 2, :], ALU.add).then_inc(rd_x, 1)
                gemm(f"ret_q{hh}")
                gemm(f"ret_k{hh}")
                wait_gemm_out(dve, f"ret_k{hh}")
                cos, sin = cret[:, C_COS:C_COS + T], cret[:, C_SIN:C_SIN + T]
                for k in range(2):
                    a_, b_ = qk[:, 2 * k, 0:T], qk[:, 2 * k + 1, 0:T]
                    chain(dve.tensor_tensor(hf[:, 0, 0:T], b_, sin, ALU.mult))
                    chain(dve.tensor_tensor(hf[:, 1, 0:T], a_, sin, ALU.mult))
                    chain(dve.tensor_tensor(qr[:, 2 * k, :], a_, cos, ALU.mult))
                    chain(dve.tensor_tensor(qr[:, 2 * k + 1, :], b_, cos, ALU.mult))
                    dve.tensor_tensor(qr[:, 2 * k, :], qr[:, 2 * k, :], hf[:, 0, 0:T], ALU.subtract).then_inc(r_rope, 1)
                    dve.tensor_tensor(qr[:, 2 * k + 1, :], qr[:, 2 * k + 1, :], hf[:, 1, 0:T], ALU.add).then_inc(r_rope, 1)
                    dve.wait_ge(r_rope, 4 * hh + 2 * k + 2)
                gemm(f"ret_v{hh}")
                dve.wait_ge(rd_x, 4 * hh + 4)
                for k, dd in ((0, 0), (1, 1), (2, 0)):
                    dve.wait_ge(r_score, 3 * hh + k + 1)
                    for jt in range(2):
                        ins = dve.tensor_tensor(att[:, 2 * k + jt, :], aux[k][:, T * jt:T * jt + T],
                                                dx[:, dd, P * (1 - jt):P * (1 - jt) + T], ALU.mult)
                    ins.then_inc(r_att, 1)
                gemm(f"ret_g{hh}")
                dve.wait_ge(r_mu, hh + 1)
                dve.wait_ge(r_of, 4 * hh + 4)
                for v in range(4):
                    dve.scalar_tensor_tensor(out=oc[:, v, :], in0=aux[0][:, :], scalar=-1.0 / 512, in1=oc[:, v, :],
                                             op0=ALU.mult, op1=ALU.add).then_inc(r_cen, 1)
                dve.wait_ge(r_std, hh + 1)
                chain(dve.reciprocal(rstd[:, :], std[:, :]))
                for v in range(4):
                    g0 = VB["gn_g"] + 4 * hh + v
                    chain(dve.scalar_tensor_tensor(out=oc[:, v, :], in0=oc[:, v, :], scalar=vecB[:, g0:g0 + 1],
                                                   in1=rstd[:, :], op0=ALU.mult, op1=ALU.mult))
                    dve.tensor_tensor(oc[:, v, :], oc[:, v, :], gr[:, v, :], ALU.mult).then_inc(r_gat, 1)
                for v in range(4):
                    dve.wait_ge(r_high, 4 * hh + v + 1)
                    dve.tensor_tensor(ol[:, v, :], oc[:, v, :], oh[:, v, :].bitcast(F32), ALU.subtract).then_inc(r_low, 1)
                gemm(f"ret_out{hh}")
            ffn(0, 1, 2)
            ffn(1, 0, 0)
            norm("n11")
            gemm("nat_q")
            gemm("nat_k")
            gemm("nat_v")
            attention("nat")
            gemm("nat_o")
            ffn(1, 1, 2)
            norm("final")
            R = slice(64, 96)
            dve.wait_ge(h_update, 8)
            dve.wait_ge(pos_in, 16)
            chain(dve.tensor_copy(ang[R, 0, :], po[R, :]))
            chain(dve.tensor_scalar(ang[R, 0, :], ang[R, 0, :], cst[R, C_INV:C_INV + 1], None, ALU.mult))
            chain(dve.tensor_scalar(ang[R, 1, :], ang[R, 0, :], float(1 / (2 * np.pi)), 12582912.0, ALU.mult, ALU.add))
            chain(dve.tensor_scalar(ang[R, 1, :], ang[R, 1, :], -12582912.0, None, ALU.add))
            for part in LOG2PI:
                chain(dve.scalar_tensor_tensor(out=ang[R, 0, :], in0=ang[R, 1, :], scalar=-float(part), in1=ang[R, 0, :],
                                               op0=ALU.mult, op1=ALU.add))
            dve.tensor_scalar(ang[R, 0, :], ang[R, 0, :], 3.1415925, -3.1415925, ALU.min, ALU.max).then_inc(ang_r, 1)
            dve.wait_ge(sin_ready, 2)
            chain(dve.tensor_tensor(ang[R, 2, :], ang[R, 2, :], ang[R, 2, :], ALU.mult))
            chain(dve.tensor_scalar(ang[R, 2, :], ang[R, 2, :], -2.0, 1.0, ALU.mult, ALU.add))
            dve.wait_ge(t5_in, 128)
            for l in range(2):
                norm(f"mix_pre{l}")
                for k in "qkv":
                    gemm(f"diff_{k}{l}")
                attention(f"diff{l}")
                for hd in range(DH):
                    i = DH * l + hd
                    dve.wait_ge(sub_std, i + 1)
                    chain(dve.reciprocal(rstd[:, 0:T], std[:, 0:T]))
                    dve.scalar_tensor_tensor(out=oraw[:, hd, :], in0=oraw[:, hd, :],
                                             scalar=vecC[:, VC["subln"] + l:VC["subln"] + l + 1],
                                             in1=rstd[:, 0:T], op0=ALU.mult, op1=ALU.mult).then_inc(sub_t, 1)
                    dve.wait_ge(sub_high, i + 1)
                    dve.scalar_tensor_tensor(out=al[:, hd, :], in0=oraw[:, hd, :], scalar=1.0 - LAM_INIT[l],
                                             in1=ah[:, hd, :].bitcast(F32), op0=ALU.mult,
                                             op1=ALU.subtract).then_inc(sub_low, 1)
                for k in "qkv":
                    gemm(f"moba_{k}{l}")
                attention(f"moba{l}")
                gemm(f"mla_cq{l}")
                gemm(f"mla_ckv{l}")
                norm(f"cq{l}")
                norm(f"ckv{l}")
                gemm(f"mla_uq{l}")
                gemm(f"mla_ukv{l}")
                wait_gemm_out(dve, f"mla_ukv{l}")
                for k in range(MH + 1):
                    i = (MH + 1) * l + k
                    x = mq[R, k, :] if k < MH else kpe[R, :]
                    dve.wait_ge(rot_x, i + 1)
                    chain(dve.tensor_tensor(ang[R, 3, :], aux[i % 2][R, 0:T], ang[R, 1, :], ALU.mult))
                    chain(dve.tensor_tensor(x, x, ang[R, 2, :], ALU.mult))
                    if k < MH:
                        dve.tensor_tensor(x, x, ang[R, 3, :], ALU.add).then_inc(roped, 1)
                        dve.wait_ge(roped, (2 * MH) * l + k + 1)
                    else:
                        chain(dve.tensor_tensor(x, x, ang[R, 3, :], ALU.add))
                        for hd in range(MH):
                            dve.tensor_copy(mk[R, hd, :], kpe[R, :]).then_inc(roped, 1)
                attention(f"mla{l}")
                for g in range(3):
                    gemm(f"gate{g}{l}")
                    gemm(f"branch{g}{l}")
                gemm(f"mixed{l}")
                norm(f"mix_post{l}")
                norm(f"mlp_pre{l}")
                for s in range(4):
                    gemm(f"up{l}{s}")
                    gemm(f"down{l}{s}")
                norm(f"mlp_post{l}")
            for t in range(2):
                for k in range(4):
                    dve.wait_ge(out_turned, 4 * t + k + 1)
                    dve.tensor_copy(out_buf[t][:, T * k:T * k + T], aux[k][:, 0:T]).then_inc(out_rows, 1)

        @block.tensor
        def _(pe):
            def norm(name):
                N = norms[name]
                s_q = N["buf"][3]
                tok = N["tok"]
                for c in range(N["nc"]):
                    i = N["sq0"] + c
                    pe.wait_ge(sq_ready, i + 1)
                    if c == 0 and N["u"]:
                        pe.wait_ge(std_ready, N["u"])
                    ins = pe.matmul(aux[3][:, 0:tok], ones[:, :], s_q[:, i % 2, 0:tok], start=c == 0,
                                    stop=c == N["nc"] - 1)
                    ins.then_inc(sq_used, 1)

            def gemm(name, x_waits=None):
                g = G[name]
                n, s = g.n0, g.s0
                t0, t1 = g.tok
                seen = set()
                for bl, ch in g.groups:
                    for bi, (_, k0, nk, w) in enumerate(bl):
                        pe.wait_ge(w_low, s + 1)
                        H, L_ = wh[s % SPL], wl[s % SPL]
                        for ci, (o, a0, a1) in enumerate(ch):
                            m = n + ci
                            ps = bank[m % 4]
                            if bi == 0 and m >= 4:
                                wait_chunk_out(pe, m - 4)
                            for k in range(nk):
                                kc = k0 + k
                                if x_waits and kc not in seen:
                                    x_waits(kc)
                                    seen.add(kc)
                                first, last = bi == 0 and k == 0, bi == len(bl) - 1 and k == nk - 1
                                xhi, xlo = g.x[0](kc), g.x[1](kc)
                                if o == "A":
                                    c0 = k * w + a0
                                    hi, lo = H[:, c0:c0 + a1], L_[:, c0:c0 + a1]
                                    out = ps[0:a1, 0:t1 - t0]
                                    trio = ((hi, xhi[:, t0:t1]), (hi, xlo[:, t0:t1]), (lo, xhi[:, t0:t1]))
                                else:
                                    hi, lo = a1(H[:, k * w:k * w + w]), a1(L_[:, k * w:k * w + w])
                                    nn = w if w == WB else 512
                                    out = ps[:, 0:nn]
                                    q0 = P * a0
                                    trio = ((xhi[:, q0:q0 + P], hi), (xhi[:, q0:q0 + P], lo), (xlo[:, q0:q0 + P], hi))
                                for j, (l_, r_) in enumerate(trio):
                                    ins = pe.matmul(out, l_, r_, start=first and j == 0, stop=last and j == 2)
                            if bi == len(bl) - 1:
                                ins.then_inc(chunk_ready, 1)
                        if bi < len(bl) - 1:
                            ins.then_inc(block_used, 1)
                        s += 1
                    n += len(ch)

            def normed(name):
                N = norms[name]
                per = N["tok"] // T
                return lambda kc: pe.wait_ge(x_low, N["p0"] + per * (kc + 1))

            def attention(name):
                a = atts[name]
                pe_, pt_, dg_, st_ = a.bufs
                rev, rev64 = cst[:, C_REV:C_REV + P], cst[:, C_REV64:C_REV64 + P]
                order_of = {"nat": rev64, "dif": rev, "mob": rev, "mla": ident}

                def scores(j):
                    t, i = a.units[j]
                    u = a.u0 + j
                    tile = a.tiles[t]
                    un = tile["units"][i]
                    if u >= 2:
                        pe.wait_ge(p_ready, u - 1)
                    if name == "nat" and i == 0:
                        pe.wait_ge(tt_masked, tile["head"] + 1)
                    k = tile["keys"]
                    b0, b1, bias = un["bias"]
                    pe.matmul(aux[u % 2][:, 0:k], un["qk"][0], un["qk"][1], start=True, stop=True,
                              skip_group_check=True)
                    pe.matmul(aux[u % 2][:, b0:b1], order_of[name[:3]], bias, start=False, stop=True,
                              skip_group_check=True).then_inc(s_ready, 1)

                def turn(j):
                    t, i = a.units[j]
                    u = a.u0 + j
                    tile = a.tiles[t]
                    nu = len(tile["units"])
                    pe.wait_ge(dg_ready, u + 1)
                    if i == nu - 1:
                        if a.t0 + t >= 1:
                            pe.wait_ge(pt_out, a.t0 + t)
                        for kt in range(tile["keys"] // P):
                            for q in range(nu):
                                uq = u - nu + 1 + q
                                ins = pe.matmul(aux[2][:, P * kt:P * kt + P], pe_[:, uq % 2, P * kt:P * kt + P],
                                                dg_[:, uq % 2, :], start=q == 0, stop=q == nu - 1)
                        ins.then_inc(p_used, nu)

                def values(t):
                    tg = a.t0 + t
                    tile = a.tiles[t]
                    r0, r1 = tile["rows"]
                    pe.wait_ge(pt_out, tg + 1)
                    if tg >= 1:
                        pe.wait_ge(o_low, tg)
                        pe.wait_ge(o_high, tg)
                    nkt = tile["keys"] // P
                    for kt in range(nkt):
                        ins = pe.matmul(aux[3][r0:r1, 0:P], tile["v"](kt), pt_[:, tg % 2, P * kt:P * kt + P],
                                        start=kt == 0, stop=kt == nkt - 1)
                    ins.then_inc(o_ready, 1)

                n = len(a.units)
                scores(0)
                for j, (t, i) in enumerate(a.units):
                    nu = len(a.tiles[t]["units"])
                    if j + 1 < n:
                        scores(j + 1)
                    turn(j)
                    if i == nu - 1 and t >= 1:
                        values(t - 1)
                values(len(a.tiles) - 1)

            pe.wait_ge(consts_in, 16)
            pe.wait_ge(rows_in, 16 * 14)
            for i, w in enumerate((P, NVB, NVC)):
                pe.transpose(aux[i][:, 0:w], vrows[0:w, i, :], ident[0:w, 0:w]).then_inc(vec_turned, 1)
            pe.wait_ge(pool_ready, 5)
            pe.wait_ge(small_in, 80)
            pe.matmul(aux[3][0:8, :], tab[:, :], hot[:, :], start=True, stop=True).then_inc(t5_g, 1)
            pe.wait_ge(x_in, 64)
            for c in range(DC):
                if c < 3:
                    pe.wait_ge(vec_ready, c + 1)
                elif c == 3:
                    pe.wait_ge(t5_row, 1)
                else:
                    pe.wait_ge(h_init, c - 3)
                for t in range(4):
                    ins = pe.transpose(aux[c % 4][:, P * t:P * t + P], xrows[:, t, P * c:P * c + P], ident)
                ins.then_inc(x_turned, 1)
            pe.wait_ge(h_init, 8)
            pe.wait_ge(c_silu, 2)

            def mod_turn(b):
                q = b // 4
                if b % 4 == 0 and q >= 2:
                    pe.wait_ge(mod_out, q - 1)
                pe.wait_ge(mod_row, b + 1)
                for j in range(2):
                    o = 4 * (b % 4) + 2 * j
                    ins = pe.matmul(aux[q % 2][:, o:o + 2], mrow[:, b % 4, P * j:P * j + P], ident[0:2, 0:2],
                                    start=True, stop=True)
                ins.then_inc(mod_cols, 1)

            for b in range(NMOD):
                pe.wait_ge(raw_in[b % RAW], raw_value[b])
                if b >= 4:
                    pe.wait_ge(mod_row, b - 3)
                for k in range(DC):
                    ins = pe.matmul(bank[b % 4][0:2, 0:WB], sc[:, k, :], raw[b % RAW][:, WB * k:WB * k + WB],
                                    start=k == 0, stop=k == DC - 1)
                ins.then_inc(chunk_mod, 1)
                if b:
                    mod_turn(b - 1)
            mod_turn(NMOD - 1)
            pe.wait_ge(mod_row, NMOD)

            def ffn(l, f, j):
                norm(f"n{l}{j}")
                for s in range(2):
                    gemm(f"in{l}{f}{s}", normed(f"n{l}{j}"))
                    base = G[f"in{l}{f}{s}"].hid0
                    gemm(f"out{l}{f}{s}", lambda kc: pe.wait_ge(hid_low, base + kc - s * FH + 1))

            pe.wait_ge(coef_ready, 1)
            ffn(0, 0, 0)
            norm("n01")
            for hh in range(RH):
                gemm(f"ret_q{hh}", normed("n01"))
                gemm(f"ret_k{hh}")
                gemm(f"ret_v{hh}")
                pe.wait_ge(r_rope, 4 * hh + 4)
                wait_gemm_out(pe, f"ret_k{hh}")
                for k in range(3):
                    if k == 0 and hh:
                        pe.wait_ge(r_cen, 4 * hh)
                    if k == 1 and hh:
                        pe.wait_ge(r_std, hh)
                    for jt in range(2):
                        for d in range(2):
                            kk = qr[:, 2 + d, P * jt:P * jt + P] if k == 0 else qk[:, 2 + d, T + P * jt:T + P * jt + P]
                            qq = qk[:, d, T:T2] if k == 2 else qr[:, d, :]
                            ins = pe.matmul(aux[k][:, T * jt:T * jt + T], kk, qq, start=d == 0, stop=d == 1)
                    ins.then_inc(r_score, 1)
                gemm(f"ret_g{hh}")
                pe.wait_ge(r_att, 3 * hh + 3)
                wait_gemm_out(pe, f"ret_v{hh}")
                for v in range(4):
                    ps = aux[(v + 3) % 4]
                    for q in range(2):
                        js = ((0, 0), (1, 1), (2, 2), (3, 3)) if q == 0 else ((2, 4), (3, 5))
                        for x, (vt, at) in enumerate(js):
                            ins = pe.matmul(ps[:, T * q:T * q + T], vr[:, vt, P * v:P * v + P], att[:, at, :],
                                            start=x == 0, stop=x == len(js) - 1)
                    ins.then_inc(r_o, 1)
                for v in range(4):
                    pe.wait_ge(r_of, 4 * hh + (v + 1 if v else 2))
                    ins = pe.matmul(aux[0][:, :], ones[:, :], oc[:, v, :], start=v == 0, stop=v == 3)
                ins.then_inc(r_mu, 1)
                for v in range(4):
                    pe.wait_ge(r_sq, 4 * hh + v + 1)
                    ins = pe.matmul(aux[1][:, :], ones[:, :], sa[:, v % 2, :], start=v == 0, stop=v == 3)
                    ins.then_inc(r_sqf, 1)
                gemm(f"ret_out{hh}", lambda kc: pe.wait_ge(r_low, kc + 1))
            ffn(0, 1, 2)
            ffn(1, 0, 0)
            norm("n11")
            gemm("nat_q", normed("n11"))
            gemm("nat_k")
            gemm("nat_v")
            wait_gemm_out(pe, "nat_v")
            attention("nat")
            pe.wait_ge(o_low, atts["nat"].t1)
            gemm("nat_o")
            ffn(1, 1, 2)
            norm("final")
            for l in range(2):
                norm(f"mix_pre{l}")
                gemm(f"diff_q{l}", normed(f"mix_pre{l}"))
                gemm(f"diff_k{l}")
                gemm(f"diff_v{l}")
                wait_gemm_out(pe, f"diff_v{l}")
                pe.wait_ge(t5_in, 128)
                attention(f"diff{l}")
                for hd in range(DH):
                    i = DH * l + hd
                    pe.wait_ge(sub_sq, i + 1)
                    pe.wait_ge(o_high, atts[f"diff{l}"].t1)
                    if i % DH:
                        pe.wait_ge(sub_std, i)
                    pe.matmul(aux[3][:, 0:T], ones[:, :], sq2[:, 0, :], start=True, stop=True).then_inc(sub_ms, 1)
                for k in "qkv":
                    gemm(f"moba_{k}{l}")
                wait_gemm_out(pe, f"moba_v{l}")
                pe.wait_ge(sub_std, DH * l + DH)
                attention(f"moba{l}")
                gemm(f"mla_cq{l}")
                gemm(f"mla_ckv{l}")
                pe.wait_ge(o_low, atts[f"moba{l}"].t1)
                norm(f"cq{l}")
                norm(f"ckv{l}")
                gemm(f"mla_uq{l}", normed(f"cq{l}"))
                gemm(f"mla_ukv{l}", normed(f"ckv{l}"))
                wait_gemm_out(pe, f"mla_uq{l}")
                for k in range(MH + 1):
                    i = (MH + 1) * l + k
                    if k >= 2:
                        pe.wait_ge(roped, 2 * MH * l + k - 1)
                    x = mq[64:96, k, :] if k < MH else kpe[64:96, :]
                    pe.matmul(aux[i % 2][64:96, 0:T], cst[64:96, C_ROT:C_ROT + 32], x, start=True,
                              stop=True).then_inc(rot_x, 1)
                wait_gemm_out(pe, f"mla_ukv{l}")
                pe.wait_ge(roped, 2 * MH * (l + 1))
                attention(f"mla{l}")
                pe.wait_ge(o_low, atts[f"mla{l}"].t1)
                pe.wait_ge(sub_low, DH * (l + 1))
                for g in range(3):
                    gemm(f"gate{g}{l}")
                    gemm(f"branch{g}{l}")
                gemm(f"mixed{l}", lambda kc: pe.wait_ge(mix_low, 8 * l + kc + 1))
                norm(f"mix_post{l}")
                norm(f"mlp_pre{l}")
                for s in range(4):
                    gemm(f"up{l}{s}", normed(f"mlp_pre{l}"))
                    base = G[f"up{l}{s}"].hid0
                    gemm(f"down{l}{s}", lambda kc: pe.wait_ge(hid_low, base + kc - s * DC + 1))
                norm(f"mlp_post{l}")
            pe.wait_ge(h_update, 8 + 32)
            for t in range(2):
                for k in range(4):
                    if t:
                        pe.wait_ge(out_rows, k + 1)
                    for c in range(2):
                        ins = pe.transpose(aux[k][:, P * c:P * c + P], h[:, 2 * k + c, P * t:P * t + P], ident)
                    ins.then_inc(out_turned, 1)


NAMES = ["x", "c", "ctx", "c_ctx", "w_mod", "b_mod", "norm_g", "ffn_w_in", "ffn_w_out", "ret_w_in", "ret_w_out",
         "ret_gn_g", "ret_decay_f", "ret_decay_b", "nat_w_qkv", "nat_w_o", "nat_rpb", "final_norm_g", "positions_2",
         "rel_bias_2", "norm_mix_pre_2", "norm_mix_post_2", "norm_mlp_pre_2", "norm_mlp_post_2", "w_in_2",
         "diff_lambda_2", "diff_subln_2", "mla_q_norm_2", "mla_w_uq_2", "mla_kv_norm_2", "mla_w_ukv_2", "w_branch_2",
         "w_out_2", "w_up_2", "w_down_2"]


def kernel(**inputs):
    import concourse.bacc as bacc
    from concourse.bass_utils import run_bass_kernel_spmd

    nc = bacc.Bacc("TRN2", target_bir_lowering=False, num_devices=1)
    arrays, aps = {}, {}
    small, ret = shape_constants()
    for name, a in [(n, np.ascontiguousarray(inputs[n])) for n in NAMES] + [("consts", small), ("ret_consts", ret)]:
        arrays[f"in_{name}"] = a
        aps[name] = nc.dram_tensor(f"in_{name}", a.shape, mybir.dt.from_np(a.dtype), kind="ExternalInput").ap()
    aps["out"] = nc.dram_tensor("out_0", (1, T, D), F32, kind="ExternalOutput").ap()
    program(nc, aps)
    r = run_bass_kernel_spmd(nc, [arrays], core_ids=[0])
    return r.results[0]["out_0"]
```

```python
from contextlib import ExitStack

import numpy as np
import concourse.bass as bass
from concourse import mybir

F32 = mybir.dt.float32
F32R = mybir.dt.float32r
I32 = mybir.dt.int32
ALU = mybir.AluOpType
ACT = mybir.ActivationFunctionType
AX = mybir.AxisListType

P = 128
D = 1024
DC = D // P
T = 256
T2 = 2 * T
EPS = 1e-6
NEG = -1e30
FFN = 2816
FC = FFN // P
FH = FC // 2
WB = 256
BLK = DC * WB
RAW = 4
SPL = 2
RH, NH, DH, MH = 4, 16, 4, 8
NMOD = 72
MOD0 = 12
LOG2PI = (6.28125, 0.0019350051879882812, 2.0 * np.pi - 6.28125 - 0.0019350051879882812)
LAM_INIT = [0.8 - 0.6 * float(np.exp(-0.3 * l)) for l in range(2)]

C_ID, C_MASK, C_CAUSAL, C_INV, C_ROT, C_REV, C_REV64, C_HOT = 0, 128, 192, 320, 321, 353, 481, 609
C_SMALL = 609 + 512
C_COS, C_SIN, C_DF, C_DB, C_DIFF = 0, 256, 512, 896, 1280
C_RET = 1664


def shape_constants():
    p = np.arange(P)[:, None]
    small = np.zeros((P, C_SMALL), np.float32)
    small[:, C_ID:C_ID + P] = np.eye(P)
    small[:, C_REV:C_REV + P] = np.eye(P)[::-1]
    small[:, C_REV64:C_REV64 + P] = np.kron(np.eye(2), np.eye(64)[::-1])
    col, key = 63 - p % 64, np.arange(64)[None]
    lo = np.clip(col - 8, 0, 48)
    small[:, C_MASK:C_MASK + 64] = np.where((key >= lo) & (key < lo + 16), 0.0, NEG)
    small[:, C_CAUSAL:C_CAUSAL + P] = np.where(np.arange(P)[None] <= p, 0.0, NEG)
    inv = np.float32(10000.0) ** (-np.arange(16, dtype=np.float32) * np.float32(2.0) / np.float32(32))
    small[64:80, C_INV] = inv
    small[80:96, C_INV] = inv
    for i in range(16):
        small[64 + i + 16, C_ROT + i] = -1.0
        small[64 + i, C_ROT + i + 16] = 1.0
    rel = 255 - np.arange(512)
    n = np.maximum(rel, 0)
    nf = np.maximum(n, 1).astype(np.float32)
    large = 16 + (np.log(nf / np.float32(16)) / np.float32(np.log(64.0)) * np.float32(16)).astype(np.int32)
    bucket = np.where(n < 16, n, np.minimum(large, 31))
    for x in range(512):
        if rel[x] >= 0:
            small[bucket[x], C_HOT + x] = 1.0
        else:
            small[32, C_HOT + x] = NEG
    ret = np.zeros((P, C_RET), np.float32)
    invr = np.float32(10000.0) ** (-np.arange(0, 256, 2, dtype=np.float32) / np.float32(256))
    ang = invr[:, None] * np.arange(T, dtype=np.float32)[None]
    ret[:, C_COS:C_COS + T] = np.cos(ang)
    ret[:, C_SIN:C_SIN + T] = np.sin(ang)
    diff = np.arange(384)[None] - 128 - p
    ret[:, C_DF:C_DF + 384] = np.maximum(diff, 0)
    ret[:, C_DB:C_DB + 384] = np.maximum(-diff, 0)
    ret[:, C_DIFF:C_DIFF + 384] = diff
    return small, ret


VA = {"b_mod0": 0, "norm_g": 72, "final": 120}
VB = {"b_mod1": 0, "gn_g": 72, "c": 88, "c_ctx": 96}
VC = {"mix_pre": 0, "mix_post": 16, "mlp_pre": 32, "mlp_post": 48, "q_norm": 64, "kv_norm": 68, "subln": 70}
NVB, NVC = 104, 72


class Gemm:

    def __init__(self, name, kind, groups, x, tok, dst=None, arg=None):
        self.name, self.kind, self.groups, self.x, self.tok = name, kind, groups, x, tok
        self.dst, self.arg = dst, arg
        self.per_group = len(groups[0][1])


def program(nc, A):
    ctx = ExitStack()
    with ctx:
        def sem(name):
            return ctx.enter_context(nc.semaphore(name))

        def keep(name, shape, dt=F32):
            return ctx.enter_context(nc.sbuf_tensor(name, shape, dt))

        raw = [keep(f"raw{i}", [P, BLK]) for i in range(RAW)]
        wh = [keep(f"w_high{i}", [P, BLK], F32R) for i in range(SPL)]
        wl = [keep(f"w_low{i}", [P, BLK], F32R) for i in range(SPL)]
        h = keep("h", [P, DC, T2])
        cst = keep("cst", [P, C_HOT])
        ones = keep("ones", [P, P])
        vecA = keep("vecA", [P, P])
        vecB = keep("vecB", [P, NVB])
        vecC = keep("vecC", [P, NVC])
        mod = keep("mod", [P, 2 * NMOD, 2])
        nsc = keep("nsc", [P, 6, DC, 2])
        half = keep("half", [P, 6, DC, 2])
        zero = keep("zero", [P, 1])
        eps = keep("eps", [P, 1])
        sc = keep("sc", [P, DC, 2])
        dec = keep("dec", [P, 8])
        lg = keep("lg", [P, 6, 8])
        lam = keep("lam", [P, 8])
        lamn = keep("lam_negated", [P, 2])
        dxb = keep("decay_negated", [P, 1])
        std = keep("std", [P, T2])
        rstd = keep("rstd", [P, T2])
        ident = cst[:, C_ID:C_ID + P]

        def first_named(tensors, prefix):
            return [(prefix + n, sh, dt) for n, sh, dt in tensors]

        def scope(tensors):
            with ExitStack() as s:
                return [s.enter_context(nc.sbuf_tensor(n, sh, dt)) for n, sh, dt in tensors]

        first = [("xh", [P, DC, T2], F32R), ("xl", [P, DC, T2], F32R), ("xt", [P, 4, T], F32),
                 ("sq", [P, 2, T2], F32), ("hf", [P, 2, T2], F32),
                 ("macc", [P, 2, 2, WB], F32)]
        xh, xl, xt, sq, hf, macc, hidh, hidl, mprod = scope(
            first + [("hid_high", [P, FH, T2], F32R), ("hid_low", [P, FH, T2], F32R), ("mprod", [P, 2, WB], F32)])
        sa = sq
        xrows = scope(first_named(first, "i_") + [("pad0", [P, 11 * T2], F32), ("xrows", [P, 4, D], F32), ("vrows", [P, 3, P], F32),
                               ("lamv", [P, 2, 4, 64], F32), ("lamp", [P, 2, 2, 64], F32), ("rpbp", [112, 127], F32),
                               ("gt5", [8, 512], F32), ("tab", [33, 8], F32),
                               ("hot", [33, 512], F32), ("mrow", [2, 4, WB], F32)])[7:]
        xrows, vrows, lamv, lamp, rpbp, gt5, tab, hot, mrow = xrows
        oh, ol, cret, qk, qr, vr, gr, att, oc, dx = scope(first_named(first, "r_") + [
            ("ret_high", [P, 4, T2], F32R), ("ret_low", [P, 4, T2], F32R), ("cret", [P, C_RET], F32),
            ("qk", [P, 4, T2], F32), ("qr", [P, 4, T], F32), ("vr", [P, 4, T2], F32), ("gr", [P, 4, T2], F32),
            ("att", [P, 6, T], F32), ("oc", [P, 4, T2], F32), ("dx", [P, 3, 384], F32)])[6:]
        att_bufs = [("pexp", [P, 2, 512], F32), ("ptr", [P, 2, 512], F32), ("dg", [P, 2, P], F32),
                    ("stat", [P, 4, 8], F32)]
        nah, nal, nq, nk, nv, tt, pexp, ptr, dg, stat = scope(first_named(first, "n_") + [
            ("nat_high", [P, DC, T], F32R), ("nat_low", [P, DC, T], F32R), ("nq", [P, DC, T], F32),
            ("nk", [P, DC, T2], F32), ("nv", [P, 4, D], F32), ("tt", [P, 2, 6, 64], F32)] + att_bufs)[6:]
        (yh, yl, yt, sq2, hf2, ah, al, sig, v2, v3, cqh, cql, ckh, ckl, mq, mk, mv, t5, ang, po, oraw,
         pexp2, ptr2, dg2, stat2) = scope([
             ("yh", [P, DC, T], F32R), ("yl", [P, DC, T], F32R), ("yt", [P, 4, T], F32), ("sq2", [P, 2, T], F32),
             ("hf2", [P, 2, T], F32), ("act_high", [P, 12, T], F32R), ("act_low", [P, 12, T], F32R),
             ("diff_qk_gate", [P, DC, T], F32), ("v2", [P, 2, 512], F32), ("v3", [P, 2, 512], F32),
             ("cq_high", [P, 2, T], F32R), ("cq_low", [P, 2, T], F32R), ("ckv_high", [P, 1, T], F32R),
             ("ckv_low", [P, 1, T], F32R), ("mq", [P, MH, T], F32), ("mk", [P, MH, T], F32),
             ("mv", [P, 2, 512], F32), ("t5", [P, 8, 384], F32), ("ang", [P, 4, T], F32), ("posi", [P, T], I32),
             ("oraw", [P, 4, T], F32)]
             + [(n + "2", [s[0], s[1], min(s[2], T)], d) for n, s, d in att_bufs])
        q2, k2 = sig[:, 0:4, :], sig[:, 4:8, :]
        mixed = h[:, :, T:T2]
        q3, k3 = mixed[:, 0:4, :], mixed[:, 4:8, :]
        cq, ckv, kpe = mk[:, 0:2, :], mk[:, 2, :], mk[:, 7, :]
        rows_of = t5[:, :, :].rearrange("p a b -> p (a b)")
        out_buf = [rows_of[:, D * t:D * t + D] for t in range(2)]
        yb = mixed

        bank = [ctx.enter_context(nc.psum_tensor(f"gemm{i}", [P, 512], F32)) for i in range(4)]
        aux = [ctx.enter_context(nc.psum_tensor(f"aux{i}", [P, 512], F32)) for i in range(4)]

        rpb_dram = nc.dram_tensor("rpb_padded", [112, 127], F32)
        t5_dram = nc.dram_tensor("t5_by_distance", [8, 512], F32)

        def kview(w, k0, nk, c0, n):
            return w[k0 * P:(k0 + nk) * P, c0:c0 + n].rearrange("(k p) n -> p k n", p=P)

        def A_groups(w, cols, kbs=((0, DC),), c00=0):
            return [([(kview(w, k0, nk, c00 + c, WB), k0, nk, WB) for k0, nk in kbs],
                     [("A", 0, P), ("A", P, P)]) for c in range(0, cols, WB)]

        def B_groups(w, cols, tiles, c00=0):
            return [([(kview(w, 0, DC, c00 + c, WB), 0, DC, WB)],
                     [("B", t, lambda ap: ap) for t in range(tiles)]) for c in range(0, cols, WB)]

        gemms = []

        def add(*a, **k):
            gemms.append(Gemm(*a, **k))

        X = (lambda c: xh[:, c, :], lambda c: xl[:, c, :])
        Hd = (lambda c: hidh[:, c, :], lambda c: hidl[:, c, :])

        def ffn(l, f, tok, j):
            w_in, w_out = A["ffn_w_in"][l, f], A["ffn_w_out"][l, f]
            for s in range(2):
                groups = []
                for g in range(FH):
                    c0 = (s * FH + g) * P
                    ap = w_in[:, :].rearrange("(k p) (s n) -> p k s n", p=P, s=2)[:, :, :, c0:c0 + P]
                    groups.append(([(ap, 0, DC, WB)], [("A", 0, P), ("A", P, P)]))
                add(f"in{l}{f}{s}", "swiglu", groups, X, tok)
                add(f"out{l}{f}{s}", "resid", A_groups(w_out, D, ((s * FH, 6), (s * FH + 6, 5))),
                    (lambda c, s=s: hidh[:, c - s * FH, :], lambda c, s=s: hidl[:, c - s * FH, :]), tok, arg=3 * l + j)

        ffn(0, 0, (0, T2), 0)
        wr = A["ret_w_in"][0]
        Rt = (lambda c: oh[:, c % 4, :], lambda c: ol[:, c % 4, :])

        def ret_out(hh):
            add(f"ret_out{hh}", "resid", A_groups(A["ret_w_out"][0], D, ((4 * hh, 4),)), Rt, (0, T2), arg=1)

        for hh in range(RH):
            add(f"ret_q{hh}", "scaled", A_groups(wr, 256, c00=256 * hh), X, (0, T2),
                dst=lambda i: qk[:, i, :], arg=1.0)
            add(f"ret_k{hh}", "scaled", A_groups(wr, 256, c00=1024 + 256 * hh), X, (0, T2),
                dst=lambda i: qk[:, 2 + i, :], arg=1.0 / 16)
            add(f"ret_v{hh}", "scaled", B_groups(wr, 512, 4, c00=2048 + 512 * hh), X, (0, T2),
                dst=lambda i: vr[:, i % 4, (i // 4) * WB:(i // 4 + 1) * WB], arg=1.0)
            if hh:
                ret_out(hh - 1)
            add(f"ret_g{hh}", "silu", A_groups(wr, 512, c00=4096 + 512 * hh), X, (0, T2),
                dst=lambda i: gr[:, i, :])
        ret_out(RH - 1)
        ffn(0, 1, (0, T2), 2)
        ffn(1, 0, (0, T2), 0)
        wn = A["nat_w_qkv"][0]
        for g in range(4):
            add(f"nat_q{g}", "scaled", A_groups(wn, WB, c00=WB * g), X, (0, T),
                dst=lambda i, g=g: nq[:, 2 * g + i, :], arg=0.125)
            add(f"nat_k{g}", "scaled", A_groups(wn, WB, c00=D + WB * g), X, (0, T2),
                dst=lambda i, g=g: nk[:, 2 * g + i, :], arg=1.0)
            add(f"nat_v{g}", "scaled", B_groups(wn, WB, 4, c00=2 * D + WB * g), X, (0, T2),
                dst=lambda i, g=g: nv[:, i, WB * g:WB * g + WB], arg=1.0)
        add("nat_o", "resid", A_groups(A["nat_w_o"][0], D), (lambda c: nah[:, c, :], lambda c: nal[:, c, :]),
            (0, T), arg=4)
        ffn(1, 1, (0, T), 2)
        Y = (lambda c: yh[:, c, :], lambda c: yl[:, c, :])
        L = (0, T)
        for l in range(2):
            w = A["w_in_2"][l]
            for a, (name, s, qb, kb_, vb) in enumerate((("diff", 0.125, q2, k2, v2),
                                                        ("moba", float(128 ** -0.5), q3, k3, v3))):
                o = 1536 * a
                add(f"{name}_q{l}", "scaled", A_groups(w, 512, c00=o), Y, L, dst=lambda i, b=qb: b[:, i, :], arg=s)
                add(f"{name}_k{l}", "scaled", A_groups(w, 512, c00=o + 512), Y, L, dst=lambda i, b=kb_: b[:, i, :], arg=1.0)
                add(f"{name}_v{l}", "scaled", B_groups(w, 512, 2, c00=o + 1024), Y, L,
                    dst=lambda i, b=vb: b[:, i % 2, (i // 2) * WB:(i // 2 + 1) * WB], arg=1.0)
            add(f"mla_cq{l}", "scaled", A_groups(w, 256, c00=3072), Y, L, dst=lambda i: cq[:, i, :], arg=1.0)
            add(f"mla_ckv{l}", "scaled", [([(kview(w, 0, DC, 3328, 160), 0, DC, 160)],
                                          [("A", 0, P), ("A", 64, 96)])], Y, L,
                dst=lambda i: (ckv[:, :], kpe[64:96, :])[i], arg=1.0)
            add(f"mla_uq{l}", "scaled", [([(kview(A["mla_w_uq_2"][l], 0, 2, 0, 768), 0, 2, 768)],
                                         [("A", 96 * i, 96) for i in range(MH)])],
                (lambda c: cqh[:, c, :], lambda c: cql[:, c, :]), L, dst=lambda i: mq[0:96, i, :],
                arg=float(96 ** -0.5))
            vcols = lambda ap: ap.rearrange("p (h n) -> p h n", h=MH)[:, :, 64:128]
            add(f"mla_ukv{l}", "scaled", [([(kview(A["mla_w_ukv_2"][l], 0, 1, 0, 1024), 0, 1, 1024)],
                                          [("A", P * i, P) for i in range(MH)] + [("B", t, vcols) for t in range(2)])],
                (lambda c: ckh[:, c, :], lambda c: ckl[:, c, :]), L,
                dst=lambda i: mk[0:64, i, :] if i < MH else mv[:, i - MH, :], arg=1.0)
            for g in range(3):
                add(f"gate{g}{l}", "sigmoid", A_groups(w, D, c00=3488 + g * D), Y, L, dst=lambda i: sig[:, i, :])
                add(f"branch{g}{l}", "mix", A_groups(A["w_branch_2"][l, g], D, ((0, 4),)),
                    (lambda c, g=g: ah[:, 4 * g + c, :], lambda c, g=g: al[:, 4 * g + c, :]), L, arg=g)
            add(f"mixed{l}", "copy_y", A_groups(A["w_out_2"][l], D), Y, L, arg=0)
            for s in range(4):
                add(f"up{l}{s}", "relu2", A_groups(A["w_up_2"][l], D, c00=s * D), Y, L)
                add(f"down{l}{s}", "copy_y", A_groups(A["w_down_2"][l], D, ((s * DC, DC),)),
                    (lambda c, s=s: ah[:, c - s * DC, :], lambda c, s=s: al[:, c - s * DC, :]), L, arg=s)

        chunks = blocks = hids = mixes = partials = relus = 0
        block_list, used = [], []
        G = {}
        for g in gemms:
            G[g.name] = g
            g.n0, g.s0, g.hid0, g.mix0, g.rl0 = chunks, blocks, hids, mixes, relus
            for bl, ch in g.groups:
                chunks += len(ch)
                for i, b in enumerate(bl):
                    block_list.append(b)
                    blocks += 1
                    if i == len(bl) - 1:
                        used.append(("chunk", chunks))
                    else:
                        partials += 1
                        used.append(("partial", partials))
            g.n1 = chunks
            g.nch = g.n1 - g.n0
            hids += {"swiglu": g.nch // 2, "relu2": g.nch}.get(g.kind, 0)
            relus += g.nch if g.kind == "relu2" else 0
            mixes += g.nch if g.kind == "mix" and g.arg else 0
        NB = blocks

        def with_diff(l):
            return [f"{k}{l}" for k in ("moba_q", "moba_k", "moba_v", "mla_cq", "mla_ckv")]

        def with_mla(l):
            return [f"{k}{l}" for k in ("branch0", "gate1", "branch1", "gate2")]

        WOVEN = {f"nat_{k}{g}" for k in "qkv" for g in range(1, 4)}
        for l in range(2):
            WOVEN |= {*with_diff(l), f"gate0{l}", *with_mla(l)}

        seq = [("m", b) for b in range(MOD0)]
        mod_after = {}
        spans = ((G["in000"].s0, G["ret_q0"].s0, MOD0, 36), (G["in010"].s0, G["in100"].s0, 36, 72))
        for w0, w1, m0, m1 in spans:
            for m in range(m0, m1):
                mod_after[w0 + (m - m0) * (w1 - w0 - 2) // (m1 - m0)] = m
        for i in range(NB):
            seq.append(("w", i))
            if i in mod_after:
                seq.append(("m", mod_after[i]))
        slot_of, value_of, counts = {}, {}, [0] * RAW
        for pos, (kind, i) in enumerate(seq):
            two = kind == "w" and len(block_list[i][0].shape) == 4
            counts[pos % RAW] += 32 if two else 16
            slot_of[kind, i], value_of[kind, i] = pos % RAW, counts[pos % RAW]

        norms = {}
        order = []

        def add_norm(name, **k):
            k["u"] = len(order)
            norms[name] = k
            order.append(name)

        def nmod(l, j):
            return dict(scale=lambda c, ts: nsc[:, 3 * l + j, c, ts:ts + 1],
                        bias=lambda c, ts: mod[:, l * NMOD + 24 * j + c, ts:ts + 1])

        def gcol(v, o):
            return dict(scale=lambda c, ts: v[:, o + c:o + c + 1], bias=lambda c, ts: zero[:, 0:1])

        N1 = dict(buf=(xh, xl, xt, sq), nc=DC, dim=D, src=lambda c: h[:, c, :])
        N2 = dict(buf=(yh, yl, yt, sq2), nc=DC, dim=D, src=lambda c: h[:, c, :])
        for l in range(2):
            for j in range(3):
                add_norm(f"n{l}{j}", **N1, tok=T if (l, j) == (1, 2) else T2, how="split", **nmod(l, j),
                         after={(0, 0): "init", (0, 1): "out001", (0, 2): "ret_out3", (1, 0): "out011",
                                (1, 1): "out101", (1, 2): "nat_o"}[l, j])
        add_norm("final", **N1, tok=T, how="assign", **gcol(vecA, VA["final"]), after="out111")
        for l in range(2):
            add_norm(f"mix_pre{l}", **N2, tok=T, how="split", **gcol(vecC, VC["mix_pre"] + 8 * l), after="self")
            add_norm(f"cq{l}", buf=(cqh, cql, yt, sq2), nc=2, dim=256, src=lambda c: cq[:, c, :], tok=T, how="split",
                     **gcol(vecC, VC["q_norm"] + 2 * l), after=f"mla_cq{l}")
            add_norm(f"ckv{l}", buf=(ckh, ckl, yt, sq2), nc=1, dim=128, src=lambda c: ckv[:, :], tok=T, how="split",
                     **gcol(vecC, VC["kv_norm"] + l), after=f"mla_ckv{l}")
            add_norm(f"mix_post{l}", **(N2 | dict(src=lambda c: yb[:, c, :])), tok=T, how="add",
                     **gcol(vecC, VC["mix_post"] + 8 * l), after=f"mixed{l}")
            add_norm(f"mlp_pre{l}", **N2, tok=T, how="split", **gcol(vecC, VC["mlp_pre"] + 8 * l), after="self")
            add_norm(f"mlp_post{l}", **(N2 | dict(src=lambda c: yb[:, c, :])), tok=T, how="add",
                     **gcol(vecC, VC["mlp_post"] + 8 * l), after=f"down{l}3")
        sqs = pieces = updates = 0
        for name in order:
            N = norms[name]
            N["sq0"], N["p0"], N["up0"] = sqs, pieces, updates
            sqs += N["nc"]
            if N["how"] == "split":
                pieces += N["nc"] * (N["tok"] // T)
            else:
                updates += N["nc"]

        class Att:
            pass

        atts = {}
        unit_total = tile_total = 0

        def add_att(name, tiles, bufs):
            nonlocal unit_total, tile_total
            a = Att()
            a.name, a.tiles, a.bufs = name, tiles, bufs
            a.u0, a.t0 = unit_total, tile_total
            a.units = [(t, i) for t, tile in enumerate(tiles) for i in range(len(tile["units"]))]
            unit_total += len(a.units)
            tile_total += len(tiles)
            a.u1, a.t1 = unit_total, tile_total
            atts[name] = a

        tiles = []
        for hd in range(NH):
            c, r = hd // 2, 64 * (hd % 2)
            for qt in range(2):
                tiles.append(dict(
                    units=[dict(qk=(nq[r:r + 64, c, P * qt:P * qt + P], nk[r:r + 64, c, :]), coef=None,
                                bias=(0, T, tt[:, hd % 2, 2 - 2 * qt:6 - 2 * qt, :]))],
                    keys=512, rows=(r, r + 64),
                    v=lambda k, hd=hd: nv[:, k, 64 * hd:64 * hd + 64],
                    out=(nah[r:r + 64, c, P * qt:P * qt + P], nal[r:r + 64, c, P * qt:P * qt + P]),
                    head=hd))
        for g in range(4):
            add_att(f"nat{g}", tiles[8 * g:8 * g + 8], (pexp, ptr, dg, stat))
        for l in range(2):
            B2 = (pexp2, ptr2, dg2, stat2)
            tiles = []
            for hd in range(DH):
                for qt in range(2):
                    n = P * (qt + 1)
                    y0 = P * (1 - qt)
                    tiles.append(dict(
                        units=[dict(qk=(q2[r:r + 64, hd, P * qt:P * qt + P], k2[r:r + 64, hd, 0:n]), coef=co,
                                    bias=(0, n, t5[:, hd, y0:y0 + n])) for r, co in ((0, None), (64, l))],
                        keys=n, rows=(0, P), v=lambda k, hd=hd: v2[:, k, P * hd:P * hd + P],
                        out=oraw[:, hd, P * qt:P * qt + P], head=hd))
            add_att(f"diff{l}", tiles, B2)
            tiles = []
            for hd in range(DH):
                for qt in range(2):
                    n = P * (qt + 1)
                    y0 = P * (1 - qt)
                    tiles.append(dict(
                        units=[dict(qk=(q3[:, hd, P * qt:P * qt + P], k3[:, hd, 0:n]), coef=None,
                                    bias=(0, n, t5[:, 4 + hd, y0:y0 + n]))],
                        keys=n, rows=(0, P), v=lambda k, hd=hd: v3[:, k, P * hd:P * hd + P],
                        out=(ah[:, 4 + hd, P * qt:P * qt + P], al[:, 4 + hd, P * qt:P * qt + P]), head=hd))
            add_att(f"moba{l}", tiles, B2)
            tiles = []
            for hd in range(MH):
                r = 64 * (hd % 2)
                for qt in range(2):
                    n = P * (qt + 1)
                    tiles.append(dict(
                        units=[dict(qk=(mq[0:96, hd, P * qt:P * qt + P], mk[0:96, hd, 0:n]), coef=None,
                                    bias=(P * qt, P * qt + P, cst[:, C_CAUSAL:C_CAUSAL + P]))],
                        keys=n, rows=(r, r + 64), v=lambda k, hd=hd: mv[:, k, 64 * hd:64 * hd + 64],
                        out=(ah[r:r + 64, 8 + hd // 2, P * qt:P * qt + P], al[r:r + 64, 8 + hd // 2, P * qt:P * qt + P]),
                        head=hd))
            add_att(f"mla{l}", tiles, B2)

        consts_in = sem("consts_in")
        rows_in = sem("rows_in")
        x_in = sem("x_in")
        small_in = sem("small_in")
        ret_consts_in = sem("ret_consts_in")
        raw_in = [sem(f"raw_in{i}") for i in range(RAW)]
        chunk_mod = sem("mod_row_in_psum")
        mod_row = sem("mod_row")
        mod_cols = sem("mod_cols")
        mod_out = sem("mod_out")
        mod_prod = sem("mod_products")
        mod_ctx = sem("mod_ctx_sums")
        mod_lat = sem("mod_latent_sums")
        mod_made = sem("mod_made")
        mod_taken = sem("mod_taken")
        w_high = sem("w_high_ready")
        w_low = sem("w_low_ready")
        block_used = sem("partial_block_used")
        chunk_ready = sem("chunk_ready")
        even_free = sem("even_chunk_out")
        odd_free = sem("odd_chunk_out")
        hid_f = sem("hidden_ready")
        hid_high = sem("hidden_high_ready")
        hid_low = sem("hidden_low_ready")
        mix_f = sem("mixed_ready")
        mix_high = sem("mixed_high_ready")
        mix_low = sem("mixed_low_ready")
        sq_ready = sem("square_ready")
        sq_used = sem("square_used")
        std_ready = sem("std_ready")
        rstd_ready = sem("rstd_ready")
        xt_ready = sem("scaled_ready")
        x_high = sem("x_high_ready")
        x_low = sem("x_low_ready")
        h_update = sem("h_updated")
        dve_chain = sem("dve_chain")
        act_chain = sem("act_chain")
        pool_ready = sem("pool_ready")
        vec_turned = sem("vectors_turned")
        vec_ready = sem("vectors_ready")
        x_turned = sem("x_turned")
        h_init = sem("h_init")
        c_silu = sem("c_silu")
        cexp = sem("decay_exp")
        cabs = sem("decay_abs")
        cln = sem("decay_ln")
        lg_ready = sem("log_decay_ready")
        lam_dots = sem("lambda_dots")
        lam_exp = sem("lambda_exp")
        coef_ready = sem("coefficients_ready")
        t5_g = sem("t5_product")
        t5_row = sem("t5_row_ready")
        t5_out = sem("t5_stored")
        t5_in = sem("t5_loaded")
        rpb_in = sem("rpb_in")
        rpb_out = sem("rpb_stored")
        tt_in = [sem(f"nat_bias_in{i}") for i in range(2)]
        tt_masked = sem("nat_bias_masked")
        rd_exp = sem("ret_decay_terms")
        rd_x = sem("ret_cross_ready")
        r_rope = sem("ret_rope_ready")
        r_score = sem("ret_scores_ready")
        r_att = sem("ret_weights_ready")
        r_o = sem("ret_o_ready")
        r_of = sem("ret_o_out")
        r_mu = sem("ret_mean_ready")
        r_cen = sem("ret_centred")
        r_sq = sem("ret_square")
        r_sqf = sem("ret_square_used")
        r_std = sem("ret_std_ready")
        r_gat = sem("ret_gated")
        r_high = sem("ret_high_ready")
        r_low = sem("ret_low_ready")
        s_ready = sem("scores_ready")
        s_max = sem("scores_max")
        p_ready = sem("probs_ready")
        dg_ready = sem("diagonal_ready")
        p_used = sem("probs_used")
        pt_out = sem("turned_probs_out")
        o_ready = sem("attention_out_ready")
        o_high = sem("attention_high_ready")
        o_low = sem("attention_low_ready")
        pos_in = sem("positions_in")
        ang_r = sem("angles_ready")
        sin_ready = sem("sines_ready")
        rot_x = sem("rotated_ready")
        rot_used = sem("rotated_used")
        roped = sem("rope_done")
        sub_sq = sem("subln_square")
        sub_ms = sem("subln_mean_square")
        sub_std = sem("subln_std")
        sub_t = sem("subln_scaled")
        sub_high = sem("subln_high")
        sub_low = sem("subln_low")
        out_turned = sem("out_turned")
        out_rows = sem("out_rows_ready")
        out_stored = sem("out_stored")

        def wait_chunk_out(eng, n):
            eng.wait_ge(odd_free if n % 2 else even_free, n // 2 + 1)

        def wait_gemm_out(eng, name):
            wait_chunk_out(eng, G[name].n1 - 2)
            wait_chunk_out(eng, G[name].n1 - 1)

        def halves(nk, w):
            m = (nk + 1) // 2 * w if nk > 1 else w // 2
            return (0, m), (m, nk * w)

        def run(steps):
            for _ in steps:
                pass

        def alongside(name, steps, gemm, others):
            na = len(atts[name].units)
            nb = sum(len(G[o].groups) for o in others)
            rest, done = both(*(gemm(o) for o in others)), 0
            for x in range(na):
                next(steps)
                while done < (x + 1) * nb // na:
                    next(rest)
                    done += 1
            run(steps)
            run(rest)

        def after_each(steps, parts):
            for _ in steps:
                next(parts, None)
            run(parts)

        def both(*stages):
            for st in stages:
                yield from st

        def scaled_src(g, i, ps, dst):
            r0 = 64 if g.name[:7] == "mla_ckv" and i == 1 else 0
            return ps[r0:r0 + dst.shape[0], 0:dst.shape[1]]

        def free(n):
            return odd_free if n % 2 else even_free

        def wait_block_used(eng, s):
            kind, v = used[s]
            eng.wait_ge(chunk_ready if kind == "chunk" else block_used, v)

        def wait_source(eng, N, c):
            a = N["after"]
            if a == "init":
                eng.wait_ge(h_init, c + 1)
            elif a == "self":
                eng.wait_ge(h_update, N["up0"] - N["nc"] + c + 1)
            else:
                wait_chunk_out(eng, G[a].n1 - N["nc"] + c if a[:7] != "mla_ckv" else G[a].n0)

        class Chain:

            def __init__(self, eng, s):
                self.eng, self.s, self.n = eng, s, 0

            def __call__(self, ins):
                self.n += 1
                ins.then_inc(self.s, 1)
                self.eng.wait_ge(self.s, self.n)

        block = ctx.enter_context(nc.Block())

        @block.sync
        def _(sp):
            sp.dma_start(cst[:, :], A["consts"][:, 0:C_HOT]).then_inc(consts_in, 16)
            for r0, n, i, src in (
                    (VA["b_mod0"], 72, 0, A["b_mod"][0:1]), (VA["norm_g"], 48, 0, A["norm_g"]),
                    (VA["final"], 8, 0, A["final_norm_g"]), (VB["b_mod1"], 72, 1, A["b_mod"][1:2]),
                    (VB["gn_g"], 16, 1, A["ret_gn_g"]), (VB["c"], 8, 1, A["c"]), (VB["c_ctx"], 8, 1, A["c_ctx"]),
                    (VC["mix_pre"], 16, 2, A["norm_mix_pre_2"]), (VC["mix_post"], 16, 2, A["norm_mix_post_2"]),
                    (VC["mlp_pre"], 16, 2, A["norm_mlp_pre_2"]), (VC["mlp_post"], 16, 2, A["norm_mlp_post_2"]),
                    (VC["q_norm"], 4, 2, A["mla_q_norm_2"]), (VC["kv_norm"], 2, 2, A["mla_kv_norm_2"]),
                    (VC["subln"], 2, 2, A["diff_subln_2"])):
                flat = src
                if len(src.shape) == 3:
                    flat = src.rearrange("a b (r n) -> (a b r) n", n=P)
                elif len(src.shape) == 2:
                    flat = src.rearrange("a (r n) -> (a r) n", n=P)
                else:
                    flat = src.rearrange("(r n) -> r n", n=P)
                sp.dma_start(vrows[r0:r0 + n, i, :], flat).then_inc(rows_in, 16)

            def load_block(pos):
                slot = pos % RAW
                if pos >= RAW:
                    kind, i = seq[pos - RAW]
                    if kind == "w":
                        sp.wait_ge(w_low, 2 * i + 2)
                    elif i < MOD0:
                        sp.wait_ge(chunk_mod, i + 1)
                    else:
                        sp.wait_ge(mod_ctx, (DC - 1) * (i - MOD0 + 1))
                        sp.wait_ge(mod_lat, i - MOD0 + 1)
                kind, i = seq[pos]
                if kind == "m":
                    l, c0 = i // 36, (i % 36) * WB
                    dst = raw[slot][:, :].rearrange("p (k n) -> p k n", k=DC)
                    sp.dma_start(dst, kview(A["w_mod"][l], 0, DC, c0, WB)).then_inc(raw_in[slot], 16)
                    return
                ap, k0, nk, w = block_list[i]
                if len(ap.shape) == 4:
                    for s in range(2):
                        dst = raw[slot][:, 0:nk * w].rearrange("p (k s n) -> p k s n", k=nk, s=2)[:, :, s, :]
                        sp.dma_start(dst, ap[:, :, s, :]).then_inc(raw_in[slot], 16)
                    return
                dst = raw[slot][:, 0:nk * w].rearrange("p (k n) -> p k n", k=nk)
                sp.dma_start(dst, ap).then_inc(raw_in[slot], 16)

            for b in range(4):
                load_block(b)
            for t in range(4):
                src = A["x"] if t < 2 else A["ctx"]
                sp.dma_start(xrows[:, t, :], src[0, P * (t % 2):P * (t % 2) + P, :]).then_inc(x_in, 16)
            for b in range(4, len(seq)):
                load_block(b)
            for t in range(2):
                sp.wait_ge(out_rows, 4 * (t + 1))
                sp.dma_start(A["out"][0, P * t:P * t + P, :],
                             out_buf[t]).then_inc(out_stored, 16)
            sp.wait_ge(out_stored, 32)

        @block.gpsimd
        def _(pool):
            def mod_range(b0, b1):
                for b in range(b0, b1):
                    i = b - MOD0
                    slot = slot_of["m", b]
                    pool.wait_ge(raw_in[slot], value_of["m", b])
                    if i >= 2:
                        pool.wait_ge(mod_made, i - 1)
                    acc = macc[:, i % 2, 1, :]

                    def product(k):
                        p = (DC - 1) * i + k - 1
                        if k and p >= 2:
                            pool.wait_ge(mod_ctx, p - 1)
                        dst = mprod[:, p % 2, :] if k else acc
                        pool.tensor_tensor(dst, raw[slot][:, WB * k:WB * k + WB], sc[:, k, 1:2].to_broadcast([P, WB]),
                                           ALU.mult).then_inc(mod_prod, 1)

                    product(0)
                    product(1)
                    for k in range(1, DC):
                        p = (DC - 1) * i + k - 1
                        pool.wait_ge(mod_prod, DC * i + k + 1)
                        if k > 1:
                            pool.wait_ge(mod_ctx, p)
                        pool.tensor_tensor(acc, acc, mprod[:, p % 2, :], ALU.add).then_inc(mod_ctx, 1)
                        if k + 1 < DC:
                            product(k + 1)

            pool.memset(ones[:, :], 1.0).then_inc(pool_ready, 1)
            pool.memset(zero[:, :], 0.0).then_inc(pool_ready, 1)
            pool.memset(eps[:, :], EPS).then_inc(pool_ready, 1)
            pool.memset(rpbp[:, :], 0.0).then_inc(pool_ready, 1)
            pool.memset(tab[:, :], 1.0).then_inc(pool_ready, 1)
            pool.wait_ge(pool_ready, 5)
            dsrc = lambda a: bass.AP(a.tensor, a.offset, [[0, P], [1, 4]])
            pool.dma_start(dec[:, 0:4], dsrc(A["ret_decay_f"])).then_inc(small_in, 16)
            pool.dma_start(dec[:, 4:8], dsrc(A["ret_decay_b"])).then_inc(small_in, 16)
            pool.dma_start(lamv[:, :, :, :], bass.AP(A["diff_lambda_2"].tensor, 0, [[0, P], [1, 512]])).then_inc(small_in, 16)
            pool.dma_start(tab[0:32, :], A["rel_bias_2"]).then_inc(small_in, 16)
            pool.dma_start(hot[:, :], A["consts"][0:33, C_HOT:C_HOT + 512]).then_inc(small_in, 16)
            for hd in range(NH):
                pool.dma_start(rpbp[7 * hd:7 * hd + 7, 48:79], A["nat_rpb"][0, hd, 4:11, :]).then_inc(rpb_in, 16)
            pool.wait_ge(rpb_in, 16 * NH)
            pool.dma_start(rpb_dram.ap(), rpbp[:, :]).then_inc(rpb_out, 16)
            pool.wait_ge(t5_row, 1)
            pool.dma_start(t5_dram.ap(), gt5[:, :]).then_inc(t5_out, 16)
            pool.wait_ge(x_turned, 8)
            pool.wait_ge(h_init, 8)
            pool.wait_ge(coef_ready, 1)
            pool.wait_ge(t5_out, 16)
            pool.wait_ge(rpb_out, 16)
            mod_range(MOD0, 36)
            wait_gemm_out(pool, "out001")
            pool.dma_start(cret[:, :], A["ret_consts"]).then_inc(ret_consts_in, 16)
            wait_gemm_out(pool, f"ret_out{RH - 1}")
            mod_range(36, 72)
            wait_gemm_out(pool, "out101")
            for hd in range(NH):
                if hd >= 2:
                    pool.wait_ge(s_ready, atts["nat0"].u0 + 2 * (hd - 2) + 2)
                for r2 in range(2):
                    src = bass.AP(rpb_dram, (7 * hd + 1 - r2) * 127, [[1, 64], [127, 6], [1, 64]])
                    pool.dma_start(tt[64 * r2:64 * r2 + 64, hd % 2, :, :], src).then_inc(tt_in[hd % 2], 16)
            pool.wait_ge(x_low, norms["mix_pre0"]["p0"])
            pool.wait_ge(h_update, 8)
            for g in range(8):
                src = bass.AP(t5_dram, g * 512, [[1, P], [1, 384]])
                pool.dma_start(t5[:, g, :], src).then_inc(t5_in, 16)
            pool.dma_start(po[64:96, :], bass.AP(A["positions_2"].tensor, 0, [[0, 32], [1, T]])).then_inc(pos_in, 16)

        @block.scalar
        def _(act):
            chain = Chain(act, act_chain)
            split = [0]

            def splits_upto(s):
                while split[0] <= min(s, NB - 1):
                    i = split[0]
                    _, _, nk, w = block_list[i]
                    act.wait_ge(raw_in[slot_of["w", i]], value_of["w", i])
                    if i >= SPL:
                        wait_block_used(act, i - SPL)
                    for a, b in halves(nk, w):
                        act.activation(wh[i % SPL][:, a:b], raw[slot_of["w", i]][:, a:b], ACT.Copy).then_inc(w_high, 1)
                    split[0] += 1

            def norm(name):
                N = norms[name]
                X_h, X_l, x_t, s_q = N["buf"]
                u, tok = N["u"], N["tok"]
                for c in range(N["nc"]):
                    wait_source(act, N, c)
                    i = N["sq0"] + c
                    if i >= 2:
                        act.wait_ge(sq_used, i - 1)
                    act.activation(s_q[:, i % 2, 0:tok], N["src"](c)[:, 0:tok], ACT.Square).then_inc(sq_ready, 1)
                act.wait_ge(sq_used, N["sq0"] + N["nc"])
                if u >= 1:
                    act.wait_ge(rstd_ready, u)
                act.activation(std[:, 0:tok], aux[3][:, 0:tok], ACT.Sqrt, bias=eps[:, 0:1],
                               scale=1.0 / N["dim"]).then_inc(std_ready, 1)
                if N["how"] == "split":
                    for k in range(N["nc"] * (tok // T)):
                        c, ts = divmod(k, tok // T)
                        p = N["p0"] + k
                        act.wait_ge(xt_ready, p + 1)
                        act.activation(X_h[:, c, ts * T:ts * T + T], x_t[:, p % 4, :], ACT.Identity,
                                       bias=N["bias"](c, ts)).then_inc(x_high, 1)

            def gemm(name, by_chunk=False):
                g = G[name]
                n, s = g.n0, g.s0
                t0, t1 = g.tok
                tok = t1 - t0
                if n:
                    wait_chunk_out(act, n - 2)
                    wait_chunk_out(act, n - 1)
                for bl, ch in g.groups:
                    s += len(bl)
                    splits_upto(s)
                    for ci, (o, a0, M) in enumerate(ch):
                        i = n - g.n0
                        ps = bank[n % 4]
                        if g.kind == "scaled":
                            if n % 2 == 0:
                                act.wait_ge(chunk_ready, n + 1)
                                dst = g.dst(i)
                                act.activation(dst, scaled_src(g, i, ps, dst), ACT.Copy, scale=g.arg).then_inc(free(n), 1)
                        elif g.kind == "silu":
                            act.wait_ge(chunk_ready, n + 1)
                            act.activation(g.dst(i), ps[:, 0:tok], ACT.Silu).then_inc(free(n), 1)
                        elif g.kind == "sigmoid":
                            act.wait_ge(chunk_ready, n + 1)
                            act.activation(g.dst(i), ps[:, 0:tok], ACT.Tanh, scale=0.5).then_inc(free(n), 1)
                        elif g.kind == "swiglu":
                            pr = g.hid0 + i // 2
                            if n % 2 == 0:
                                act.wait_ge(chunk_ready, n + 1)
                                if n >= 4:
                                    act.wait_ge(odd_free, n // 2 - 1)
                                act.activation(sa[:, pr % 2, 0:tok], ps[:, 0:tok], ACT.Silu).then_inc(even_free, 1)
                            else:
                                act.wait_ge(odd_free, n // 2 + 1)
                                act.activation(hidh[:, i // 2, 0:tok], hf[:, pr % 2, 0:tok], ACT.Copy).then_inc(hid_high, 1)
                        elif g.kind == "relu2":
                            pr = g.hid0 + i
                            act.wait_ge(hid_f, g.rl0 + i + 1)
                            act.activation(ah[:, i, :], hf2[:, pr % 2, :], ACT.Copy).then_inc(hid_high, 1)
                        elif g.kind == "mix" and g.arg == 2:
                            m = g.mix0 + i
                            act.wait_ge(mix_f, m + 1)
                            act.activation(yh[:, i, :], mixed[:, i, :], ACT.Copy, scale=0.5).then_inc(mix_high, 1)
                        n += 1
                        if ci == len(ch) - 1 and name not in WOVEN:
                            splits_upto(s + 1)
                        if by_chunk or ci == len(ch) - 1:
                            yield 1

            def attention(name):
                a = atts[name]
                pe_, pt_, dg_, st_ = a.bufs

                def turn_out(t):
                    tg = a.t0 + t
                    last = a.u0 + max(j for j, (tt_, _) in enumerate(a.units) if tt_ == t)
                    act.wait_ge(p_used, last + 1)
                    if tg >= 2:
                        act.wait_ge(o_ready, tg - 1)
                    k = a.tiles[t]["keys"]
                    act.activation(pt_[:, tg % 2, 0:k], aux[2][:, 0:k], ACT.Copy).then_inc(pt_out, 1)

                def out_high(t):
                    tg = a.t0 + t
                    tile = a.tiles[t]
                    r0, r1 = tile["rows"]
                    act.wait_ge(o_ready, tg + 1)
                    dst = tile["out"][0] if isinstance(tile["out"], tuple) else tile["out"]
                    act.activation(dst, aux[3][r0:r1, 0:P], ACT.Copy).then_inc(o_high, 1)

                def exponentials(j):
                    t, i = a.units[j]
                    u = a.u0 + j
                    k = a.tiles[t]["keys"]
                    act.wait_ge(s_max, u + 1)
                    if u >= 2:
                        act.wait_ge(p_used, u - 1)
                    if u >= 8:
                        act.wait_ge(dg_ready, u - 7)
                    act.activation(pe_[:, u % 2, 0:k], aux[u % 2][:, 0:k], ACT.Exp, bias=st_[:, 0, u % 8:u % 8 + 1],
                                   accum_out=st_[:, 1, u % 8:u % 8 + 1]).then_inc(p_ready, 1)

                exponentials(0)
                for j, (t, i) in enumerate(a.units):
                    if j and a.units[j - 1][0] != t:
                        turn_out(t - 1)
                        if t >= 2:
                            out_high(t - 2)
                    if j + 1 < len(a.units):
                        exponentials(j + 1)
                    yield 1
                turn_out(len(a.tiles) - 1)
                out_high(len(a.tiles) - 2)
                out_high(len(a.tiles) - 1)

            act.wait_ge(pool_ready, 5)
            act.wait_ge(vec_ready, 3)
            act.activation(sc[:, :, 0], vecB[:, VB["c"]:VB["c"] + 8], ACT.Silu).then_inc(c_silu, 1)
            act.activation(sc[:, :, 1], vecB[:, VB["c_ctx"]:VB["c_ctx"] + 8], ACT.Silu).then_inc(c_silu, 1)
            for b in range(4):
                act.wait_ge(chunk_mod, b + 1)
                act.activation(mrow[:, b % 4, :], bank[b % 4][0:2, 0:WB], ACT.Copy).then_inc(mod_row, 1)
            for c in range(DC):
                act.wait_ge(x_turned, c + 1)
                act.activation(h[:, c, :], aux[c % 4][:, :], ACT.Copy).then_inc(h_init, 1)
            act.wait_ge(small_in, 80)
            chain(act.activation(lg[:, 0, :], dec[:, :], ACT.Abs))
            act.activation(lg[:, 1, :], lg[:, 0, :], ACT.Exp, scale=-1.0).then_inc(cexp, 1)
            act.wait_ge(cabs, 1)
            act.activation(lg[:, 3, :], lg[:, 2, :], ACT.Ln).then_inc(cln, 1)
            act.wait_ge(lam_dots, 1)
            act.activation(lam[:, 4:8], lam[:, 0:4], ACT.Exp).then_inc(lam_exp, 1)
            for b in range(4, MOD0):
                act.wait_ge(chunk_mod, b + 1)
                if b >= 4:
                    act.wait_ge(mod_cols, b - 3)
                act.activation(mrow[:, b % 4, :], bank[b % 4][0:2, 0:WB], ACT.Copy).then_inc(mod_row, 1)

            def ffn(l, f, j):
                norm(f"n{l}{j}")
                for s in range(2):
                    run(gemm(f"in{l}{f}{s}"))
                    run(gemm(f"out{l}{f}{s}"))

            splits_upto(1)
            act.wait_ge(rpb_out, 16)
            act.wait_ge(t5_out, 16)
            ffn(0, 0, 0)
            def squares(hh):
                for v in range(4):
                    act.wait_ge(r_cen, 4 * hh + v + 1)
                    i = 4 * hh + v
                    if i >= 2:
                        act.wait_ge(r_sqf, i - 1)
                    act.activation(sa[:, i % 2, :], oc[:, v, :], ACT.Square).then_inc(r_sq, 1)

            def gated(hh):
                act.wait_ge(r_sqf, 4 * hh + 4)
                act.activation(std[:, :], aux[1][:, :], ACT.Sqrt, bias=eps[:, 0:1], scale=1.0 / 512).then_inc(r_std, 1)
                yield 1
                for v in range(4):
                    act.wait_ge(r_gat, 4 * hh + v + 1)
                    act.activation(oh[:, v, :], oc[:, v, :], ACT.Copy).then_inc(r_high, 1)
                    yield 1

            norm("n01")
            for hh in range(RH):
                if hh == 0:
                    act.wait_ge(ret_consts_in, 16)
                    act.wait_ge(lg_ready, 3)
                f, b = lg[:, 4, hh:hh + 1], lg[:, 4, 4 + hh:5 + hh]
                f2, b2 = lg[:, 5, hh:hh + 1], lg[:, 5, 4 + hh:5 + hh]
                if hh:
                    act.wait_ge(r_att, 3 * hh)
                act.activation(dx[:, 1, :], cret[:, C_DIFF:C_DIFF + 384], ACT.Exp, bias=f2, scale=f).then_inc(rd_exp, 1)
                act.wait_ge(rd_x, 4 * hh + 1)
                act.activation(dx[:, 2, :], cret[:, C_DIFF:C_DIFF + 384], ACT.Exp, bias=b2,
                               scale=dxb[:, 0:1]).then_inc(rd_exp, 1)
                act.wait_ge(rd_x, 4 * hh + 3)
                act.activation(dx[:, 0, :], dx[:, 0, :], ACT.Exp).then_inc(rd_exp, 1)
                if hh:
                    for v in range(4):
                        act.wait_ge(r_o, 4 * hh - 4 + v + 1)
                        if hh > 1 and v == 0:
                            act.wait_ge(r_low, 4 * (hh - 1))
                        act.activation(oc[:, v, :], aux[(v + 3) % 4][:, :], ACT.Copy).then_inc(r_of, 1)
                run(gemm(f"ret_q{hh}"))
                if hh:
                    squares(hh - 1)
                run(gemm(f"ret_k{hh}"))
                after_each(gemm(f"ret_v{hh}", True), gated(hh - 1) if hh else iter(()))
                if hh:
                    run(gemm(f"ret_out{hh - 1}"))
                run(gemm(f"ret_g{hh}"))
            hh = RH - 1
            for v in range(4):
                act.wait_ge(r_o, 4 * hh + v + 1)
                if v == 0:
                    act.wait_ge(r_low, 4 * hh)
                act.activation(oc[:, v, :], aux[(v + 3) % 4][:, :], ACT.Copy).then_inc(r_of, 1)
            squares(hh)
            run(gated(hh))
            run(gemm(f"ret_out{hh}"))
            ffn(0, 1, 2)
            ffn(1, 0, 0)
            norm("n11")
            run(gemm("nat_q0"))
            run(gemm("nat_k0"))
            run(gemm("nat_v0"))
            for g in range(4):
                nxt = [f"nat_{k}{g + 1}" for k in "qkv"] if g < 3 else []
                alongside(f"nat{g}", attention(f"nat{g}"), gemm, nxt)
            run(gemm("nat_o"))
            ffn(1, 1, 2)
            norm("final")
            for l in range(2):
                norm(f"mix_pre{l}")
                for k in "qkv":
                    run(gemm(f"diff_{k}{l}"))
                if l == 0:
                    act.wait_ge(ang_r, 1)
                    act.activation(ang[64:96, 1, :], ang[64:96, 0, :], ACT.Sin).then_inc(sin_ready, 1)
                    act.activation(ang[64:96, 2, :], ang[64:96, 0, :], ACT.Sin, scale=0.5).then_inc(sin_ready, 1)
                alongside(f"diff{l}", attention(f"diff{l}"), gemm, with_diff(l))
                def head_square(hd):
                    i = DH * l + hd
                    act.wait_ge(o_high, atts[f"diff{l}"].t0 + 2 * hd + 2)
                    if i >= 2:
                        act.wait_ge(sub_ms, i - 1)
                    act.activation(sq2[:, i % 2, :], oraw[:, hd, :], ACT.Square).then_inc(sub_sq, 1)

                def head_high(hd):
                    act.wait_ge(sub_t, DH * l + hd + 1)
                    act.activation(ah[:, hd, :], oraw[:, hd, :], ACT.Copy, scale=1.0 - LAM_INIT[l]).then_inc(sub_high, 1)

                head_square(0)
                head_square(1)
                for hd in range(DH):
                    i = DH * l + hd
                    act.wait_ge(sub_ms, i + 1)
                    if i >= 2:
                        act.wait_ge(sub_t, i - 1)
                    act.activation(std[:, T * (i % 2):T * (i % 2) + T], aux[2 + i % 2][:, 0:T], ACT.Sqrt, bias=eps[:, 0:1],
                                   scale=1.0 / P).then_inc(sub_std, 1)
                    if hd + 2 < DH:
                        head_square(hd + 2)
                    if hd:
                        head_high(hd - 1)
                head_high(DH - 1)
                norm(f"cq{l}")
                norm(f"ckv{l}")
                run(gemm(f"mla_uq{l}"))
                run(gemm(f"mla_ukv{l}"))
                alongside(f"moba{l}", attention(f"moba{l}"), gemm, [f"gate0{l}"])
                alongside(f"mla{l}", attention(f"mla{l}"), gemm, with_mla(l))
                run(gemm(f"branch2{l}"))
                run(gemm(f"mixed{l}"))
                norm(f"mix_post{l}")
                norm(f"mlp_pre{l}")
                for s in range(4):
                    run(gemm(f"up{l}{s}"))
                    run(gemm(f"down{l}{s}"))
                norm(f"mlp_post{l}")

        @block.vector
        def _(dve):
            chain = Chain(dve, dve_chain)
            split = [0]

            taken = set()

            def sum_mod(b):
                i = b - MOD0
                slot = slot_of["m", b]
                dve.wait_ge(raw_in[slot], value_of["m", b])
                if i >= 2:
                    dve.wait_ge(mod_made, i - 1)
                acc = macc[:, i % 2, 0, :]
                chain(dve.tensor_scalar(acc, raw[slot][:, 0:WB], sc[:, 0, 0:1], None, ALU.mult))
                for k in range(1, DC):
                    ins = dve.scalar_tensor_tensor(out=acc, in0=raw[slot][:, WB * k:WB * k + WB], scalar=sc[:, k, 0:1],
                                                   in1=acc, op0=ALU.mult, op1=ALU.add)
                    if k < DC - 1:
                        chain(ins)
                ins.then_inc(mod_lat, 1)

            def take_mod(b):
                i = b - MOD0
                taken.add(b)
                v = vecA if b < 36 else vecB
                c = 2 * (b % 36)
                dve.wait_ge(mod_made, i + 1)
                dve.tensor_tensor(mod[:, 2 * b:2 * b + 2, :], aux[i % 2][:, 0:4].rearrange("p (c v) -> p c v", v=2),
                                  v[:, c:c + 2].unsqueeze(2).to_broadcast([P, 2, 2]), ALU.add).then_inc(mod_taken, 1)

            def splits_upto(s):
                while split[0] <= min(s, NB - 1):
                    i = split[0]
                    _, _, nk, w = block_list[i]
                    if i - 2 in mod_after:
                        sum_mod(mod_after[i - 2])
                    if i - 4 in mod_after and mod_after[i - 4] not in taken:
                        take_mod(mod_after[i - 4])
                    for j, (a, b) in enumerate(halves(nk, w)):
                        dve.wait_ge(w_high, 2 * i + j + 1)
                        dve.tensor_tensor(wl[i % SPL][:, a:b], raw[slot_of["w", i]][:, a:b],
                                          wh[i % SPL][:, a:b].bitcast(F32), ALU.subtract).then_inc(w_low, 1)
                    split[0] += 1

            def norm(name):
                N = norms[name]
                X_h, X_l, x_t, s_q = N["buf"]
                u, tok = N["u"], N["tok"]
                dve.wait_ge(std_ready, u + 1)
                if N["p0"]:
                    dve.wait_ge(x_low, N["p0"])
                dve.reciprocal(rstd[:, 0:tok], std[:, 0:tok]).then_inc(rstd_ready, 1)
                dve.wait_ge(rstd_ready, u + 1)
                if N["how"] != "split":
                    for c in range(N["nc"]):
                        if N["how"] == "assign":
                            dve.scalar_tensor_tensor(out=h[:, c, 0:T], in0=h[:, c, 0:T], scalar=N["scale"](c, 0),
                                                     in1=rstd[:, 0:T], op0=ALU.mult, op1=ALU.mult).then_inc(h_update, 1)
                        else:
                            chain(dve.scalar_tensor_tensor(out=yb[:, c, :], in0=yb[:, c, :], scalar=N["scale"](c, 0),
                                                           in1=rstd[:, 0:T], op0=ALU.mult, op1=ALU.mult))
                            dve.tensor_tensor(h[:, c, 0:T], h[:, c, 0:T], yb[:, c, :], ALU.add).then_inc(h_update, 1)
                    return

                def low(k):
                    c, ts = divmod(k, tok // T)
                    p = N["p0"] + k
                    dve.wait_ge(x_high, p + 1)
                    dve.scalar_tensor_tensor(out=X_l[:, c, ts * T:ts * T + T], in0=x_t[:, p % 4, :],
                                             scalar=N["bias"](c, ts), in1=X_h[:, c, ts * T:ts * T + T].bitcast(F32),
                                             op0=ALU.add, op1=ALU.subtract).then_inc(x_low, 1)

                n = N["nc"] * (tok // T)
                for k in range(n):
                    c, ts = divmod(k, tok // T)
                    p = N["p0"] + k
                    if p >= 4:
                        dve.wait_ge(x_low, p - 3)
                    dve.scalar_tensor_tensor(out=x_t[:, p % 4, :], in0=N["src"](c)[:, ts * T:ts * T + T],
                                             scalar=N["scale"](c, ts), in1=rstd[:, ts * T:ts * T + T],
                                             op0=ALU.mult, op1=ALU.mult).then_inc(xt_ready, 1)
                    if k >= 2:
                        low(k - 2)
                for k in range(max(0, n - 2), n):
                    low(k)

            def gemm(name, by_chunk=False):
                g = G[name]
                n, s = g.n0, g.s0
                t0, t1 = g.tok
                tok = t1 - t0
                if n:
                    wait_chunk_out(dve, n - 2)
                    wait_chunk_out(dve, n - 1)
                for bl, ch in g.groups:
                    s += len(bl)
                    splits_upto(s)
                    for ci, (o, a0, M) in enumerate(ch):
                        i = n - g.n0
                        ps = bank[n % 4]
                        if g.kind == "scaled":
                            if n % 2:
                                dve.wait_ge(chunk_ready, n + 1)
                                dst = g.dst(i)
                                dve.tensor_scalar(dst, scaled_src(g, i, ps, dst), g.arg, None,
                                                  ALU.mult).then_inc(free(n), 1)
                        elif g.kind == "resid":
                            dve.wait_ge(chunk_ready, n + 1)
                            for ts in range(tok // T):
                                ins = dve.scalar_tensor_tensor(
                                    out=h[:, i, ts * T:ts * T + T], in0=ps[:, ts * T:ts * T + T],
                                    scalar=half[:, g.arg, i, ts:ts + 1], in1=h[:, i, ts * T:ts * T + T],
                                    op0=ALU.mult, op1=ALU.add)
                            ins.then_inc(free(n), 1)
                        elif g.kind == "swiglu":
                            pr = g.hid0 + i // 2
                            if n % 2:
                                dve.wait_ge(chunk_ready, n + 1)
                                dve.wait_ge(even_free, n // 2 + 1)
                                if pr >= 2:
                                    dve.wait_ge(hid_low, pr - 1)
                                dve.tensor_tensor(hf[:, pr % 2, 0:tok], sa[:, pr % 2, 0:tok], ps[:, 0:tok],
                                                  ALU.mult).then_inc(odd_free, 1)
                                dve.wait_ge(hid_high, pr + 1)
                                dve.tensor_tensor(hidl[:, i // 2, 0:tok], hf[:, pr % 2, 0:tok],
                                                  hidh[:, i // 2, 0:tok].bitcast(F32), ALU.subtract).then_inc(hid_low, 1)
                        elif g.kind == "relu2":
                            pr = g.hid0 + i
                            dve.wait_ge(chunk_ready, n + 1)
                            if pr >= 2:
                                dve.wait_ge(hid_low, pr - 1)
                            dve.tensor_scalar(yt[:, pr % 4, :], ps[:, 0:T], 0.0, None, ALU.max).then_inc(free(n), 1)
                            dve.wait_ge(free(n), n // 2 + 1)
                            dve.tensor_tensor(hf2[:, pr % 2, :], yt[:, pr % 4, :], yt[:, pr % 4, :],
                                              ALU.mult).then_inc(hid_f, 1)
                            dve.wait_ge(hid_high, pr + 1)
                            dve.tensor_tensor(al[:, i, :], hf2[:, pr % 2, :], ah[:, i, :].bitcast(F32),
                                              ALU.subtract).then_inc(hid_low, 1)
                        elif g.kind == "mix":
                            m = g.mix0 + i
                            dve.wait_ge(chunk_ready, n + 1)
                            if g.arg == 0:
                                dve.scalar_tensor_tensor(out=mixed[:, i, :], in0=sig[:, i, :], scalar=1.0, in1=ps[:, 0:T],
                                                         op0=ALU.add, op1=ALU.mult).then_inc(free(n), 1)
                            else:
                                dve.scalar_tensor_tensor(out=yt[:, m % 4, :], in0=sig[:, i, :], scalar=1.0, in1=ps[:, 0:T],
                                                         op0=ALU.add, op1=ALU.mult).then_inc(free(n), 1)
                                dve.wait_ge(free(n), n // 2 + 1)
                                if g.arg == 2:
                                    dve.wait_ge(mix_f, m - 7)
                                dve.tensor_tensor(mixed[:, i, :], mixed[:, i, :], yt[:, m % 4, :],
                                                  ALU.add).then_inc(mix_f, 1)
                            if g.arg == 2:
                                dve.wait_ge(mix_f, m + 1)
                                dve.wait_ge(mix_high, 8 * (m // 16) + i + 1)
                                dve.scalar_tensor_tensor(out=yl[:, i, :], in0=mixed[:, i, :], scalar=0.5,
                                                         in1=yh[:, i, :].bitcast(F32), op0=ALU.mult,
                                                         op1=ALU.subtract).then_inc(mix_low, 1)
                        elif g.kind == "copy_y":
                            dve.wait_ge(chunk_ready, n + 1)
                            if g.arg == 0:
                                dve.tensor_copy(yb[:, i, :], ps[:, 0:T]).then_inc(free(n), 1)
                            else:
                                dve.tensor_tensor(yb[:, i, :], yb[:, i, :], ps[:, 0:T], ALU.add).then_inc(free(n), 1)
                        n += 1
                        if ci == len(ch) - 1 and name not in WOVEN:
                            splits_upto(s + 1)
                        if by_chunk or ci == len(ch) - 1:
                            yield 1

            def attention(name):
                a = atts[name]
                pe_, pt_, dg_, st_ = a.bufs

                def row_max(j):
                    t, i = a.units[j]
                    u = a.u0 + j
                    k = a.tiles[t]["keys"]
                    s8 = u % 8
                    dve.wait_ge(s_ready, u + 1)
                    if u >= 8:
                        dve.wait_ge(p_used, u - 7)
                    chain(dve.tensor_reduce(st_[:, 2, s8:s8 + 1], aux[u % 2][:, 0:k], AX.X, ALU.max))
                    dve.tensor_scalar(st_[:, 0, s8:s8 + 1], st_[:, 2, s8:s8 + 1], -1.0, None, ALU.mult).then_inc(s_max, 1)

                def diagonal(j):
                    t, i = a.units[j]
                    u = a.u0 + j
                    s8 = u % 8
                    dve.wait_ge(p_ready, u + 1)
                    if u >= 2:
                        dve.wait_ge(p_used, u - 1)
                    chain(dve.reciprocal(st_[:, 3, s8:s8 + 1], st_[:, 1, s8:s8 + 1]))
                    co = a.tiles[t]["units"][i]["coef"]
                    if co is None:
                        dve.tensor_scalar(dg_[:, u % 2, :], ident, st_[:, 3, s8:s8 + 1], None,
                                          ALU.mult).then_inc(dg_ready, 1)
                    else:
                        dve.tensor_scalar(dg_[:, u % 2, :], ident, st_[:, 3, s8:s8 + 1], lamn[:, co:co + 1],
                                          ALU.mult, ALU.mult).then_inc(dg_ready, 1)

                def out_low(t):
                    tg = a.t0 + t
                    tile = a.tiles[t]
                    r0, r1 = tile["rows"]
                    dve.wait_ge(o_high, tg + 1)
                    if isinstance(tile["out"], tuple):
                        dve.tensor_tensor(tile["out"][1], aux[3][r0:r1, 0:P], tile["out"][0].bitcast(F32),
                                          ALU.subtract).then_inc(o_low, 1)
                    else:
                        dve.sem_inc(o_low, 1)

                def mask_bias(hd):
                    dve.wait_ge(tt_in[hd % 2], 32 * (hd // 2 + 1))
                    b = tt[:, hd % 2, :, :]
                    m = cst[:, C_MASK:C_MASK + 64]
                    for e in range(6):
                        ins = dve.tensor_tensor(tt[:, hd % 2, e, :], tt[:, hd % 2, e, :], m, ALU.add)
                    ins.then_inc(tt_masked, 1)

                n = len(a.units)
                if name == "nat0":
                    mask_bias(0)
                    mask_bias(1)
                row_max(0)
                for j, (t, i) in enumerate(a.units):
                    diagonal(j)
                    if j + 1 < n:
                        row_max(j + 1)
                    if j and a.units[j - 1][0] != t and t >= 2:
                        out_low(t - 2)
                    if name[:3] == "nat" and j % 2 == 0:
                        hd = 4 * int(name[3]) + j // 2 + 1
                        if 2 <= hd < NH:
                            mask_bias(hd)
                    yield 1
                out_low(len(a.tiles) - 2)
                out_low(len(a.tiles) - 1)

            def take_rows(q):
                dve.wait_ge(mod_cols, 4 * q + 4)
                dve.tensor_copy(mod[:, 8 * q:8 * q + 8, :],
                                aux[q % 2][:, 0:16].rearrange("p (c v) -> p c v", v=2)).then_inc(mod_out, 1)

            def coefficients(i):
                m0 = NMOD * (i // 3) + 24 * (i % 3)
                for v in range(2):
                    chain(dve.scalar_tensor_tensor(out=nsc[:, i, :, v], in0=mod[:, m0 + 8:m0 + 16, v], scalar=1.0,
                                                   in1=vecA[:, VA["norm_g"] + 8 * i:VA["norm_g"] + 8 * i + 8],
                                                   op0=ALU.add, op1=ALU.mult))
                dve.tensor_scalar(half[:, i, :, :], mod[:, m0 + 16:m0 + 24, :], 1.0 if i % 3 == 1 else 0.5, None,
                                  ALU.mult).then_inc(coef_ready, 1)

            dve.wait_ge(vec_turned, 3)
            for i, (v, w) in enumerate(((vecA, P), (vecB, NVB), (vecC, NVC))):
                dve.tensor_copy(v[:, :], aux[i][:, 0:w]).then_inc(vec_ready, 1)
            dve.wait_ge(small_in, 80)
            take_rows(0)
            dve.wait_ge(t5_g, 1)
            dve.tensor_copy(gt5[:, :], aux[3][0:8, :]).then_inc(t5_row, 1)
            dve.wait_ge(cexp, 1)
            dve.tensor_scalar(lg[:, 2, :], lg[:, 1, :], 1.0, None, ALU.add).then_inc(cabs, 1)
            dve.wait_ge(cln, 1)
            chain(dve.tensor_scalar(lg[:, 2, :], lg[:, 2, :], -1.0, 1e-30, ALU.add, ALU.max))
            chain(dve.reciprocal(lg[:, 2, :], lg[:, 2, :]))
            chain(dve.tensor_tensor(lg[:, 2, :], lg[:, 2, :], lg[:, 1, :], ALU.mult))
            chain(dve.tensor_tensor(lg[:, 2, :], lg[:, 2, :], lg[:, 3, :], ALU.mult))
            chain(dve.tensor_scalar(lg[:, 0, :], dec[:, :], 0.0, None, ALU.min))
            chain(dve.tensor_tensor(lg[:, 4, :], lg[:, 0, :], lg[:, 2, :], ALU.subtract))
            dve.tensor_scalar(lg[:, 5, :], lg[:, 4, :], float(T), None, ALU.mult).then_inc(lg_ready, 3)
            for l in range(2):
                for k in range(2):
                    chain(dve.tensor_tensor(lamp[:, l, k, :], lamv[:, l, 2 * k, :], lamv[:, l, 2 * k + 1, :], ALU.mult))
            for l in range(2):
                for k in range(2):
                    ins = dve.tensor_reduce(lam[:, 2 * l + k:2 * l + k + 1], lamp[:, l, k, :], AX.X, ALU.add)
                    if l + k < 2:
                        chain(ins)
            ins.then_inc(lam_dots, 1)
            dve.wait_ge(lam_exp, 1)
            for l in range(2):
                chain(dve.tensor_tensor(lamn[:, l:l + 1], lam[:, 5 + 2 * l:6 + 2 * l], lam[:, 4 + 2 * l:5 + 2 * l],
                                        ALU.subtract))
                chain(dve.tensor_scalar(lamn[:, l:l + 1], lamn[:, l:l + 1], -LAM_INIT[l], None, ALU.add))
            for q in range(1, MOD0 // 4):
                take_rows(q)
            dve.wait_ge(mod_out, MOD0 // 4)
            for v in range(2):
                chain(dve.tensor_tensor(mod[:, 0:2 * MOD0, v], mod[:, 0:2 * MOD0, v], vecA[:, 0:2 * MOD0], ALU.add))
            coefficients(0)

            def ffn(l, f, j):
                norm(f"n{l}{j}")
                for s in range(2):
                    run(gemm(f"in{l}{f}{s}"))
                    run(gemm(f"out{l}{f}{s}"))

            splits_upto(1)
            dve.wait_ge(rpb_out, 16)
            dve.wait_ge(t5_out, 16)
            ffn(0, 0, 0)
            for b in range(MOD0 + len(taken), 36):
                take_mod(b)
            dve.wait_ge(mod_taken, 36 - MOD0)
            coefficients(1)
            coefficients(2)
            dve.wait_ge(coef_ready, 3)
            def centre(hh):
                dve.wait_ge(r_mu, hh + 1)
                dve.wait_ge(r_of, 4 * hh + 4)
                for v in range(4):
                    dve.scalar_tensor_tensor(out=oc[:, v, :], in0=aux[0][:, :], scalar=-1.0 / 512, in1=oc[:, v, :],
                                             op0=ALU.mult, op1=ALU.add).then_inc(r_cen, 1)

            def gated(hh):
                dve.wait_ge(r_std, hh + 1)
                chain(dve.reciprocal(rstd[:, :], std[:, :]))
                yield 1
                for v in range(4):
                    g0 = VB["gn_g"] + 4 * hh + v
                    chain(dve.scalar_tensor_tensor(out=oc[:, v, :], in0=oc[:, v, :], scalar=vecB[:, g0:g0 + 1],
                                                   in1=rstd[:, :], op0=ALU.mult, op1=ALU.mult))
                    dve.tensor_tensor(oc[:, v, :], oc[:, v, :], gr[:, v, :], ALU.mult).then_inc(r_gat, 1)
                    yield 1
                for v in range(4):
                    dve.wait_ge(r_high, 4 * hh + v + 1)
                    dve.tensor_tensor(ol[:, v, :], oc[:, v, :], oh[:, v, :].bitcast(F32), ALU.subtract).then_inc(r_low, 1)
                    if v % 2:
                        yield 1

            norm("n01")
            for hh in range(RH):
                if hh == 0:
                    dve.wait_ge(ret_consts_in, 16)
                dve.tensor_scalar(dxb[:, 0:1], lg[:, 4, 4 + hh:5 + hh], -1.0, None, ALU.mult).then_inc(rd_x, 1)
                dve.wait_ge(rd_x, 4 * hh + 1)
                dve.tensor_scalar(dx[:, 0, :], cret[:, C_DB:C_DB + 384], lg[:, 4, 4 + hh:5 + hh], None,
                                  ALU.mult).then_inc(rd_x, 1)
                dve.wait_ge(rd_x, 4 * hh + 2)
                dve.scalar_tensor_tensor(out=dx[:, 0, :], in0=cret[:, C_DF:C_DF + 384], scalar=lg[:, 4, hh:hh + 1],
                                         in1=dx[:, 0, :], op0=ALU.mult, op1=ALU.add).then_inc(rd_x, 1)
                dve.wait_ge(rd_exp, 3 * hh + 3)
                dve.tensor_tensor(dx[:, 1, :], dx[:, 1, :], dx[:, 2, :], ALU.add).then_inc(rd_x, 1)
                run(gemm(f"ret_q{hh}"))
                if hh:
                    centre(hh - 1)
                run(gemm(f"ret_k{hh}"))
                wait_gemm_out(dve, f"ret_k{hh}")
                cos, sin = cret[:, C_COS:C_COS + T], cret[:, C_SIN:C_SIN + T]
                for k in range(2):
                    a_, b_ = qk[:, 2 * k, 0:T], qk[:, 2 * k + 1, 0:T]
                    chain(dve.tensor_tensor(hf[:, 0, 0:T], b_, sin, ALU.mult))
                    chain(dve.tensor_tensor(hf[:, 1, 0:T], a_, sin, ALU.mult))
                    chain(dve.tensor_tensor(qr[:, 2 * k, :], a_, cos, ALU.mult))
                    chain(dve.tensor_tensor(qr[:, 2 * k + 1, :], b_, cos, ALU.mult))
                    dve.tensor_tensor(qr[:, 2 * k, :], qr[:, 2 * k, :], hf[:, 0, 0:T], ALU.subtract).then_inc(r_rope, 1)
                    dve.tensor_tensor(qr[:, 2 * k + 1, :], qr[:, 2 * k + 1, :], hf[:, 1, 0:T], ALU.add).then_inc(r_rope, 1)
                    dve.wait_ge(r_rope, 4 * hh + 2 * k + 2)
                after_each(gemm(f"ret_v{hh}", True), gated(hh - 1) if hh else iter(()))
                if hh:
                    run(gemm(f"ret_out{hh - 1}"))
                dve.wait_ge(rd_x, 4 * hh + 4)
                for k, dd in ((0, 0), (1, 1), (2, 0)):
                    dve.wait_ge(r_score, 3 * hh + k + 1)
                    for jt in range(2):
                        ins = dve.tensor_tensor(att[:, 2 * k + jt, :], aux[k][:, T * jt:T * jt + T],
                                                dx[:, dd, P * (1 - jt):P * (1 - jt) + T], ALU.mult)
                    ins.then_inc(r_att, 1)
                run(gemm(f"ret_g{hh}"))
            centre(RH - 1)
            run(gated(RH - 1))
            run(gemm(f"ret_out{RH - 1}"))
            ffn(0, 1, 2)
            for b in range(MOD0 + len(taken), 72):
                take_mod(b)
            dve.wait_ge(mod_taken, 72 - MOD0)
            for i in range(3, 6):
                coefficients(i)
            dve.wait_ge(coef_ready, 6)
            ffn(1, 0, 0)
            norm("n11")
            run(gemm("nat_q0"))
            run(gemm("nat_k0"))
            run(gemm("nat_v0"))
            for g in range(4):
                nxt = [f"nat_{k}{g + 1}" for k in "qkv"] if g < 3 else []
                alongside(f"nat{g}", attention(f"nat{g}"), gemm, nxt)
            run(gemm("nat_o"))
            ffn(1, 1, 2)
            norm("final")
            for l in range(2):
                norm(f"mix_pre{l}")
                for k in "qkv":
                    run(gemm(f"diff_{k}{l}"))
                if l == 0:
                    R = slice(64, 96)
                    dve.wait_ge(h_update, 8)
                    dve.wait_ge(pos_in, 16)
                    chain(dve.tensor_copy(ang[R, 0, :], po[R, :]))
                    chain(dve.tensor_scalar(ang[R, 0, :], ang[R, 0, :], cst[R, C_INV:C_INV + 1], None, ALU.mult))
                    chain(dve.tensor_scalar(ang[R, 1, :], ang[R, 0, :], float(1 / (2 * np.pi)), 12582912.0, ALU.mult, ALU.add))
                    chain(dve.tensor_scalar(ang[R, 1, :], ang[R, 1, :], -12582912.0, None, ALU.add))
                    for part in LOG2PI:
                        chain(dve.scalar_tensor_tensor(out=ang[R, 0, :], in0=ang[R, 1, :], scalar=-float(part), in1=ang[R, 0, :],
                                                       op0=ALU.mult, op1=ALU.add))
                    dve.tensor_scalar(ang[R, 0, :], ang[R, 0, :], 3.1415925, -3.1415925, ALU.min, ALU.max).then_inc(ang_r, 1)
                    dve.wait_ge(sin_ready, 2)
                    chain(dve.tensor_tensor(ang[R, 2, :], ang[R, 2, :], ang[R, 2, :], ALU.mult))
                    chain(dve.tensor_scalar(ang[R, 2, :], ang[R, 2, :], -2.0, 1.0, ALU.mult, ALU.add))
                    dve.wait_ge(t5_in, 128)
                alongside(f"diff{l}", attention(f"diff{l}"), gemm, with_diff(l))
                def head_low(hd):
                    dve.wait_ge(sub_high, DH * l + hd + 1)
                    dve.scalar_tensor_tensor(out=al[:, hd, :], in0=oraw[:, hd, :], scalar=1.0 - LAM_INIT[l],
                                             in1=ah[:, hd, :].bitcast(F32), op0=ALU.mult,
                                             op1=ALU.subtract).then_inc(sub_low, 1)

                for hd in range(DH):
                    i = DH * l + hd
                    ts = slice(T * (i % 2), T * (i % 2) + T)
                    dve.wait_ge(sub_std, i + 1)
                    chain(dve.reciprocal(rstd[:, ts], std[:, ts]))
                    dve.scalar_tensor_tensor(out=oraw[:, hd, :], in0=oraw[:, hd, :],
                                             scalar=vecC[:, VC["subln"] + l:VC["subln"] + l + 1],
                                             in1=rstd[:, ts], op0=ALU.mult, op1=ALU.mult).then_inc(sub_t, 1)
                    if hd:
                        head_low(hd - 1)
                head_low(DH - 1)
                norm(f"cq{l}")
                norm(f"ckv{l}")
                run(gemm(f"mla_uq{l}"))
                run(gemm(f"mla_ukv{l}"))
                wait_gemm_out(dve, f"mla_ukv{l}")
                for k in range(MH + 1):
                    i = (MH + 1) * l + k
                    x = mq[R, k, :] if k < MH else kpe[R, :]
                    dve.wait_ge(rot_x, i + 1)
                    chain(dve.tensor_tensor(ang[R, 3, :], aux[i % 2][R, 0:T], ang[R, 1, :], ALU.mult))
                    chain(dve.tensor_tensor(x, x, ang[R, 2, :], ALU.mult))
                    if k < MH:
                        dve.tensor_tensor(x, x, ang[R, 3, :], ALU.add).then_inc(roped, 1)
                        dve.wait_ge(roped, (2 * MH) * l + k + 1)
                    else:
                        dve.tensor_tensor(x, x, ang[R, 3, :], ALU.add).then_inc(roped, 1)
                        dve.wait_ge(roped, 2 * MH * l + MH + 1)
                        for hd in range(MH - 1):
                            dve.tensor_copy(mk[R, hd, :], kpe[R, :]).then_inc(roped, 1)
                alongside(f"moba{l}", attention(f"moba{l}"), gemm, [f"gate0{l}"])
                alongside(f"mla{l}", attention(f"mla{l}"), gemm, with_mla(l))
                run(gemm(f"branch2{l}"))
                run(gemm(f"mixed{l}"))
                norm(f"mix_post{l}")
                norm(f"mlp_pre{l}")
                for s in range(4):
                    run(gemm(f"up{l}{s}"))
                    run(gemm(f"down{l}{s}"))
                norm(f"mlp_post{l}")
            for t in range(2):
                for k in range(4):
                    dve.wait_ge(out_turned, 4 * t + k + 1)
                    dve.tensor_copy(out_buf[t][:, T * k:T * k + T], aux[k][:, 0:T]).then_inc(out_rows, 1)

        @block.tensor
        def _(pe):
            def norm(name):
                N = norms[name]
                s_q = N["buf"][3]
                tok = N["tok"]
                for c in range(N["nc"]):
                    i = N["sq0"] + c
                    pe.wait_ge(sq_ready, i + 1)
                    if c == 0 and N["u"]:
                        pe.wait_ge(std_ready, N["u"])
                    ins = pe.matmul(aux[3][:, 0:tok], ones[:, :], s_q[:, i % 2, 0:tok], start=c == 0,
                                    stop=c == N["nc"] - 1)
                    ins.then_inc(sq_used, 1)

            def add_partitions(b):
                i = b - MOD0
                pe.wait_ge(mod_ctx, (DC - 1) * (i + 1))
                pe.wait_ge(mod_lat, i + 1)
                if i >= 2:
                    pe.wait_ge(mod_taken, i - 1)
                for c in range(2):
                    for v in range(2):
                        o = 2 * c + v
                        ins = pe.matmul(aux[i % 2][:, o:o + 1], macc[:, i % 2, v, P * c:P * c + P], ones[:, 0:1],
                                        start=True, stop=True)
                ins.then_inc(mod_made, 1)

            def gemm(name, x_waits=None):
                g = G[name]
                n, s = g.n0, g.s0
                t0, t1 = g.tok
                seen = set()
                for bl, ch in g.groups:
                    for bi, (_, k0, nk, w) in enumerate(bl):
                        pe.wait_ge(w_low, 2 * s + 2)
                        H, L_ = wh[s % SPL], wl[s % SPL]
                        for ci, (o, a0, a1) in enumerate(ch):
                            m = n + ci
                            ps = bank[m % 4]
                            if bi == 0 and m >= 4:
                                wait_chunk_out(pe, m - 4)
                            for k in range(nk):
                                kc = k0 + k
                                if x_waits and kc not in seen:
                                    x_waits(kc)
                                    seen.add(kc)
                                first, last = bi == 0 and k == 0, bi == len(bl) - 1 and k == nk - 1
                                xhi, xlo = g.x[0](kc), g.x[1](kc)
                                if o == "A":
                                    c0 = k * w + a0
                                    hi, lo = H[:, c0:c0 + a1], L_[:, c0:c0 + a1]
                                    out = ps[0:a1, 0:t1 - t0]
                                    trio = ((hi, xhi[:, t0:t1]), (hi, xlo[:, t0:t1]), (lo, xhi[:, t0:t1]))
                                else:
                                    hi, lo = a1(H[:, k * w:k * w + w]), a1(L_[:, k * w:k * w + w])
                                    nn = w if w == WB else 512
                                    out = ps[:, 0:nn]
                                    q0 = P * a0
                                    trio = ((xhi[:, q0:q0 + P], hi), (xhi[:, q0:q0 + P], lo), (xlo[:, q0:q0 + P], hi))
                                for j, (l_, r_) in enumerate(trio):
                                    ins = pe.matmul(out, l_, r_, start=first and j == 0, stop=last and j == 2)
                            if bi == len(bl) - 1:
                                ins.then_inc(chunk_ready, 1)
                        if bi < len(bl) - 1:
                            ins.then_inc(block_used, 1)
                        if s - 1 in mod_after:
                            add_partitions(mod_after[s - 1])
                        s += 1
                    n += len(ch)
                    yield 1

            def normed(name):
                N = norms[name]
                per = N["tok"] // T
                return lambda kc: pe.wait_ge(x_low, N["p0"] + per * (kc + 1))

            def attention(name, after):
                a = atts[name]
                wait_gemm_out(pe, after)
                pe_, pt_, dg_, st_ = a.bufs
                rev, rev64 = cst[:, C_REV:C_REV + P], cst[:, C_REV64:C_REV64 + P]
                order_of = {"nat": rev64, "dif": rev, "mob": rev, "mla": ident}

                def scores(j):
                    t, i = a.units[j]
                    u = a.u0 + j
                    tile = a.tiles[t]
                    un = tile["units"][i]
                    if u >= 2:
                        pe.wait_ge(p_ready, u - 1)
                    if name[:3] == "nat" and i == 0:
                        pe.wait_ge(tt_masked, tile["head"] + 1)
                    k = tile["keys"]
                    b0, b1, bias = un["bias"]
                    pe.matmul(aux[u % 2][:, 0:k], un["qk"][0], un["qk"][1], start=True, stop=True,
                              skip_group_check=True)
                    pe.matmul(aux[u % 2][:, b0:b1], order_of[name[:3]], bias, start=False, stop=True,
                              skip_group_check=True).then_inc(s_ready, 1)

                def turn(j):
                    t, i = a.units[j]
                    u = a.u0 + j
                    tile = a.tiles[t]
                    nu = len(tile["units"])
                    pe.wait_ge(dg_ready, u + 1)
                    if i == nu - 1:
                        if a.t0 + t >= 1:
                            pe.wait_ge(pt_out, a.t0 + t)
                        for kt in range(tile["keys"] // P):
                            for q in range(nu):
                                uq = u - nu + 1 + q
                                ins = pe.matmul(aux[2][:, P * kt:P * kt + P], pe_[:, uq % 2, P * kt:P * kt + P],
                                                dg_[:, uq % 2, :], start=q == 0, stop=q == nu - 1)
                        ins.then_inc(p_used, nu)

                def values(t):
                    tg = a.t0 + t
                    tile = a.tiles[t]
                    r0, r1 = tile["rows"]
                    pe.wait_ge(pt_out, tg + 1)
                    if tg >= 1:
                        pe.wait_ge(o_low, tg)
                        pe.wait_ge(o_high, tg)
                    nkt = tile["keys"] // P
                    for kt in range(nkt):
                        ins = pe.matmul(aux[3][r0:r1, 0:P], tile["v"](kt), pt_[:, tg % 2, P * kt:P * kt + P],
                                        start=kt == 0, stop=kt == nkt - 1)
                    ins.then_inc(o_ready, 1)

                n = len(a.units)
                scores(0)
                for j, (t, i) in enumerate(a.units):
                    nu = len(a.tiles[t]["units"])
                    if j + 1 < n:
                        scores(j + 1)
                    turn(j)
                    if i == nu - 1 and t >= 1:
                        values(t - 1)
                    yield 1
                values(len(a.tiles) - 1)

            pe.wait_ge(consts_in, 16)
            pe.wait_ge(rows_in, 16 * 14)
            for i, w in enumerate((P, NVB, NVC)):
                pe.transpose(aux[i][:, 0:w], vrows[0:w, i, :], ident[0:w, 0:w]).then_inc(vec_turned, 1)
            pe.wait_ge(c_silu, 2)

            def mod_turn(b):
                q = b // 4
                if b % 4 == 0 and q >= 2:
                    pe.wait_ge(mod_out, q - 1)
                pe.wait_ge(mod_row, b + 1)
                for j in range(2):
                    o = 4 * (b % 4) + 2 * j
                    ins = pe.matmul(aux[q % 2][:, o:o + 2], mrow[:, b % 4, P * j:P * j + P], ident[0:2, 0:2],
                                    start=True, stop=True)
                ins.then_inc(mod_cols, 1)

            def mod_rows(b):
                pe.wait_ge(raw_in[b % RAW], value_of["m", b])
                if b >= 4:
                    pe.wait_ge(mod_row, b - 3)
                for k in range(DC):
                    ins = pe.matmul(bank[b % 4][0:2, 0:WB], sc[:, k, :], raw[b % RAW][:, WB * k:WB * k + WB],
                                    start=k == 0, stop=k == DC - 1)
                ins.then_inc(chunk_mod, 1)

            pe.wait_ge(vec_ready, 3)
            for b in range(4):
                mod_rows(b)
                if b:
                    mod_turn(b - 1)
            mod_turn(3)
            pe.wait_ge(pool_ready, 5)
            pe.wait_ge(small_in, 80)
            pe.matmul(aux[3][0:8, :], tab[:, :], hot[:, :], start=True, stop=True).then_inc(t5_g, 1)
            pe.wait_ge(x_in, 64)
            pe.wait_ge(mod_out, 1)
            for c in range(DC):
                if c == 3:
                    pe.wait_ge(t5_row, 1)
                elif c > 3:
                    pe.wait_ge(h_init, c - 3)
                for t in range(4):
                    ins = pe.transpose(aux[c % 4][:, P * t:P * t + P], xrows[:, t, P * c:P * c + P], ident)
                ins.then_inc(x_turned, 1)
            pe.wait_ge(h_init, 8)
            for b in range(4, MOD0):
                mod_rows(b)
                if b > 4:
                    mod_turn(b - 1)
            mod_turn(MOD0 - 1)
            pe.wait_ge(mod_row, MOD0)

            def ffn(l, f, j):
                norm(f"n{l}{j}")
                for s in range(2):
                    run(gemm(f"in{l}{f}{s}", normed(f"n{l}{j}")))
                    base = G[f"in{l}{f}{s}"].hid0
                    run(gemm(f"out{l}{f}{s}", lambda kc: pe.wait_ge(hid_low, base + kc - s * FH + 1)))

            pe.wait_ge(coef_ready, 1)
            ffn(0, 0, 0)
            pe.wait_ge(mod_taken, 36 - MOD0)
            norm("n01")
            def mean(hh):
                for v in range(4):
                    pe.wait_ge(r_of, 4 * hh + (v + 1 if v else 2))
                    ins = pe.matmul(aux[0][:, :], ones[:, :], oc[:, v, :], start=v == 0, stop=v == 3)
                ins.then_inc(r_mu, 1)

            def variance(hh):
                for v in range(4):
                    pe.wait_ge(r_sq, 4 * hh + v + 1)
                    pe.matmul(aux[1][:, :], ones[:, :], sa[:, v % 2, :], start=v == 0, stop=v == 3).then_inc(r_sqf, 1)

            def ret_out(hh):
                run(gemm(f"ret_out{hh}", lambda kc: pe.wait_ge(r_low, kc + 1)))

            for hh in range(RH):
                run(gemm(f"ret_q{hh}", normed("n01")))
                if hh:
                    mean(hh - 1)
                run(gemm(f"ret_k{hh}"))
                if hh:
                    variance(hh - 1)
                run(gemm(f"ret_v{hh}"))
                pe.wait_ge(r_rope, 4 * hh + 4)
                wait_gemm_out(pe, f"ret_k{hh}")
                for k in range(3):
                    if k == 0 and hh:
                        pe.wait_ge(r_cen, 4 * hh)
                    if k == 1 and hh:
                        pe.wait_ge(r_std, hh)
                    for jt in range(2):
                        for d in range(2):
                            kk = qr[:, 2 + d, P * jt:P * jt + P] if k == 0 else qk[:, 2 + d, T + P * jt:T + P * jt + P]
                            qq = qk[:, d, T:T2] if k == 2 else qr[:, d, :]
                            ins = pe.matmul(aux[k][:, T * jt:T * jt + T], kk, qq, start=d == 0, stop=d == 1)
                    ins.then_inc(r_score, 1)
                if hh:
                    ret_out(hh - 1)
                run(gemm(f"ret_g{hh}"))
                pe.wait_ge(r_att, 3 * hh + 3)
                wait_gemm_out(pe, f"ret_v{hh}")
                for v in range(4):
                    ps = aux[(v + 3) % 4]
                    for q in range(2):
                        js = ((0, 0), (1, 1), (2, 2), (3, 3)) if q == 0 else ((2, 4), (3, 5))
                        for x, (vt, at) in enumerate(js):
                            ins = pe.matmul(ps[:, T * q:T * q + T], vr[:, vt, P * v:P * v + P], att[:, at, :],
                                            start=x == 0, stop=x == len(js) - 1)
                    ins.then_inc(r_o, 1)
            mean(RH - 1)
            variance(RH - 1)
            ret_out(RH - 1)
            ffn(0, 1, 2)
            pe.wait_ge(mod_taken, 72 - MOD0)
            ffn(1, 0, 0)
            norm("n11")
            run(gemm("nat_q0", normed("n11")))
            run(gemm("nat_k0"))
            run(gemm("nat_v0"))
            for g in range(4):
                nxt = [f"nat_{k}{g + 1}" for k in "qkv"] if g < 3 else []
                alongside(f"nat{g}", attention(f"nat{g}", f"nat_v{g}"), gemm, nxt)
            pe.wait_ge(o_low, atts["nat3"].t1)
            run(gemm("nat_o"))
            ffn(1, 1, 2)
            norm("final")
            for l in range(2):
                norm(f"mix_pre{l}")
                run(gemm(f"diff_q{l}", normed(f"mix_pre{l}")))
                run(gemm(f"diff_k{l}"))
                run(gemm(f"diff_v{l}"))
                pe.wait_ge(t5_in, 128)
                alongside(f"diff{l}", attention(f"diff{l}", f"diff_v{l}"), gemm, with_diff(l))
                for hd in range(DH):
                    i = DH * l + hd
                    pe.wait_ge(sub_sq, i + 1)
                    pe.wait_ge(o_low, atts[f"diff{l}"].t1)
                    pe.wait_ge(pt_out, atts[f"diff{l}"].t1)
                    if hd >= 2:
                        pe.wait_ge(sub_std, i - 1)
                    pe.matmul(aux[2 + i % 2][:, 0:T], ones[:, :], sq2[:, i % 2, :], start=True, stop=True).then_inc(sub_ms, 1)
                pe.wait_ge(sub_std, DH * l + DH)
                norm(f"cq{l}")
                norm(f"ckv{l}")
                run(gemm(f"mla_uq{l}", normed(f"cq{l}")))
                run(gemm(f"mla_ukv{l}", normed(f"ckv{l}")))
                wait_gemm_out(pe, f"mla_uq{l}")
                for k in range(MH + 1):
                    i = (MH + 1) * l + k
                    if k >= 2:
                        pe.wait_ge(roped, 2 * MH * l + k - 1)
                    x = mq[64:96, k, :] if k < MH else kpe[64:96, :]
                    pe.matmul(aux[i % 2][64:96, 0:T], cst[64:96, C_ROT:C_ROT + 32], x, start=True,
                              stop=True).then_inc(rot_x, 1)
                pe.wait_ge(roped, 2 * MH * l + MH + 1)
                alongside(f"moba{l}", attention(f"moba{l}", f"mla_ukv{l}"), gemm, [f"gate0{l}"])
                pe.wait_ge(roped, 2 * MH * (l + 1))
                pe.wait_ge(sub_low, DH * (l + 1))
                pe.wait_ge(o_low, atts[f"moba{l}"].t1)
                alongside(f"mla{l}", attention(f"mla{l}", f"gate0{l}"), gemm, with_mla(l))
                pe.wait_ge(o_low, atts[f"mla{l}"].t1)
                run(gemm(f"branch2{l}"))
                run(gemm(f"mixed{l}", lambda kc: pe.wait_ge(mix_low, 8 * l + kc + 1)))
                norm(f"mix_post{l}")
                norm(f"mlp_pre{l}")
                for s in range(4):
                    run(gemm(f"up{l}{s}", normed(f"mlp_pre{l}")))
                    base = G[f"up{l}{s}"].hid0
                    run(gemm(f"down{l}{s}", lambda kc: pe.wait_ge(hid_low, base + kc - s * DC + 1)))
                norm(f"mlp_post{l}")
            pe.wait_ge(h_update, 8 + 32)
            for t in range(2):
                for k in range(4):
                    if t:
                        pe.wait_ge(out_rows, k + 1)
                    for c in range(2):
                        ins = pe.transpose(aux[k][:, P * c:P * c + P], h[:, 2 * k + c, P * t:P * t + P], ident)
                    ins.then_inc(out_turned, 1)


NAMES = ["x", "c", "ctx", "c_ctx", "w_mod", "b_mod", "norm_g", "ffn_w_in", "ffn_w_out", "ret_w_in", "ret_w_out",
         "ret_gn_g", "ret_decay_f", "ret_decay_b", "nat_w_qkv", "nat_w_o", "nat_rpb", "final_norm_g", "positions_2",
         "rel_bias_2", "norm_mix_pre_2", "norm_mix_post_2", "norm_mlp_pre_2", "norm_mlp_post_2", "w_in_2",
         "diff_lambda_2", "diff_subln_2", "mla_q_norm_2", "mla_w_uq_2", "mla_kv_norm_2", "mla_w_ukv_2", "w_branch_2",
         "w_out_2", "w_up_2", "w_down_2"]


def kernel(**inputs):
    import concourse.bacc as bacc
    from concourse.bass_utils import run_bass_kernel_spmd

    nc = bacc.Bacc("TRN2", target_bir_lowering=False, num_devices=1)
    arrays, aps = {}, {}
    small, ret = shape_constants()
    for name, a in [(n, np.ascontiguousarray(inputs[n])) for n in NAMES] + [("consts", small), ("ret_consts", ret)]:
        arrays[f"in_{name}"] = a
        aps[name] = nc.dram_tensor(f"in_{name}", a.shape, mybir.dt.from_np(a.dtype), kind="ExternalInput").ap()
    aps["out"] = nc.dram_tensor("out_0", (1, T, D), F32, kind="ExternalOutput").ap()
    program(nc, aps)
    r = run_bass_kernel_spmd(nc, [arrays], core_ids=[0])
    return r.results[0]["out_0"]
```
